# Optimizing a Trainium2 kernel written in Bass

```python
import math
import jax, jax.numpy as jnp
from jax import lax
import numpy as np

D_MODEL = 1024
BATCH = 1
SEQ = 512
DEPTH = 2
DEC_BATCH = 8
DEC_SEQ = 8
PAST_LEN = 2048
PAGE_SIZE = 128

HEAD_DIM = 64
N_HEADS = D_MODEL // HEAD_DIM
SCALE = HEAD_DIM ** -0.5
H_A = N_HEADS // 2
KV_A = 2
G_A = H_A // KV_A
H_IDX = 8
D_IDX = 64
DSA_TOPK = 256
H_B = N_HEADS - H_A
DILATIONS = ((128, 1), (512, 4), (2048, 16))
B_WIN = max(w for w, _ in DILATIONS)
H_C = N_HEADS
KV_C = 2
G_C = H_C // KV_C
CMP_STRIDE = 16
CMP_LEN = 2 * CMP_STRIDE
SEL_BLOCK = 64
SEL_TOPK = 16
C_WIN = 512
SEL_BONUS = 1e3
D_FF = 2816
CONV_W = 3
N_BUCKETS = 32
T5_MAX_DIST = 128
ALPHA = (2 * DEPTH) ** 0.25
BETA = (8 * DEPTH) ** -0.25
LN_EPS = 1e-5
N_AB = (DEPTH + 1) // 2
N_C = DEPTH // 2
Q_BLOCK = 128
NSA_Q_BLOCK = 32
NEG_INF = -1e30
AB_SPLITS = (H_A * HEAD_DIM, KV_A * HEAD_DIM, KV_A * HEAD_DIM, H_IDX * D_IDX, D_IDX, H_IDX,
             H_B * HEAD_DIM, H_B * HEAD_DIM, H_B * HEAD_DIM)
AB_COLS = sum(AB_SPLITS)
C_SPLITS = (H_C * HEAD_DIM, 6 * KV_C * HEAD_DIM, 3 * H_C)
C_COLS = sum(C_SPLITS)
B_BUF = min(B_WIN, PAST_LEN)
C_BUF = min(C_WIN, PAST_LEN)

kernel_name = 'hybrid_dsa_dilated_nsa_convffn_step'

def split_cols(h, sizes):
    idx = [int(i) for i in np.cumsum(sizes)[:-1]]
    return jnp.split(h, idx, axis=-1)

def layer_norm(x, g, b):
    xf = x.astype(jnp.float32)
    mu = jnp.mean(xf, -1, keepdims=True)
    var = jnp.mean(jnp.square(xf - mu), -1, keepdims=True)
    return ((xf - mu) * lax.rsqrt(var + LN_EPS) * g + b).astype(x.dtype)

def t5_bucket(dist):
    n = jnp.maximum(dist, 0)
    exact = N_BUCKETS // 2
    nf = jnp.maximum(n, 1).astype(jnp.float32)
    far = exact + (jnp.log(nf / exact) / math.log(T5_MAX_DIST / exact) * (N_BUCKETS - exact)).astype(jnp.int32)
    return jnp.where(n < exact, n, jnp.minimum(far, N_BUCKETS - 1))

def masked_softmax(logits, mask):
    logits = jnp.where(mask, logits.astype(jnp.float32), NEG_INF)
    m = jnp.max(logits, axis=-1, keepdims=True)
    p = jnp.exp(logits - m) * mask
    s = jnp.maximum(jnp.sum(p, axis=-1, keepdims=True), 1e-30)
    return p / s, (m + jnp.log(s))[..., 0]

def map_query_blocks(fn, q_arrays, q_pos, block):
    nq = q_pos.shape[0]
    qb = block if nq % block == 0 else nq
    nb = nq // qb
    if nb == 1:
        return fn(*q_arrays, q_pos)

    def body(i):
        start = i * qb
        sl = [lax.dynamic_slice_in_dim(a, start, qb, axis=1) for a in q_arrays]
        return fn(*sl, lax.dynamic_slice_in_dim(q_pos, start, qb, axis=0))

    out = lax.map(body, jnp.arange(nb))
    merge = lambda o: jnp.moveaxis(o, 0, 1).reshape((o.shape[1], nq) + o.shape[3:])
    return jax.tree_util.tree_map(merge, out)

def gather_pages(cache, page_table):
    pages = cache[page_table]
    return pages.reshape((page_table.shape[0], -1) + pages.shape[3:])

def last_rows(a, n):
    L = a.shape[1]
    if L >= n:
        return a[:, L - n:]
    return jnp.pad(a, [(0, 0), (n - L, 0)] + [(0, 0)] * (a.ndim - 2))

def dsa_attend(q, qi, wi, q_pos, k, v, ki, tab):
    L = k.shape[1]
    top = min(DSA_TOPK, L // 4)
    kpos = jnp.arange(L)
    tab_a = tab[:, :H_A]

    def block(qb, qib, wib, pb):
        b, n = qb.shape[:2]
        s = jnp.einsum('bqhe,ble->bqhl', qib, ki).astype(jnp.float32) * (D_IDX ** -0.5)
        score = jnp.einsum('bqhl,bqh->bql', jax.nn.relu(s), wib.astype(jnp.float32)) * (H_IDX ** -0.5)
        score = jnp.where((kpos[None, :] <= pb[:, None])[None], score, -jnp.inf)
        _, idx = lax.top_k(score, top)
        kg = jax.vmap(lambda kk, ii: kk[ii])(k, idx)
        vg = jax.vmap(lambda vv, ii: vv[ii])(v, idx)
        dist = pb[None, :, None] - idx
        qg = qb.reshape(b, n, KV_A, G_A, HEAD_DIM)
        logits = jnp.einsum('bqgjd,bqkgd->bqgjk', qg, kg) * SCALE
        bias = tab_a[t5_bucket(dist)].reshape(b, n, top, KV_A, G_A).transpose(0, 1, 3, 4, 2)
        p, _ = masked_softmax(logits + bias, (dist >= 0)[:, :, None, None, :])
        o = jnp.einsum('bqgjk,bqkgd->bqgjd', p.astype(vg.dtype), vg)
        return o.reshape(b, n, H_A * HEAD_DIM)

    return map_query_blocks(block, (q, qi, wi), q_pos, Q_BLOCK)

def dilated_prompt(q, k, v, window, dil, tab_b):
    b, S, H, _ = q.shape
    span = window // dil
    unit = span * dil
    P = -(-S // unit) * unit
    nb = P // unit

    def blocks(a):
        a = jnp.pad(a, ((0, 0), (0, P - S), (0, 0), (0, 0)))
        a = a.reshape(b, P // dil, dil, H, HEAD_DIM).transpose(0, 2, 1, 3, 4)
        return a.reshape(b, dil, nb, span, H, HEAD_DIM)

    qb, kb, vb = blocks(q), blocks(k), blocks(v)
    shift = lambda a: jnp.pad(a, ((0, 0), (0, 0), (1, 0), (0, 0), (0, 0), (0, 0)))[:, :, :-1]
    kk = jnp.concatenate([shift(kb), kb], 3)
    vv = jnp.concatenate([shift(vb), vb], 3)
    logits = jnp.einsum('brnqhe,brnkhe->brnhqk', qb, kk) * SCALE
    key_sub = jnp.arange(2 * span) - span
    sub = jnp.arange(span)[:, None] - key_sub[None, :]
    first = (jnp.arange(nb)[:, None] * span + key_sub[None, :]) >= 0
    valid = (sub >= 0) & (sub <= span) & first[:, None, :]
    bias = tab_b[t5_bucket(sub * dil)].transpose(2, 0, 1)
    p, lse = masked_softmax(logits + bias, valid[None, None, :, None])
    o = jnp.einsum('brnhqk,brnkhe->brnqhe', p.astype(vv.dtype), vv)
    o = o.reshape(b, dil, P // dil, H, HEAD_DIM).transpose(0, 2, 1, 3, 4).reshape(b, P, H, HEAD_DIM)[:, :S]
    lse = lse.transpose(0, 1, 2, 4, 3).reshape(b, dil, P // dil, H).transpose(0, 2, 1, 3).reshape(b, P, H)[:, :S]
    return o, lse

def dilated_sample(q, q_pos, k, v, k_start, window, dil, tab_b):
    span = window // dil
    steps = dil * jnp.arange(span + 1)
    idx = q_pos[:, None] - steps[None, :] - k_start
    valid = idx >= 0
    idx = jnp.clip(idx, 0, k.shape[1] - 1)
    kg, vg = k[:, idx], v[:, idx]
    logits = jnp.einsum('bqhe,bqkhe->bqhk', q, kg) * SCALE
    bias = tab_b[t5_bucket(steps)].T
    p, lse = masked_softmax(logits + bias[None, None], valid[None, :, None, :])
    o = jnp.einsum('bqhk,bqkhe->bqhe', p.astype(vg.dtype), vg)
    return o, lse

def combine_dilations(res):
    outs = jnp.stack([o for o, _ in res])
    w = jax.nn.softmax(jnp.stack([l for _, l in res]), axis=0)
    return jnp.einsum('rbqh,rbqhe->bqhe', w.astype(outs.dtype), outs)

def ab_project(x, w_in):
    b, n = x.shape[:2]
    qa, ka, va, qi, ki, wi, qb, kb, vb = split_cols(x @ w_in, AB_SPLITS)
    hd = lambda a, h: a.reshape(b, n, h, HEAD_DIM)
    return (hd(qa, H_A), hd(ka, KV_A), hd(va, KV_A), qi.reshape(b, n, H_IDX, D_IDX), ki, wi,
            hd(qb, H_B), hd(kb, H_B), hd(vb, H_B))

def ab_prompt(x, w_in, tab):
    b, S = x.shape[:2]
    qa, ka, va, qi, ki, wi, qb, kb, vb = ab_project(x, w_in)
    pos = jnp.arange(S)
    o_a = dsa_attend(qa, qi, wi, pos, ka, va, ki, tab)
    tab_b = tab[:, H_A:]
    o_b = combine_dilations([dilated_prompt(qb, kb, vb, w, d, tab_b) for w, d in DILATIONS])
    mix = jnp.concatenate([o_a, o_b.reshape(b, S, H_B * HEAD_DIM)], -1)
    return mix, jnp.stack([ka, va], 2), ki, last_rows(jnp.stack([kb, vb], 2), B_BUF)

def ab_sample(x, w_in, tab, cache_kv, cache_kidx, page_table, state_kv):
    b, n = x.shape[:2]
    qa, ka, va, qi, ki, wi, qb, kb, vb = ab_project(x, w_in)
    pos = PAST_LEN + jnp.arange(n)
    past_kv = gather_pages(cache_kv, page_table)
    past_ki = gather_pages(cache_kidx, page_table)
    k_all = jnp.concatenate([past_kv[:, :, 0], ka], 1)
    v_all = jnp.concatenate([past_kv[:, :, 1], va], 1)
    ki_all = jnp.concatenate([past_ki, ki], 1)
    o_a = dsa_attend(qa, qi, wi, pos, k_all, v_all, ki_all, tab)
    kv_b = jnp.concatenate([state_kv, jnp.stack([kb, vb], 2)], 1)
    tab_b = tab[:, H_A:]
    start = PAST_LEN - B_BUF
    o_b = combine_dilations([dilated_sample(qb, pos, kv_b[:, :, 0], kv_b[:, :, 1], start, w, d, tab_b)
                             for w, d in DILATIONS])
    mix = jnp.concatenate([o_a, o_b.reshape(b, n, H_B * HEAD_DIM)], -1)
    return mix, jnp.stack([ka, va], 2), ki, kv_b[:, -B_BUF:]

def compress(k, pe, w1, b1, w2):
    b, L = k.shape[:2]
    nch = L // CMP_STRIDE
    ch = k[:, :nch * CMP_STRIDE].reshape(b, nch, CMP_STRIDE, KV_C, HEAD_DIM)
    ha = jnp.einsum('bcjge,jef->bcgf', ch, w1[:CMP_STRIDE])
    hb = jnp.einsum('bcjge,jef->bcgf', ch, w1[CMP_STRIDE:])
    const = jnp.einsum('je,jef->f', pe, w1) + b1
    h = jax.nn.gelu(ha[:, :-1] + hb[:, 1:] + const)
    return jnp.einsum('bcgf,fe->bcge', h, w2)

def to_sel_blocks(a):
    b, L = a.shape[:2]
    n_sel = -(-L // SEL_BLOCK)
    a = jnp.pad(a, ((0, 0), (0, n_sel * SEL_BLOCK - L), (0, 0), (0, 0)))
    return a.reshape(b, n_sel, SEL_BLOCK, KV_C, HEAD_DIM).transpose(0, 3, 1, 2, 4)

def nsa_sparse(q, q_pos, kc, vc, ks_blk, vs_blk, tab):
    n_cmp = kc.shape[1]
    n_sel = ks_blk.shape[2]
    n_top = min(SEL_TOPK, n_sel)
    c_end = jnp.arange(n_cmp) * CMP_STRIDE + (CMP_LEN - 1)
    blk = jnp.arange(n_sel)
    group = SEL_BLOCK // CMP_STRIDE
    n_pad = group * n_sel - (n_cmp + 1)
    tab_g = tab.reshape(N_BUCKETS, KV_C, G_C).transpose(1, 0, 2)
    kv_ix = jnp.arange(KV_C)[None, :, None, None]
    take = jax.vmap(jax.vmap(lambda blocks, ii: blocks[ii]))
    nk = n_top * SEL_BLOCK

    def block(qb, pb):
        b, n = qb.shape[:2]
        qg = qb.reshape(b, n, KV_C, G_C, HEAD_DIM)
        lc = jnp.einsum('bqgjd,bcgd->bqgjc', qg, kc) * SCALE
        pc, _ = masked_softmax(lc, (c_end[None, :] <= pb[:, None])[None, :, None, None, :])
        o_cmp = jnp.einsum('bqgjc,bcgd->bqgjd', pc.astype(vc.dtype), vc)
        imp = pc.sum(3)
        pad = lambda a, lo, hi: jnp.pad(a, ((0, 0), (0, 0), (0, 0), (lo, hi)))
        chunk = pad(imp, 0, 1) + pad(imp, 1, 0)
        p_slc = pad(chunk, 0, n_pad).reshape(b, n, KV_C, n_sel, group).sum(-1)
        cur = pb // SEL_BLOCK
        forced = (blk[None, :] == 0) | (blk[None, :] == cur[:, None]) | (blk[None, :] == cur[:, None] - 1)
        valid = blk[None, :] * SEL_BLOCK <= pb[:, None]
        score = jnp.where(valid[None, :, None], p_slc + jnp.where(forced, SEL_BONUS, 0.0)[None, :, None], -jnp.inf)
        _, bidx = lax.top_k(score, n_top)
        bidx = bidx.transpose(0, 2, 1, 3)
        kg = take(ks_blk, bidx).reshape(b, KV_C, n, nk, HEAD_DIM)
        vg = take(vs_blk, bidx).reshape(b, KV_C, n, nk, HEAD_DIM)
        kpos = (bidx[..., None] * SEL_BLOCK + jnp.arange(SEL_BLOCK)).reshape(b, KV_C, n, nk)
        dist = pb[None, None, :, None] - kpos
        ls = jnp.einsum('bqgjd,bgqkd->bqgjk', qg, kg) * SCALE
        bias = tab_g[kv_ix, t5_bucket(dist)].transpose(0, 2, 1, 4, 3)
        ps, _ = masked_softmax(ls + bias, (dist >= 0).transpose(0, 2, 1, 3)[:, :, :, None, :])
        o_slc = jnp.einsum('bqgjk,bgqkd->bqgjd', ps.astype(vg.dtype), vg)
        return o_cmp.reshape(b, n, H_C, HEAD_DIM), o_slc.reshape(b, n, H_C, HEAD_DIM)

    return map_query_blocks(block, (q,), q_pos, NSA_Q_BLOCK)

def window_attend(q, q_pos, k, v, k_pos, tab):
    b, n = q.shape[:2]
    nk = k_pos.shape[0]
    dist = q_pos[:, None] - k_pos[None, :]
    mask = (dist >= 0) & (dist < C_WIN) & (k_pos[None, :] >= 0)
    qg = q.reshape(b, n, KV_C, G_C, HEAD_DIM)
    logits = jnp.einsum('bqgjd,bkgd->bqgjk', qg, k) * SCALE
    bias = tab[t5_bucket(dist)].reshape(n, nk, KV_C, G_C).transpose(0, 2, 3, 1)
    p, _ = masked_softmax(logits + bias[None], mask[None, :, None, None, :])
    o = jnp.einsum('bqgjk,bkgd->bqgjd', p.astype(v.dtype), v)
    return o.reshape(b, n, H_C, HEAD_DIM)

def window_prompt(q, k, v, tab):
    b, S = q.shape[:2]
    qb = Q_BLOCK if S % Q_BLOCK == 0 else S
    back = -(-C_WIN // qb) * qb
    kp = jnp.pad(k, ((0, 0), (back, 0), (0, 0), (0, 0)))
    vp = jnp.pad(v, ((0, 0), (back, 0), (0, 0), (0, 0)))

    def body(i):
        start = i * qb
        qs = lax.dynamic_slice_in_dim(q, start, qb, 1)
        ks = lax.dynamic_slice_in_dim(kp, start, qb + back, 1)
        vs = lax.dynamic_slice_in_dim(vp, start, qb + back, 1)
        return window_attend(qs, start + jnp.arange(qb), ks, vs, start - back + jnp.arange(qb + back), tab)

    out = lax.map(body, jnp.arange(S // qb))
    return jnp.moveaxis(out, 0, 1).reshape(b, S, H_C, HEAD_DIM)

def c_project(x, w_in):
    b, n = x.shape[:2]
    q, kv, g = split_cols(x @ w_in, C_SPLITS)
    return (q.reshape(b, n, H_C, HEAD_DIM), kv.reshape(b, n, 6, KV_C, HEAD_DIM),
            jax.nn.sigmoid(g.reshape(b, n, 3, H_C).astype(jnp.float32)).astype(x.dtype))

def nsa_cmp_slc(q, pos, rows, pe, w1, b1, w2, tab):
    kc = compress(rows[:, :, 0], pe[0], w1[0], b1[0], w2[0])
    vc = compress(rows[:, :, 1], pe[1], w1[1], b1[1], w2[1])
    return nsa_sparse(q, pos, kc, vc, to_sel_blocks(rows[:, :, 2]), to_sel_blocks(rows[:, :, 3]), tab)

def gate_merge(g, o_cmp, o_slc, o_win):
    b, n = o_cmp.shape[:2]
    o = g[:, :, 0, :, None] * o_cmp + g[:, :, 1, :, None] * o_slc + g[:, :, 2, :, None] * o_win
    return o.reshape(b, n, H_C * HEAD_DIM)

def c_prompt(x, w_in, pe, w1, b1, w2, tab):
    S = x.shape[1]
    q, kv, g = c_project(x, w_in)
    pos = jnp.arange(S)
    o_cmp, o_slc = nsa_cmp_slc(q, pos, kv[:, :, :4], pe, w1, b1, w2, tab)
    o_win = window_prompt(q, kv[:, :, 4], kv[:, :, 5], tab)
    return gate_merge(g, o_cmp, o_slc, o_win), kv[:, :, :4], last_rows(kv[:, :, 4:], C_BUF)

def c_sample(x, w_in, pe, w1, b1, w2, tab, cache_kv, page_table, state_win):
    n = x.shape[1]
    q, kv, g = c_project(x, w_in)
    pos = PAST_LEN + jnp.arange(n)
    rows = jnp.concatenate([gather_pages(cache_kv, page_table), kv[:, :, :4]], 1)
    o_cmp, o_slc = nsa_cmp_slc(q, pos, rows, pe, w1, b1, w2, tab)
    win = jnp.concatenate([state_win, kv[:, :, 4:]], 1)
    k_pos = PAST_LEN - C_BUF + jnp.arange(C_BUF + n)
    o_win = window_attend(q, pos, win[:, :, 0], win[:, :, 1], k_pos, tab)
    return gate_merge(g, o_cmp, o_slc, o_win), kv[:, :, :4], win[:, -C_BUF:]

def conv_ffn(x, prev, w_up, conv_w, conv_b, w_down):
    n = x.shape[1]
    ext = jnp.concatenate([prev, x @ w_up], 1)
    c = conv_b + conv_w[0] * ext[:, :n]
    for j in range(1, CONV_W):
        c = c + conv_w[j] * ext[:, j:j + n]
    gate, val = jnp.split(c, 2, axis=-1)
    return (jax.nn.gelu(gate) * val) @ w_down, ext[:, n:]

def setup_inputs(seed: int = 0) -> dict:
    key = jax.random.key(seed)
    k = jax.random.split(key, 26)
    n_pages = PAST_LEN // PAGE_SIZE
    n_phys = (DEC_BATCH * n_pages * 5) // 4

    def nrm(kk, shape, scale):
        return jax.random.normal(kk, shape, jnp.float32) * scale

    perm = jax.random.permutation(k[0], n_phys)
    page_table = perm[:DEC_BATCH * n_pages].reshape(DEC_BATCH, n_pages).astype(jnp.int32)
    mix_w = (H_A + H_B) * HEAD_DIM
    return {
        'x_prompt': nrm(k[1], (BATCH, SEQ, D_MODEL), 1.0),
        'x_sample': nrm(k[2], (DEC_BATCH, DEC_SEQ, D_MODEL), 1.0),
        'cache_a_kv': nrm(k[3], (N_AB, n_phys, PAGE_SIZE, 2, KV_A, HEAD_DIM), 1.0),
        'cache_a_kidx': nrm(k[4], (N_AB, n_phys, PAGE_SIZE, D_IDX), 1.0),
        'cache_c_kv': nrm(k[5], (N_C, n_phys, PAGE_SIZE, 4, KV_C, HEAD_DIM), 1.0),
        'state_b_kv': nrm(k[6], (N_AB, DEC_BATCH, B_BUF, 2, H_B, HEAD_DIM), 1.0),
        'state_c_kv': nrm(k[7], (N_C, DEC_BATCH, C_BUF, 2, KV_C, HEAD_DIM), 1.0),
        'state_ffn': nrm(k[8], (DEPTH, DEC_BATCH, CONV_W - 1, 2 * D_FF), 1.0),
        'page_table': page_table,
        'rel_bias': nrm(k[9], (N_BUCKETS, N_HEADS), 0.2),
        'w_in_ab': nrm(k[10], (N_AB, D_MODEL, AB_COLS), D_MODEL ** -0.5),
        'w_out_ab': nrm(k[11], (N_AB, mix_w, D_MODEL), BETA * mix_w ** -0.5),
        'w_in_c': nrm(k[12], (N_C, D_MODEL, C_COLS), D_MODEL ** -0.5),
        'w_out_c': nrm(k[13], (N_C, H_C * HEAD_DIM, D_MODEL), BETA * (H_C * HEAD_DIM) ** -0.5),
        'phi_pe': nrm(k[14], (N_C, 2, CMP_LEN, HEAD_DIM), 0.1),
        'phi_w1': nrm(k[15], (N_C, 2, CMP_LEN, HEAD_DIM, HEAD_DIM), (CMP_LEN * HEAD_DIM) ** -0.5),
        'phi_b1': nrm(k[16], (N_C, 2, HEAD_DIM), 0.02),
        'phi_w2': nrm(k[17], (N_C, 2, HEAD_DIM, HEAD_DIM), HEAD_DIM ** -0.5),
        'ln1_g': 1.0 + nrm(k[18], (DEPTH, D_MODEL), 0.02),
        'ln1_b': nrm(k[19], (DEPTH, D_MODEL), 0.02),
        'ln2_g': 1.0 + nrm(k[20], (DEPTH, D_MODEL), 0.02),
        'ln2_b': nrm(k[21], (DEPTH, D_MODEL), 0.02),
        'ffn_up': nrm(k[22], (DEPTH, D_MODEL, 2 * D_FF), D_MODEL ** -0.5),
        'ffn_conv_w': nrm(k[23], (DEPTH, CONV_W, 2 * D_FF), CONV_W ** -0.5),
        'ffn_conv_b': nrm(k[24], (DEPTH, 2 * D_FF), 0.02),
        'ffn_down': nrm(k[25], (DEPTH, D_FF, D_MODEL), BETA * D_FF ** -0.5),
    }

def reference(x_prompt, x_sample, cache_a_kv, cache_a_kidx, cache_c_kv, state_b_kv, state_c_kv, state_ffn,
              page_table, rel_bias, w_in_ab, w_out_ab, w_in_c, w_out_c, phi_pe, phi_w1, phi_b1, phi_w2,
              ln1_g, ln1_b, ln2_g, ln2_b, ffn_up, ffn_conv_w, ffn_conv_b, ffn_down):
    xp, xs = x_prompt, x_sample
    pa_kv, pa_ki, pb_kv, pc_kv, pc_win, pf = [], [], [], [], [], []
    sa_kv, sa_ki, sb_kv, sc_kv, sc_win, sf = [], [], [], [], [], []
    for layer in range(DEPTH):
        j = layer // 2
        if layer % 2 == 0:
            mp, a_kv, a_ki, b_kv = ab_prompt(xp, w_in_ab[j], rel_bias)
            ms, a_kv_s, a_ki_s, b_kv_s = ab_sample(xs, w_in_ab[j], rel_bias, cache_a_kv[j], cache_a_kidx[j],
                                                   page_table, state_b_kv[j])
            mp, ms = mp @ w_out_ab[j], ms @ w_out_ab[j]
            pa_kv.append(a_kv); pa_ki.append(a_ki); pb_kv.append(b_kv)
            sa_kv.append(a_kv_s); sa_ki.append(a_ki_s); sb_kv.append(b_kv_s)
        else:
            mp, c_kv, c_win = c_prompt(xp, w_in_c[j], phi_pe[j], phi_w1[j], phi_b1[j], phi_w2[j], rel_bias)
            ms, c_kv_s, c_win_s = c_sample(xs, w_in_c[j], phi_pe[j], phi_w1[j], phi_b1[j], phi_w2[j], rel_bias,
                                           cache_c_kv[j], page_table, state_c_kv[j])
            mp, ms = mp @ w_out_c[j], ms @ w_out_c[j]
            pc_kv.append(c_kv); pc_win.append(c_win)
            sc_kv.append(c_kv_s); sc_win.append(c_win_s)
        xp = layer_norm(ALPHA * xp + mp, ln1_g[layer], ln1_b[layer])
        xs = layer_norm(ALPHA * xs + ms, ln1_g[layer], ln1_b[layer])
        zeros = jnp.zeros((xp.shape[0], CONV_W - 1, 2 * D_FF), xp.dtype)
        fp, rp = conv_ffn(xp, zeros, ffn_up[layer], ffn_conv_w[layer], ffn_conv_b[layer], ffn_down[layer])
        fs, rs = conv_ffn(xs, state_ffn[layer], ffn_up[layer], ffn_conv_w[layer], ffn_conv_b[layer], ffn_down[layer])
        pf.append(rp); sf.append(rs)
        xp = layer_norm(ALPHA * xp + fp, ln2_g[layer], ln2_b[layer])
        xs = layer_norm(ALPHA * xs + fs, ln2_g[layer], ln2_b[layer])
    y_prompt, y_sample = xp, xs
    p_a_kv, p_a_kidx, p_b_kv = jnp.stack(pa_kv), jnp.stack(pa_ki), jnp.stack(pb_kv)
    p_c_kv, p_c_win, p_ffn = jnp.stack(pc_kv), jnp.stack(pc_win), jnp.stack(pf)
    s_a_kv, s_a_kidx, s_b_kv = jnp.stack(sa_kv), jnp.stack(sa_ki), jnp.stack(sb_kv)
    s_c_kv, s_c_win, s_ffn = jnp.stack(sc_kv), jnp.stack(sc_win), jnp.stack(sf)
    return (y_prompt, y_sample, p_a_kv, p_a_kidx, p_b_kv, p_c_kv, p_c_win, p_ffn,
            s_a_kv, s_a_kidx, s_b_kv, s_c_kv, s_c_win, s_ffn)


_drawn_inputs = setup_inputs


def setup_inputs(seed=0):
    import zlib

    import numpy as np

    out = dict(_drawn_inputs(seed))
    spreads = {}
    factors = {'cache_c_kv': 3.614, 'rel_bias': 4.48, 'phi_pe': 7.222, 'phi_b1': 8.0, 'ffn_conv_b': 6.125}
    for name, (base, spread) in spreads.items():
        noise = np.random.default_rng([zlib.crc32(name.encode()), seed]).standard_normal(out[name].shape)
        drawn = base * np.exp(spread * noise) if base else spread * noise
        out[name] = __import__('jax').numpy.asarray(drawn.astype(out[name].dtype))
    for name, factor in factors.items():
        out[name] = (out[name] * factor).astype(out[name].dtype)
    return out
```

```python
from contextlib import ExitStack, contextmanager

import concourse.bass as bass
import numpy as np
from concourse import mybir

F32 = mybir.dt.float32
BF16 = mybir.dt.bfloat16
I32 = mybir.dt.int32
ALU = mybir.AluOpType
ACT = mybir.ActivationFunctionType
AX_X = mybir.AxisListType.X

P = 128
D = 1024
KC = D // P
SEQ = 512
NQ = SEQ // P
NB, NS = 8, 8
TS = NB * NS
T = SEQ + TS
TILES = [(i * P, P) for i in range(NQ)] + [(SEQ, TS)]
NT = len(TILES)
PAST = 2048
PAGE = 128
LS = PAST + NS
HD = 64
STRIDE = 16
NCH = PAST // STRIDE
N_HEADS = 16
H_A = H_IDX = H_B = 8
AB_COLS = 2888
C_COLS = 1840
B_WINDOWS = ((128, 1), (512, 4), (2048, 16))
C_WIN = 512
DSA_TOP_PROMPT = 128
DSA_TOP_SAMPLE = 256
N_SEL = 33
SEL_TOP = 16
SEL_BONUS = 1e3
D_FF = 2816
NF = D_FF // P
CONV_W = 3
ALPHA = 4 ** 0.25
LN_EPS = 1e-5
SCALE = HD ** -0.5
IDX_SCALE = HD ** -0.5 * H_IDX ** -0.5
NEG = -1e30
FLOOR = 1e29
TAKEN = -3e38
A_Q, A_K, A_V, A_QI, A_KI, A_W, B_Q, B_K, B_V = 0, 512, 640, 768, 1280, 1344, 1352, 1864, 2376
C_Q, C_KV, C_G = 0, 1024, 1792
TA_K, TA_V, TA_KI, TA_W, TB_K, TB_V, TAB = 0, 128, 256, 320, 328, 840, 1352
TC_G, TC = 768, 816
FAR = 2056
LV = FAR + P
LU = SEQ + 2 * P
KIND_FULL, KIND_WIN, KIND_DIL = 0, 1, 2


class Phase:

    def __init__(self, nc, ctx, name):
        self.nc, self.ctx, self.name, self.sems = nc, ctx, name, []
        self.body = ExitStack()

    def sb(self, name, shape, dt=F32):
        return self.ctx.enter_context(self.nc.sbuf_tensor(f"{self.name}_{name}", shape, dt))

    def ps(self, name, shape, dt=F32):
        return self.ctx.enter_context(self.nc.psum_tensor(f"{self.name}_{name}", shape, dt))

    def sem(self, name):
        s = self.ctx.enter_context(self.nc.semaphore(f"{self.name}_{name}"))
        self.sems.append(s)
        return s


@contextmanager
def phase(nc, name):
    with ExitStack() as ctx:
        p = Phase(nc, ctx, name)
        with p.body:
            yield p
        for s in p.sems:
            nc.gpsimd.sem_clear(s)
        nc.all_engine_barrier()


def setup_phase(nc, io, keep, dram):
    with phase(nc, "setup") as p:
        onehot = p.sb("onehot", [33, 3, LV])
        onehot_up = p.sb("onehot_up", [33, 3, LU])
        tabx = p.sb("tabx", [33, N_HEADS])
        vec_sb = p.sb("vec", [N_HEADS, 3, LV])
        vec_up = p.sb("vec_up", [N_HEADS, 3, LU])
        rep8 = p.sb("rep8", [P, 1], I32)
        pages = p.sb("pages", [P, NB], I32)
        zero = p.sb("zero", [P, D])
        acc = [p.ps(f"acc{i}", [P, 512]) for i in range(4)]
        xps = [p.ps(f"xps{i}", [P, 512]) for i in range(4)]
        loaded, x_in, ones_set, vec_ready, vec_out, stored = (
            p.sem(n) for n in ("loaded", "x_in", "ones_set", "vec_ready", "vec_out", "stored"))
        x_ready, x_out, iota_done, rem_done, idx_done, zero_set, cast_done = (
            p.sem(n) for n in ("x_ready", "x_out", "iota_done", "rem_done", "idx_done", "zero_set", "cast_done"))
        ranges = [(onehot, vec_sb, k, c, min(512, LV - c)) for k in range(3) for c in range(0, LV, 512)]
        ranges += [(onehot_up, vec_up, k, c, min(512, LU - c)) for k in range(3) for c in range(0, LU, 512)]
        block = p.body.enter_context(nc.Block())

        @block.sync
        def _(sp):
            sp.dma_start(keep.xtok[:, 0:NQ, :], io["x_prompt"].rearrange("b (i p) d -> p (b i) d", p=P)).then_inc(x_in, 16)
            sp.dma_start(keep.xtok[0:TS, NQ, :], io["x_sample"].rearrange("b q d -> (b q) d")).then_inc(x_in, 16)
            sp.dma_start(keep.ident[:, :], io["c_ident"]).then_inc(x_in, 16)
            sp.dma_start(onehot[:, :, :], io["c_onehot"]).then_inc(loaded, 16)
            sp.dma_start(onehot_up[:, :, :], io["c_onehot_up"]).then_inc(loaded, 16)
            sp.dma_start(tabx[0:32, :], io["rel_bias"]).then_inc(loaded, 16)
            sp.dma_start(keep.causal[:, :], io["c_causal"]).then_inc(loaded, 16)
            with nc.allow_non_contiguous_dma(reason="one page number for each of a page's 8 chunks"):
                pt = io["page_table"]
                for b in range(NB):
                    sp.dma_start(pages[:, b:b + 1],
                                 bass.AP(tensor=pt.tensor, offset=16 * b, ap=[[1, 16], [0, 8], [1, 1]])).then_inc(loaded, 16)
            sp.wait_ge(vec_out, len(ranges))
            sp.dma_start(dram.vec.rearrange("k h m -> h k m"), vec_sb[:, :, :]).then_inc(stored, 16)
            sp.dma_start(dram.vec_up.rearrange("k h m -> h k m"), vec_up[:, :, :]).then_inc(stored, 16)
            sp.wait_ge(zero_set, 1)
            sp.dma_start(io["o_p_b_kv"][0:3 * SEQ, :].rearrange("(p n) c -> p n c", p=P),
                         zero[:, None, :].to_broadcast([P, 12, D])).then_inc(stored, 16)
            sp.wait_ge(stored, 48)
            sp.wait_ge(loaded, 16 * (4 + NB))

        @block.gpsimd
        def _(pool):
            pool.iota(rep8[:, :], pattern=[[0, 1]], base=0, channel_multiplier=1).then_inc(iota_done, 1)
            pool.memset(zero[:, :], 0.0).then_inc(zero_set, 1)

        @block.tensor
        def _(pe):
            pe.wait_ge(x_in, 48)
            n = 0
            for k in range(KC):
                for t0, tn in ((0, NQ), (NQ, 1)):
                    if n >= 4:
                        pe.wait_ge(x_out, n - 3)
                    for t in range(t0, t0 + tn):
                        w = TILES[t][1]
                        last = pe.transpose(xps[n % 4][:, (t - t0) * P:(t - t0) * P + w],
                                            keep.xtok[0:w, t, k * P:(k + 1) * P], keep.ident[0:w, 0:w])
                    last.then_inc(x_ready, 1)
                    n += 1
            pe.wait_ge(ones_set, 1)
            pe.wait_ge(loaded, 16 * (4 + NB))
            for n, (source, dest, k, c, w) in enumerate(ranges):
                if n >= 4:
                    pe.wait_ge(vec_out, n - 3)
                pe.matmul(acc[n % 4][0:N_HEADS, 0:w], tabx[:, :], source[:, k, c:c + w],
                          start=True, stop=True).then_inc(vec_ready, 1)

        @block.scalar
        def _(act):
            n = 0
            for k in range(KC):
                for t0, w in ((0, SEQ), (SEQ, TS)):
                    act.wait_ge(x_ready, n + 1)
                    act.copy(keep.xT[:, k, t0:t0 + w], xps[n % 4][:, 0:w]).then_inc(x_out, 1)
                    n += 1

        @block.vector
        def _(dve):
            dve.memset(tabx[32:33, :], 1.0).then_inc(ones_set, 1)
            dve.wait_ge(iota_done, 1)
            dve.tensor_single_scalar(rep8[:, :], rep8[:, :], 7, ALU.bitwise_and).then_inc(rem_done, 1)
            dve.wait_ge(rem_done, 1)
            dve.wait_ge(loaded, 16 * (4 + NB))
            for b in range(NB):
                dve.scalar_tensor_tensor(out=keep.chunk_row[:, b:b + 1], in0=pages[:, b:b + 1], scalar=8.0,
                                         in1=rep8[:, :], op0=ALU.mult, op1=ALU.add).then_inc(idx_done, 1)
            dve.wait_ge(x_in, 48)
            dve.tensor_copy(keep.ident_bf[:, :], keep.ident[:, :]).then_inc(cast_done, 1)
            for n, (source, dest, k, c, w) in enumerate(ranges):
                dve.wait_ge(vec_ready, n + 1)
                dve.tensor_copy(dest[:, k, c:c + w], acc[n % 4][0:N_HEADS, 0:w]).then_inc(vec_out, 1)


def project_phase(nc, name, w_in, cols, hT, keep):
    pairs, tail = cols // 256, cols % 256
    loops = pairs // 2
    with phase(nc, name) as p:
        w = p.sb("w", [P, 2, KC, 256])
        stage = p.sb("stage", [P, 4, T])
        acc = [p.ps(f"acc{i}", [P, 512]) for i in range(4)]
        acc_s = [p.ps(f"accs{i}", [P, 512]) for i in range(4)]
        w_in_sem = [p.sem(f"w_loaded{i}") for i in range(2)]
        done, copied, copied_s = p.sem("done"), p.sem("copied"), p.sem("copied_s")
        st_free = [p.sem(f"st_free{i}") for i in range(4)]
        wv = w_in.rearrange("(k p) n -> p k n", p=P)
        blocks = 4 * loops
        rest = [(256 * pr, 256) for pr in range(2 * loops, pairs)] + ([(256 * pairs, tail)] if tail else [])
        block = p.body.enter_context(nc.Block())

        @block.sync
        def _(sp):
            with sp.Fori(0, loops) as i:
                for s in range(2):
                    sp.wait_ge(done, i * 4 + (2 * s + 2))
                    sp.dma_start(w[:, s, :, :], wv[:, :, bass.ds(i * 512 + s * 256, 256)]).then_inc(w_in_sem[s], 16)
            for n, (c0, cw) in enumerate(rest):
                s = n % 2
                sp.wait_ge(done, blocks + 2 * n + 2)
                sp.dma_start(w[:, s, :, 0:cw], wv[:, :, c0:c0 + cw]).then_inc(w_in_sem[s], 16)

        def column_block(pe, n, s, lo, m, slot):
            pe.wait_ge(copied, n + 1)
            pe.wait_ge(copied_s, n + 1)
            for k in range(KC):
                pe.matmul(acc[slot][0:m, :], w[:, s, k, lo:lo + m], keep.xT[:, k, 0:SEQ], start=(k == 0), stop=(k == KC - 1))
            for k in range(KC):
                last = pe.matmul(acc_s[slot][0:m, 0:TS], w[:, s, k, lo:lo + m], keep.xT[:, k, SEQ:T], start=(k == 0), stop=(k == KC - 1))
            last.then_inc(done, 1)

        @block.tensor
        def _(pe):
            pe.sem_inc(done, 4)
            pe.sem_inc(copied, 4)
            pe.sem_inc(copied_s, 4)
            with pe.Fori(0, loops) as i:
                for s in range(2):
                    pe.wait_ge(w_in_sem[s], i * 16 + 16)
                    for j in range(2):
                        column_block(pe, i * 4 + 2 * s + j, s, j * P, P, 2 * s + j)
            n = blocks
            for r, (c0, cw) in enumerate(rest):
                s = r % 2
                pe.wait_ge(w_in_sem[s], 16 * (loops + 1 + r // 2))
                for lo in range(0, cw, P):
                    column_block(pe, n, s, lo, min(P, cw - lo), (n - blocks) % 4)
                    n += 1

        rest_blocks = [(c0 + lo, min(P, cw - lo)) for c0, cw in rest for lo in range(0, cw, P)]

        @block.scalar
        def _(act):
            for slot in range(4):
                act.sem_inc(st_free[slot], 16)

            def evacuate(n, i, slot, row, m):
                act.wait_ge(done, n + 5)
                act.wait_ge(st_free[slot], i * 16 + 16)
                act.copy(stage[0:m, slot, 0:SEQ], acc[slot][0:m, :]).then_inc(copied, 1)
                act.wait_ge(copied, n + 5)
                act.wait_ge(copied_s, n + 5)
                act.dma_start(hT[bass.ds(row, m), :], stage[0:m, slot, :]).then_inc(st_free[slot], 16)

            with act.Fori(0, loops) as i:
                for j in range(4):
                    evacuate(i * 4 + j, i, j, i * 512 + j * P, P)
            for r, (c0, m) in enumerate(rest_blocks):
                evacuate(blocks + r, loops + r // 4, r % 4, c0, m)
            for slot in range(4):
                act.wait_ge(st_free[slot], 16 + 16 * len(range(slot, blocks + len(rest_blocks), 4)))

        @block.vector
        def _(dve):
            def evacuate(n, i, slot, m):
                dve.wait_ge(done, n + 5)
                dve.wait_ge(st_free[slot], i * 16 + 16)
                dve.tensor_copy(stage[0:m, slot, SEQ:T], acc_s[slot][0:m, 0:TS]).then_inc(copied_s, 1)

            with dve.Fori(0, loops) as i:
                for j in range(4):
                    evacuate(i * 4 + j, i, j, P)
            for r, (c0, m) in enumerate(rest_blocks):
                evacuate(blocks + r, loops + r // 4, r % 4, m)


def token_major_phase(nc, name, hT, pieces, tok, stores, keep):
    chunks = [(r0 + o, min(P, n - o), c0 + o) for r0, n, c0 in pieces for o in range(0, n, P)]
    with phase(nc, name) as p:
        rows = p.sb("rows", [P, len(chunks), T])
        tp = [p.ps(f"tp{i}", [P, 512]) for i in range(4)]
        rows_in, turned, out_done, stored = (p.sem(n) for n in ("rows_in", "turned", "out_done", "stored"))
        row_sem = [p.sem(f"row_in{i}") for i in range(len(chunks))]
        block = p.body.enter_context(nc.Block())

        @block.sync
        def _(sp):
            for i, (r0, n, _) in enumerate(chunks):
                sp.dma_start(rows[0:n, i, :], hT[r0:r0 + n, :]).then_inc(row_sem[i], 16)
            sp.wait_ge(out_done, 2 * len(chunks))
            for dst, src in stores:
                sp.dma_start(dst, src).then_inc(stored, 16)
            sp.wait_ge(stored, 16 * len(stores))

        @block.tensor
        def _(pe):
            for i, (_, n, _) in enumerate(chunks):
                pe.wait_ge(row_sem[i], 16)
                for half, (t0, tn) in enumerate(((0, NQ), (NQ, 1))):
                    u = 2 * i + half
                    if u >= 4:
                        pe.wait_ge(out_done, u - 3)
                    for t in range(t0, t0 + tn):
                        lo, w = TILES[t]
                        last = pe.transpose(tp[u % 4][0:w, (t - t0) * P:(t - t0) * P + n], rows[0:n, i, lo:lo + w],
                                            keep.ident[0:n, 0:n])
                    last.then_inc(turned, 1)

        @block.vector
        def _(dve):
            for i, (_, n, c0) in enumerate(chunks):
                for half in range(2):
                    u = 2 * i + half
                    dve.wait_ge(turned, u + 1)
                    if half == 0:
                        src = tp[u % 4][:, :].rearrange("p (t c) -> p t c", t=NQ)[:, :, 0:n]
                        dve.tensor_copy(tok[:, 0:NQ, c0:c0 + n], src).then_inc(out_done, 1)
                    else:
                        dve.tensor_copy(tok[0:TS, NQ, c0:c0 + n], tp[u % 4][0:TS, 0:n]).then_inc(out_done, 1)


def prompt_indexer_phase(nc, hT, tok, sel_bias, keep):
    with phase(nc, "pidx") as p:
        qi = p.sb("qi", [HD, H_IDX, SEQ])
        ki = p.sb("ki", [HD, SEQ])
        relu = p.sb("relu", [P, 3, SEQ])
        score = p.sb("score", [P, 3, 2, SEQ])
        best = p.sb("best", [P, 2, 8])
        dots = [p.ps(f"dots{i}", [P, SEQ]) for i in range(4)]
        loaded, dot_done, relu_done, summed, picked, marked, biased = (
            p.sem(n) for n in ("loaded", "dot_done", "relu_done", "summed", "picked", "marked", "biased"))
        steps = [(i, h) for i in range(1, NQ) for h in range(H_IDX)]
        block = p.body.enter_context(nc.Block())

        @block.sync
        def _(sp):
            sp.dma_start(qi[:, :, :], hT[A_QI:A_QI + H_IDX * HD, 0:SEQ].rearrange("(h e) t -> e h t", e=HD)).then_inc(loaded, 16)
            sp.dma_start(ki[:, :], hT[A_KI:A_KI + HD, 0:SEQ]).then_inc(loaded, 16)

        @block.tensor
        def _(pe):
            pe.wait_ge(loaded, 32)
            for n, (i, h) in enumerate(steps):
                if n >= 4:
                    pe.wait_ge(relu_done, n - 3)
                L = (i + 1) * P
                pe.matmul(dots[n % 4][:, 0:L], qi[:, h, i * P:(i + 1) * P], ki[:, 0:L], start=True, stop=True).then_inc(dot_done, 1)

        @block.scalar
        def _(act):
            for n, (i, h) in enumerate(steps):
                L = (i + 1) * P
                act.wait_ge(dot_done, n + 1)
                if n >= 3:
                    act.wait_ge(summed, n - 2)
                act.activation(relu[:, n % 3, 0:L], dots[n % 4][:, 0:L], ACT.Relu, scale=IDX_SCALE).then_inc(relu_done, 1)

        @block.vector
        def _(dve):
            for n, (i, h) in enumerate(steps):
                L = (i + 1) * P
                w = tok[:, i, TA_W + h:TA_W + h + 1]
                dve.wait_ge(relu_done, n + 1)
                if h:
                    dve.wait_ge(summed, n)
                    dve.scalar_tensor_tensor(out=score[:, i - 1, h % 2, 0:L], in0=relu[:, n % 3, 0:L], scalar=w,
                                             in1=score[:, i - 1, (h + 1) % 2, 0:L], op0=ALU.mult, op1=ALU.add).then_inc(summed, 1)
                else:
                    dve.tensor_scalar(score[:, i - 1, 0, 0:L], relu[:, n % 3, 0:L], w, None, ALU.mult).then_inc(summed, 1)
            dve.wait_ge(summed, len(steps))
            last = (H_IDX - 1) % 2
            for i in range(1, NQ):
                s = score[:, i - 1, last, i * P:(i + 1) * P]
                dve.tensor_tensor(s, s, keep.causal[:, :], ALU.add).then_inc(summed, 1)
            dve.wait_ge(summed, len(steps) + 3)
            n = 0
            for i in range(1, NQ):
                s = score[:, i - 1, last, 0:(i + 1) * P]
                for r in range(DSA_TOP_PROMPT // 8):
                    if n:
                        dve.wait_ge(marked, n)
                    dve.max(best[:, n % 2, :], s).then_inc(picked, 1)
                    dve.wait_ge(picked, n + 1)
                    dve.match_replace(out=s, in_to_replace=best[:, n % 2, :], in_values=s, imm_value=TAKEN).then_inc(marked, 1)
                    n += 1
                dve.wait_ge(marked, n)
                dve.tensor_scalar(sel_bias[:, i - 1, 0:(i + 1) * P], s, TAKEN / 2, NEG, ALU.is_gt, ALU.mult).then_inc(biased, 1)


def prompt_attention_phase(nc, name, branches, hT, vec_up, tok, mix, keep):
    with phase(nc, name) as p:
        kmax = max(b["kv"] for b in branches)
        table = p.sb("table", [P, 2, 4, SEQ + P])
        kT = p.sb("kT", [HD, 2, kmax, SEQ])
        q = p.sb("q", [HD, 3, SEQ])
        shifted = p.sb("shifted", [P, 2, SEQ])
        probs = p.sb("probs", [P, 2, SEQ])
        pT = p.sb("pT", [P, 2, SEQ])
        nmax = p.sb("nmax", [P, 4])
        total = p.sb("total", [P, 4])
        weight = p.sb("weight", [P, 4])
        logit = [p.ps(f"logit{i}", [P, SEQ]) for i in range(2)]
        tps = [p.ps(f"tps{i}", [P, SEQ]) for i in range(2)]
        out = [p.ps(f"out{i}", [P, SEQ]) for i in range(2)]
        names = ("logit_ready", "shifted_ready", "probs_ready", "turned", "pT_ready0", "pT_ready1", "out_ready",
                 "weighed", "mixed", "k_scaled")
        logit_ready, shifted_ready, probs_ready, turned, pT0, pT1, out_ready, weighed, mixed, k_scaled = (p.sem(n) for n in names)
        pT_ready = [pT0, pT1]
        k_in, inverted = p.sem("k_in"), p.sem("inverted")
        q_in = [p.sem(f"q_in{i}") for i in range(3)]
        t_in = [p.sem(f"table_in{i}") for i in range(2)]
        heads = [(br, h) for br in range(len(branches)) for h in range(branches[br]["heads"])]
        steps = [(n, i) for n in range(len(heads)) for i in range(NQ)]
        S = len(steps)
        block = p.body.enter_context(nc.Block())

        @block.sync
        def _(sp):
            for br, b in enumerate(branches):
                rows = hT[b["k"]:b["k"] + b["kv"] * HD, 0:SEQ].rearrange("(g e) t -> e g t", e=HD)
                sp.dma_start(kT[:, br % 2, 0:b["kv"], :], rows).then_inc(k_in, 16)
            for n, (br, h) in enumerate(heads):
                b = branches[br]
                if n % 4 == 0:
                    g = n // 4
                    if g >= 2:
                        sp.wait_ge(shifted_ready, 16 * (g - 1))
                    first = (b["kind"] * N_HEADS + b["h0"] + h) * LU
                    sp.dma_start(table[:, g % 2, :, :], bass.AP(tensor=vec_up.tensor, offset=first,
                                                                ap=[[1, P], [LU, 4], [1, SEQ + P]])).then_inc(t_in[g % 2], 16)
                if n >= 3:
                    sp.wait_ge(logit_ready, 4 * (n - 2))
                sp.dma_start(q[:, n % 3, :], hT[b["q"] + h * HD:b["q"] + (h + 1) * HD, 0:SEQ]).then_inc(q_in[n % 3], 16)

        @block.tensor
        def _(pe):
            def scores(s):
                n, i = steps[s]
                br, h = heads[n]
                b = branches[br]
                L = (i + 1) * P
                if i == 0:
                    pe.wait_ge(q_in[n % 3], 16 * (n // 3 + 1))
                    if h == 0:
                        pe.wait_ge(k_scaled, br + 1)
                if s >= 2:
                    pe.wait_ge(shifted_ready, s - 1)
                sel = b["sel"] is not None and i > 0
                g = h // (b["heads"] // b["kv"])
                mm = pe.matmul(logit[s % 2][:, 0:L], q[:, n % 3, i * P:(i + 1) * P], kT[:, br % 2, g, 0:L], start=True, stop=not sel)
                if sel:
                    mm = pe.matmul(logit[s % 2][:, 0:L], keep.ident_bf[:, :], b["sel"][:, i - 1, 0:L], start=False, stop=True)
                mm.then_inc(logit_ready, 1)

            def turn(s):
                i = steps[s][1]
                pe.wait_ge(probs_ready, s + 1)
                if s >= 2:
                    pe.wait_ge(pT_ready[s % 2], s // 2)
                for kt in range(i + 1):
                    last = pe.transpose(tps[s % 2][:, kt * P:(kt + 1) * P], probs[:, s % 2, kt * P:(kt + 1) * P], keep.ident[:, :])
                last.then_inc(turned, 1)

            def values(s):
                n, i = steps[s]
                br, h = heads[n]
                b = branches[br]
                g = h // (b["heads"] // b["kv"])
                pe.wait_ge(pT_ready[s % 2], s // 2 + 1)
                if s >= 2:
                    pe.wait_ge(mixed, s - 1)
                for kt in range(i + 1):
                    v = tok[:, kt, b["v"] + g * HD:b["v"] + (g + 1) * HD]
                    last = pe.matmul(out[s % 2][:, 0:HD], pT[:, s % 2, kt * P:(kt + 1) * P], v, start=(kt == 0), stop=(kt == i))
                last.then_inc(out_ready, 1)

            for s in range(S + 2):
                if s < S:
                    scores(s)
                if 1 <= s <= S:
                    turn(s - 1)
                if s >= 2:
                    values(s - 2)

        @block.scalar
        def _(act):
            for br, b in enumerate(branches):
                act.wait_ge(k_in, 16 * len(branches))
                act.mul(kT[:, br % 2, 0:b["kv"], :], kT[:, br % 2, 0:b["kv"], :], SCALE).then_inc(k_scaled, 1)

            def copy_turned(s):
                L = (steps[s][1] + 1) * P
                act.wait_ge(turned, s + 1)
                if s >= 2:
                    act.wait_ge(out_ready, s - 1)
                act.copy(pT[:, s % 2, 0:L], tps[s % 2][:, 0:L]).then_inc(pT_ready[s % 2], 1)

            for s in range(S + 1):
                if s < S:
                    L = (steps[s][1] + 1) * P
                    act.wait_ge(shifted_ready, s + 1)
                    if s >= 2:
                        act.wait_ge(turned, s - 1)
                    if s >= 4:
                        act.wait_ge(weighed, s - 3)
                    act.activation(probs[:, s % 2, 0:L], shifted[:, s % 2, 0:L], ACT.Exp, bias=nmax[:, s % 4:s % 4 + 1], scale=-1.0,
                                   accum_out=total[:, s % 4:s % 4 + 1]).then_inc(probs_ready, 1)
                if s >= 1 and (s - 1) % 2 == 0:
                    copy_turned(s - 1)

        @block.vector
        def _(dve):
            def shift(s):
                n, i = steps[s]
                L = (i + 1) * P
                dve.wait_ge(logit_ready, s + 1)
                if n % 4 == 0 and i == 0:
                    dve.wait_ge(t_in[(n // 4) % 2], 16 * (n // 8 + 1))
                if s >= 2:
                    dve.wait_ge(probs_ready, s - 1)
                row = table[:, (n // 4) % 2, n % 4, 0:L]
                bias = bass.AP(tensor=row.tensor, offset=row.offset + L - 1, ap=[list(row.ap[0]), [-1, L]])
                dve.tensor_tensor_reduce(out=shifted[:, s % 2, 0:L], in0=logit[s % 2][:, 0:L], in1=bias, scale=-1.0, scalar=FLOOR,
                                         op0=ALU.add, op1=ALU.min, accum_out=nmax[:, s % 4:s % 4 + 1]).then_inc(shifted_ready, 1)

            def copy_turned(s):
                L = (steps[s][1] + 1) * P
                dve.wait_ge(turned, s + 1)
                if s >= 2:
                    dve.wait_ge(out_ready, s - 1)
                dve.tensor_copy(pT[:, s % 2, 0:L], tps[s % 2][:, 0:L]).then_inc(pT_ready[s % 2], 1)

            def mix_in(s):
                n, i = steps[s]
                br, h = heads[n]
                b = branches[br]
                w = weight[:, s % 4:s % 4 + 1]
                dst = mix[:, i, b["out"] + h * HD:b["out"] + (h + 1) * HD]
                dve.wait_ge(weighed, s + 1)
                dve.wait_ge(out_ready, s + 1)
                if b["gate"] is None:
                    dve.tensor_scalar(dst, out[s % 2][:, 0:HD], w, None, ALU.mult).then_inc(mixed, 1)
                else:
                    dve.scalar_tensor_tensor(out=dst, in0=out[s % 2][:, 0:HD], scalar=w, in1=dst, op0=ALU.mult, op1=ALU.add).then_inc(mixed, 1)

            def weigh(s):
                n, i = steps[s]
                br, h = heads[n]
                b = branches[br]
                dve.wait_ge(probs_ready, s + 1)
                if s >= 4:
                    dve.wait_ge(mixed, s - 3)
                w, t = weight[:, s % 4:s % 4 + 1], total[:, s % 4:s % 4 + 1]
                if b["gate"] is None:
                    dve.reciprocal(w, t).then_inc(weighed, 1)
                else:
                    dve.reciprocal(w, t).then_inc(inverted, 1)
                    dve.wait_ge(inverted, s + 1)
                    dve.tensor_tensor(w, keep.gate_tok[:, i, b["gate"] + h:b["gate"] + h + 1], w, ALU.mult).then_inc(weighed, 1)

            for s in range(S + 3):
                if s < S:
                    shift(s)
                if 1 <= s <= S:
                    if (s - 1) % 2 == 1:
                        copy_turned(s - 1)
                    weigh(s - 1)
                if s >= 3:
                    mix_in(s - 3)



def sample_indexer_phase(nc, hT, cache_kidx, io, sel_mask, keep):
    rows_in_cache = cache_kidx.rearrange("n (c j) e -> (n c) (j e)", j=STRIDE)
    with phase(nc, "sidx") as p:
        kidx = p.sb("kidx", [P, NB, STRIDE * HD])
        kT = p.sb("kT", [P, 2, NCH * 8])
        relu = p.sb("relu", [P, 2, NCH * 8])
        part = p.sb("part", [16, 2, NCH * 8])
        q = p.sb("q", [HD, H_IDX, TS])
        q_blk = p.sb("q_blk", [P, NB, P])
        k_new = p.sb("k_new", [HD, TS])
        w_col = p.sb("w_col", [P, NB])
        w_sel = p.sb("w_sel", [P, NB, 16])
        relu_new = p.sb("relu_new", [TS, NB, NS])
        new_part = p.sb("new_part", [NS, NB, NS])
        raw = p.sb("raw", [TS, LS])
        score = p.sb("score", [TS, LS])
        best = p.sb("best", [TS, 2, 8])
        tps = [p.ps(f"tps{i}", [P, 512]) for i in range(2)]
        dots = [p.ps(f"dots{i}", [P, 512]) for i in range(2)]
        sums = [p.ps(f"sums{i}", [P, 512]) for i in range(2)]
        dots_new = p.ps("dots_new", [P, 512])
        sums_new = p.ps("sums_new", [P, 512])
        (loaded, zeroed, built, turned, kT_ready, dot_done, relu_done, sum_done, part_done, new_dots, new_relu, new_sums,
         new_out, stored, natural, masked, picked, marked) = (p.sem(n) for n in (
             "loaded", "zeroed", "built", "turned", "kT_ready", "dot_done", "relu_done", "sum_done", "part_done", "new_dots",
             "new_relu", "new_sums", "new_out", "stored", "natural", "masked", "picked", "marked"))
        kidx_in = keep.kidx_in
        parts_out = [p.sem(f"parts_out{i}") for i in range(2)]
        halves = [(b, f) for b in range(NB) for f in range(2)]
        block = p.body.enter_context(nc.Block())

        @block.gpsimd
        def _(pool):
            for b in range(NB):
                pool.indirect_dma_start(out=kidx[:, b, :], out_offset=None, in_=rows_in_cache,
                                        in_offset=bass.IndirectOffsetOnAxis(ap=keep.chunk_row[:, b:b + 1], axis=0)).then_inc(kidx_in[b], 16)

        @block.sync
        def _(sp):
            sp.dma_start(q[:, :, :], hT[A_QI:A_QI + H_IDX * HD, SEQ:T].rearrange("(h e) t -> e h t", e=HD)).then_inc(loaded, 16)
            sp.dma_start(k_new[:, :], hT[A_KI:A_KI + HD, SEQ:T]).then_inc(loaded, 16)
            with nc.allow_non_contiguous_dma(reason="indexer weights, one per partition"):
                for j2 in range(2):
                    for h in range(H_IDX):
                        r = j2 * 64 + h * NS
                        sp.dma_start(w_col[r:r + NS, :], hT[A_W + h, SEQ:T].rearrange("(b q) -> q b", q=NS)).then_inc(loaded, 16)
            for b in range(NB):
                sp.wait_ge(part_done, 2 * (b + 1))
                for j2 in range(2):
                    sp.dma_start(raw[b * NS:(b + 1) * NS, j2 * 1024:(j2 + 1) * 1024],
                                 part[j2 * NS:(j2 + 1) * NS, b % 2, :]).then_inc(parts_out[b % 2], 16)
            sp.wait_ge(new_out, 1)
            for b in range(NB):
                sp.dma_start(raw[b * NS:(b + 1) * NS, PAST:LS], new_part[:, b, :]).then_inc(stored, 16)

        @block.tensor
        def _(pe):
            pe.wait_ge(built, 3)
            for b in range(NB):
                pe.matmul(dots_new[0:TS, b * NS:(b + 1) * NS], q_blk[0:HD, b, 0:TS], k_new[:, b * NS:(b + 1) * NS],
                          start=True, stop=True).then_inc(new_dots, 1)
            pe.wait_ge(new_relu, 1)
            for b in range(NB):
                pe.matmul(sums_new[0:NS, b * NS:(b + 1) * NS], w_sel[0:TS, b, 0:NS], relu_new[:, b, :], start=True, stop=True).then_inc(new_sums, 1)

            def turn(n):
                b, f = halves[n]
                if f == 0:
                    pe.wait_ge(kidx_in[b], 16)
                if n >= 2:
                    pe.wait_ge(kT_ready, n - 1)
                for m in range(4):
                    j = 2 * (4 * f + m)
                    last = pe.transpose(tps[n % 2][:, m * P:(m + 1) * P], kidx[:, b, j * HD:(j + 2) * HD], keep.ident[:, :])
                last.then_inc(turned, 1)

            def dot(n):
                b, f = halves[n]
                pe.wait_ge(kT_ready, n + 1)
                if n >= 2:
                    pe.wait_ge(relu_done, n - 1)
                pe.matmul(dots[n % 2][:, :], q_blk[:, b, :], kT[:, b % 2, f * 512:(f + 1) * 512], start=True, stop=True).then_inc(dot_done, 1)

            def head_sum(n):
                b, f = halves[n]
                pe.wait_ge(relu_done, n + 1)
                if n >= 2:
                    pe.wait_ge(part_done, n - 1)
                pe.matmul(sums[n % 2][0:16, :], w_sel[:, b, :], relu[:, b % 2, f * 512:(f + 1) * 512], start=True, stop=True).then_inc(sum_done, 1)

            N = len(halves)
            for n in range(N + 2):
                if n < N:
                    turn(n)
                if 1 <= n <= N:
                    dot(n - 1)
                if n >= 2:
                    head_sum(n - 2)

        @block.scalar
        def _(act):
            act.wait_ge(new_dots, NB)
            act.activation(relu_new[:, :, :], dots_new[0:TS, 0:TS].rearrange("p (b t) -> p b t", b=NB), ACT.Relu, scale=IDX_SCALE).then_inc(new_relu, 1)
            for n, (b, f) in enumerate(halves):
                act.wait_ge(dot_done, n + 1)
                if n >= 4:
                    act.wait_ge(sum_done, n - 3)
                act.activation(relu[:, b % 2, f * 512:(f + 1) * 512], dots[n % 2][:, :], ACT.Relu, scale=IDX_SCALE).then_inc(relu_done, 1)

        @block.vector
        def _(dve):
            dve.memset(q_blk[:, :, :], 0.0).then_inc(zeroed, 1)
            dve.wait_ge(zeroed, 1)
            dve.wait_ge(loaded, 16 * (2 + 2 * H_IDX))
            src = q[:, :, :].rearrange("e h (b q) -> e b h q", q=NS)
            for j2 in range(2):
                dst = q_blk[j2 * HD:(j2 + 1) * HD, :, j2 * TS:(j2 + 1) * TS].rearrange("e b (h q) -> e b h q", q=NS)
                dve.tensor_copy(dst, src).then_inc(built, 1)
            for b in range(NB):
                last = dve.tensor_scalar(w_sel[:, b, :], keep.same_token[:, :], w_col[:, b:b + 1], None, ALU.mult)
            last.then_inc(built, 1)
            dve.wait_ge(new_sums, NB)
            dve.tensor_copy(new_part[:, :, :], sums_new[0:NS, 0:TS].rearrange("p (b t) -> p b t", b=NB)).then_inc(new_out, 1)
            N = len(halves)
            for n in range(N + 2):
                if n < N:
                    b, f = halves[n]
                    dve.wait_ge(turned, n + 1)
                    if n >= 4:
                        dve.wait_ge(dot_done, n - 3)
                    dve.tensor_copy(kT[:, b % 2, f * 512:(f + 1) * 512], tps[n % 2][:, :]).then_inc(kT_ready, 1)
                if n >= 2:
                    b, f = halves[n - 2]
                    dve.wait_ge(sum_done, n - 1)
                    if b >= 2:
                        dve.wait_ge(parts_out[b % 2], 32 * (b // 2))
                    dve.tensor_copy(part[:, b % 2, f * 512:(f + 1) * 512], sums[n % 2][0:16, :]).then_inc(part_done, 1)
            for i in range(2):
                dve.wait_ge(parts_out[i], 32 * NB // 2)
            dve.wait_ge(stored, 16 * NB)
            dve.tensor_copy(score[:, 0:PAST].rearrange("r (c m s) -> r s m c", s=2, m=8),
                            raw[:, 0:PAST].rearrange("r (s m c) -> r s m c", s=2, m=8)).then_inc(natural, 1)
            dve.tensor_tensor(score[:, PAST:LS], raw[:, PAST:LS], keep.new_causal[0:TS, :], ALU.add).then_inc(natural, 1)
            dve.wait_ge(natural, 2)
            for r in range(DSA_TOP_SAMPLE // 8):
                if r:
                    dve.wait_ge(marked, r)
                dve.max(best[:, r % 2, :], score[:, :]).then_inc(picked, 1)
                dve.wait_ge(picked, r + 1)
                dve.match_replace(out=score[:, :], in_to_replace=best[:, r % 2, :], in_values=score[:, :], imm_value=TAKEN).then_inc(marked, 1)
            dve.wait_ge(marked, DSA_TOP_SAMPLE // 8)
            dve.tensor_scalar(sel_mask[:, 0:PAST].rearrange("r (j c) -> r c j", j=STRIDE),
                              score[:, 0:PAST].rearrange("r (c j) -> r c j", j=STRIDE), TAKEN / 2, NEG, ALU.is_gt, ALU.mult).then_inc(masked, 1)
            dve.tensor_scalar(sel_mask[:, PAST:LS], score[:, PAST:LS], TAKEN / 2, NEG, ALU.is_gt, ALU.mult).then_inc(masked, 1)


def query_blocks(dve, dst, src, groups, heads_per_group, done):
    for g in range(groups):
        h0, n = g * heads_per_group, heads_per_group
        out = dst[g * HD:(g + 1) * HD, :, h0 * NS:(h0 + n) * NS].rearrange("e b (h q) -> e b h q", q=NS)
        dve.tensor_scalar(out, src[:, h0:h0 + n, :].rearrange("e h (b q) -> e b h q", q=NS), SCALE, None, ALU.mult).then_inc(done, 1)


def sample_table(sp, dst, vec, kind, h0, heads, lo, n, done):
    for q in range(NS):
        first = (kind * N_HEADS + h0) * LV + FAR - PAST - q + lo
        sp.dma_start(dst[q:(heads - 1) * NS + q + 1:NS, :], bass.AP(tensor=vec.tensor, offset=first, ap=[[LV, heads], [1, n]])).then_inc(done, 16)


def sample_a_phase(nc, hT, vec, cache_kv, new_kv, io, sel_mask, keep):
    rows_in_cache = cache_kv.rearrange("n (c j) s g e -> (n c) (j s g e)", j=STRIDE)
    R = H_A * NS
    with phase(nc, "sa") as p:
        kv = p.sb("kv", [P, 2, STRIDE * 256])
        kT = p.sb("kT", [P, 2, LS])
        k_new = p.sb("k_new", [P, TS])
        v_new = p.sb("v_new", [NS, NB, P])
        q = p.sb("q", [HD, H_A, TS])
        q_blk = p.sb("q_blk", [P, NB, R])
        nat = p.sb("nat", [R, LS])
        table = p.sb("table", [R, LS])
        pick = p.sb("pick", [TS, NB, R], BF16)
        shifted = p.sb("shifted", [R, LS])
        probs = p.sb("probs", [R, LS])
        pT = p.sb("pT", [P, STRIDE + 1, R])
        o = p.sb("o", [R, 2, HD])
        nmax = p.sb("nmax", [R, 2])
        total = p.sb("total", [R, 2])
        rinv = p.sb("rinv", [R, 2])
        logit = p.ps("logit", [P, 5 * 512])
        tps = [p.ps(f"tps{i}", [P, 512]) for i in range(2)]
        outp = p.ps("outp", [P, 512])
        (loaded, t_in, zeroed, built, tabled, turned_k, kT_ready, kT_new, logit_ready, shifted_ready, probs_ready, turned_p,
         pT_ready, out_ready, weighed, o_ready, o_turned, mixed) = (p.sem(n) for n in (
             "loaded", "t_in", "zeroed", "built", "tabled", "turned_k", "kT_ready", "kT_new", "logit_ready", "shifted_ready",
             "probs_ready", "turned_p", "pT_ready", "out_ready", "weighed", "o_ready", "o_turned", "mixed"))
        kv_in = keep.a_kv_in
        block = p.body.enter_context(nc.Block())

        @block.gpsimd
        def _(pool):
            for b in range(NB):
                if b >= 2:
                    pool.wait_ge(out_ready, b - 1)
                pool.indirect_dma_start(out=kv[:, b % 2, :], out_offset=None, in_=rows_in_cache,
                                        in_offset=bass.IndirectOffsetOnAxis(ap=keep.chunk_row[:, b:b + 1], axis=0)).then_inc(kv_in[b % 2], 16)

        @block.sync
        def _(sp):
            sp.dma_start(q[:, :, :], hT[A_Q:A_Q + H_A * HD, SEQ:T].rearrange("(h e) t -> e h t", e=HD)).then_inc(loaded, 16)
            sp.dma_start(k_new[:, :], hT[A_K:A_K + P, SEQ:T]).then_inc(loaded, 16)
            sp.dma_start(v_new[:, :, :], new_kv[:, :, P:2 * P].rearrange("b q c -> q b c")).then_inc(loaded, 16)
            sample_table(sp, nat, vec, KIND_FULL, 0, H_A, 0, LS, t_in)

        @block.tensor
        def _(pe):
            pe.wait_ge(built, 3)

            def keys(b):
                pe.wait_ge(kv_in[b % 2], 16 * (b // 2 + 1))
                for m in range(4):
                    n = 4 * b + m
                    if n >= 2:
                        pe.wait_ge(kT_ready, n - 1)
                    if m < 2 and b >= 2:
                        pe.wait_ge(pT_ready, 3 * (b - 1))
                    for i in range(4):
                        j = 4 * m + i
                        last = pe.transpose(tps[n % 2][:, i * P:(i + 1) * P], kv[:, b % 2, j * 256:j * 256 + P], keep.ident[:, :])
                    last.then_inc(turned_k, 1)

            def scores(b):
                pe.wait_ge(kT_ready, 4 * b + 4)
                pe.wait_ge(kT_new, b + 1)
                if b:
                    pe.wait_ge(shifted_ready, b)
                for c in range(0, LS, 512):
                    w = min(512, LS - c)
                    pe.matmul(logit[0:R, c:c + w], q_blk[:, b, :], kT[:, b % 2, c:c + w], start=True, stop=False)
                    last = pe.matmul(logit[0:R, c:c + w], pick[:, b, :], sel_mask[:, c:c + w], start=False, stop=True)
                last.then_inc(logit_ready, 1)

            def turn(b):
                pe.wait_ge(probs_ready, b + 1)
                for m in range(3):
                    if m == 0:
                        pe.wait_ge(kT_ready, min(4 * b + 8, 4 * NB))
                    if m == 2:
                        pe.wait_ge(pT_ready, 3 * b + 1)
                    n = 8 if m < 2 else 1
                    for i in range(n):
                        j = 8 * m + i
                        w = P if m < 2 else NS
                        last = pe.transpose(tps[m % 2][0:w, i * R:(i + 1) * R], probs[:, j * P:j * P + w], keep.ident[0:R, 0:R])
                    last.then_inc(turned_p, 1)

            def values(b):
                pe.wait_ge(pT_ready, 3 * b + 3)
                if b:
                    pe.wait_ge(mixed, 2 * b)
                for j in range(STRIDE):
                    pe.matmul(outp[0:R, 0:P], pT[:, j, :], kv[:, b % 2, j * 256 + P:(j + 1) * 256], start=(j == 0), stop=False)
                pe.matmul(outp[0:R, 0:P], pT[0:NS, STRIDE, :], v_new[:, b, :], start=False, stop=True).then_inc(out_ready, 1)
                pe.wait_ge(o_ready, 2 * b + 2)
                pe.transpose(outp[0:HD, 256:256 + R], o[:, b % 2, :], keep.ident[0:R, 0:R]).then_inc(o_turned, 1)

            keys(0)
            for b in range(NB):
                scores(b)
                if b + 1 < NB:
                    keys(b + 1)
                turn(b)
                values(b)

        @block.scalar
        def _(act):
            def copy_keys(b):
                if b >= 2:
                    act.wait_ge(logit_ready, b - 1)
                for m in range(4):
                    act.wait_ge(turned_k, 4 * b + m + 1)
                    act.copy(kT[:, b % 2, m * 512:(m + 1) * 512], tps[m % 2][:, :]).then_inc(kT_ready, 1)
                act.copy(kT[:, b % 2, PAST:LS], k_new[:, b * NS:(b + 1) * NS]).then_inc(kT_new, 1)

            act.wait_ge(built, 3)
            copy_keys(0)
            for b in range(NB):
                if b + 1 < NB:
                    copy_keys(b + 1)
                act.wait_ge(shifted_ready, b + 1)
                if b:
                    act.wait_ge(turned_p, 3 * b)
                if b >= 2:
                    act.wait_ge(weighed, b - 1)
                act.activation(probs[:, :], shifted[:, :], ACT.Exp, bias=nmax[:, b % 2:b % 2 + 1], scale=-1.0,
                               accum_out=total[:, b % 2:b % 2 + 1]).then_inc(probs_ready, 1)

        @block.vector
        def _(dve):
            dve.memset(q_blk[:, :, :], 0.0).then_inc(zeroed, 1)
            dve.wait_ge(zeroed, 1)
            dve.wait_ge(loaded, 48)
            query_blocks(dve, q_blk, q, 2, H_A // 2, built)
            dve.tensor_copy(pick[:, :, :], keep.pick_row[:, :, :]).then_inc(built, 1)
            dve.wait_ge(t_in, 16 * NS)
            dve.tensor_copy(table[:, 0:PAST].rearrange("r (j c) -> r c j", j=STRIDE),
                            nat[:, 0:PAST].rearrange("r (c j) -> r c j", j=STRIDE)).then_inc(tabled, 1)
            dve.tensor_copy(table[:, PAST:LS], nat[:, PAST:LS]).then_inc(tabled, 1)
            dve.wait_ge(tabled, 2)
            for b in range(NB):
                dve.wait_ge(logit_ready, b + 1)
                if b:
                    dve.wait_ge(probs_ready, b)
                dve.tensor_tensor_reduce(out=shifted[:, :], in0=logit[0:R, 0:LS], in1=table[:, :], scale=-1.0, scalar=FLOOR,
                                         op0=ALU.add, op1=ALU.min, accum_out=nmax[:, b % 2:b % 2 + 1]).then_inc(shifted_ready, 1)
                for m in range(3):
                    dve.wait_ge(turned_p, 3 * b + m + 1)
                    if b:
                        dve.wait_ge(out_ready, b)
                    if m < 2:
                        dve.tensor_copy(pT[:, 8 * m:8 * m + 8, :], tps[m % 2][:, :].rearrange("p (j r) -> p j r", r=R)).then_inc(pT_ready, 1)
                    else:
                        dve.tensor_copy(pT[0:NS, STRIDE, :], tps[0][0:NS, 0:R]).then_inc(pT_ready, 1)
                dve.reciprocal(rinv[:, b % 2:b % 2 + 1], total[:, b % 2:b % 2 + 1]).then_inc(weighed, 1)
                dve.wait_ge(weighed, b + 1)
                dve.wait_ge(out_ready, b + 1)
                if b >= 2:
                    dve.wait_ge(o_turned, b - 1)
                for g in range(2):
                    r = slice(g * 32, (g + 1) * 32)
                    dve.tensor_scalar(o[r, b % 2, :], outp[r, g * HD:(g + 1) * HD], rinv[r, b % 2:b % 2 + 1], None, ALU.mult).then_inc(o_ready, 1)
                dve.wait_ge(o_turned, b + 1)
                src = outp[0:HD, 256:256 + R].rearrange("e (h two q) -> e h two q", two=2, q=NS)
                for odd in range(2):
                    dve.tensor_copy(keep.mixT[odd * HD:(odd + 1) * HD, 0:4, SEQ + b * NS:SEQ + (b + 1) * NS], src[:, :, odd, :]).then_inc(mixed, 1)


def sample_b_phase(nc, hT, vec, state, new_kv, io, keep):
    R = H_B * NS
    NT_K = 10
    L = NT_K * P + NS
    with phase(nc, "sb") as p:
        kv = p.sb("kv", [P, 2, NT_K, D])
        kT = p.sb("kT", [P, 4, L])
        k_new = p.sb("k_new", [P, 4, TS])
        v_new = p.sb("v_new", [NS, 2, 512])
        q = p.sb("q", [HD, H_B, TS])
        q_blk = p.sb("q_blk", [P, NB, 4, R])
        nat = p.sb("nat", [R, LS])
        table = p.sb("table", [R, L])
        shifted = p.sb("shifted", [R, L])
        probs = shifted
        pT = p.sb("pT", [P, NT_K + 1, R])
        nmax = p.sb("nmax", [R, 2])
        total = p.sb("total", [R, 2])
        rinv = p.sb("rinv", [R, 2])
        logit = p.ps("logit", [P, 3 * 512])
        tps = [p.ps(f"tps{i}", [P, 512]) for i in range(2)]
        tpp = [p.ps(f"tpp{i}", [P, 512]) for i in range(2)]
        outp = p.ps("outp", [P, 512])
        (loaded, t_in, zeroed, built, tabled, turned_k, kT_even, kT_odd, kT_new, logit_ready, shifted_ready, probs_ready, weighed,
         scaled, turned_p, pT_ready, out_ready, mixed) = (p.sem(n) for n in (
             "loaded", "t_in", "zeroed", "built", "tabled", "turned_k", "kT_even", "kT_odd", "kT_new", "logit_ready",
             "shifted_ready", "probs_ready", "weighed", "scaled", "turned_p", "pT_ready", "out_ready", "mixed"))
        kT_ready = [kT_even, kT_odd]
        kv_in = [p.sem(f"kv_in{i}") for i in range(2)]
        block = p.body.enter_context(nc.Block())

        @block.sync
        def _(sp):
            sp.dma_start(q[:, :, :], hT[B_Q:B_Q + H_B * HD, SEQ:T].rearrange("(h e) t -> e h t", e=HD)).then_inc(loaded, 16)
            sp.dma_start(k_new[:, :, :], hT[B_K:B_K + 4 * P, SEQ:T].rearrange("(m e) t -> e m t", e=P)).then_inc(loaded, 16)
            sample_table(sp, nat, vec, KIND_DIL, 8, H_B, 0, LS, t_in)
            for b in range(NB):
                if b >= 2:
                    sp.wait_ge(out_ready, b - 1)
                chunks = state[b].rearrange("(g r) c -> g r c", r=STRIDE)
                sp.dma_start(kv[:, b % 2, 0:8, :], chunks[:, 0:8, :]).then_inc(kv_in[b % 2], 16)
                late = bass.AP(tensor=state.tensor, offset=(b * PAST + 96 * STRIDE + 8) * D,
                               ap=[[STRIDE * D, 32], [2 * D, 4], [1, 2 * D]])
                sp.dma_start(kv[:, b % 2, 8:10, :], late).then_inc(kv_in[b % 2], 16)
                sp.dma_start(v_new[:, b % 2, :], new_kv[b, :, 512:1024]).then_inc(kv_in[b % 2], 16)

        @block.tensor
        def _(pe):
            pe.wait_ge(built, 8)

            def keys(b):
                pe.wait_ge(kv_in[b % 2], 48 * (b // 2 + 1))
                for t in range(NT_K):
                    n = NT_K * b + t
                    if n >= 2:
                        pe.wait_ge(kT_ready[n % 2], n // 2)
                    for m in range(4):
                        last = pe.transpose(tps[n % 2][:, m * P:(m + 1) * P], kv[:, b % 2, t, m * P:(m + 1) * P], keep.ident[:, :])
                    last.then_inc(turned_k, 1)

            def scores(b):
                for i in range(2):
                    pe.wait_ge(kT_ready[i], NT_K // 2 * (b + 1))
                pe.wait_ge(kT_new, b + 1)
                if b:
                    pe.wait_ge(shifted_ready, b)
                for c in range(0, L, 512):
                    w = min(512, L - c)
                    for m in range(4):
                        last = pe.matmul(logit[0:R, c:c + w], q_blk[:, b, m, :], kT[:, m, c:c + w], start=(m == 0), stop=(m == 3))
                last.then_inc(logit_ready, 1)

            def turn(b):
                pe.wait_ge(scaled, b + 1)
                if b:
                    pe.wait_ge(pT_ready, 3 * b)
                for t in range(NT_K + 1):
                    w = P if t < NT_K else NS
                    last = pe.transpose(tpp[t // 8][0:w, (t % 8) * R:(t % 8 + 1) * R], probs[:, t * P:t * P + w], keep.ident[0:R, 0:R])
                last.then_inc(turned_p, 1)

            def values(b):
                pe.wait_ge(pT_ready, 3 * b + 3)
                if b:
                    pe.wait_ge(mixed, 2 * b)
                for m in range(4):
                    v = slice(512 + m * P, 512 + (m + 1) * P)
                    for t in range(NT_K):
                        pe.matmul(outp[:, m * 16:(m + 1) * 16], kv[:, b % 2, t, v], pT[:, t, m * 16:(m + 1) * 16], start=(t == 0), stop=False)
                    last = pe.matmul(outp[:, m * 16:(m + 1) * 16], v_new[:, b % 2, m * P:(m + 1) * P], pT[0:NS, NT_K, m * 16:(m + 1) * 16], start=False, stop=True)
                last.then_inc(out_ready, 1)

            keys(0)
            for b in range(NB):
                scores(b)
                if b + 1 < NB:
                    keys(b + 1)
                turn(b)
                values(b)

        def copy_key_tile(eng, copy, b, t):
            n = NT_K * b + t
            eng.wait_ge(turned_k, n + 1)
            if b:
                eng.wait_ge(logit_ready, b)
            copy(kT[:, :, t * P:(t + 1) * P], tps[n % 2][:, :].rearrange("p (m c) -> p m c", m=4)).then_inc(kT_ready[n % 2], 1)

        @block.scalar
        def _(act):
            act.wait_ge(loaded, 32)

            def copy_keys(b):
                for t in range(0, NT_K, 2):
                    copy_key_tile(act, act.copy, b, t)
                act.copy(kT[:, :, NT_K * P:L], k_new[:, :, b * NS:(b + 1) * NS]).then_inc(kT_new, 1)

            copy_keys(0)
            for b in range(NB):
                if b + 1 < NB:
                    copy_keys(b + 1)
                act.wait_ge(shifted_ready, b + 1)
                if b:
                    act.wait_ge(turned_p, b)
                if b >= 2:
                    act.wait_ge(weighed, b - 1)
                act.activation(probs[:, :], shifted[:, :], ACT.Exp, bias=nmax[:, b % 2:b % 2 + 1], scale=-1.0,
                               accum_out=total[:, b % 2:b % 2 + 1]).then_inc(probs_ready, 1)

        @block.vector
        def _(dve):
            dve.memset(q_blk[:, :, :, :], 0.0).then_inc(zeroed, 1)
            dve.wait_ge(zeroed, 1)
            dve.wait_ge(loaded, 32)
            for h in range(H_B):
                dst = q_blk[(h % 2) * HD:(h % 2 + 1) * HD, :, h // 2, h * NS:(h + 1) * NS]
                dve.tensor_scalar(dst, q[:, h, :].rearrange("e (b q) -> e b q", q=NS), SCALE, None, ALU.mult).then_inc(built, 1)
            dve.wait_ge(t_in, 16 * NS)
            dve.tensor_copy(table[:, 0:8 * P].rearrange("r (t g) -> r t g", t=8),
                            nat[:, 0:PAST].rearrange("r (g t) -> r t g", t=STRIDE)[:, 0:8, :]).then_inc(tabled, 1)
            for t in range(2):
                dst = table[:, (8 + t) * P:(9 + t) * P].rearrange("r (g s) -> r g s", s=4)
                src = nat[:, 96 * STRIDE:PAST].rearrange("r (g h s t) -> r t h g s", h=2, s=4, t=2)[:, t, 1, :, :]
                dve.tensor_copy(dst, src).then_inc(tabled, 1)
            dve.tensor_copy(table[:, NT_K * P:L], nat[:, PAST:LS]).then_inc(tabled, 1)
            dve.wait_ge(tabled, 4)

            def copy_keys(b):
                for t in range(1, NT_K, 2):
                    copy_key_tile(dve, dve.tensor_copy, b, t)

            copy_keys(0)
            for b in range(NB):
                dve.wait_ge(logit_ready, b + 1)
                if b:
                    dve.wait_ge(probs_ready, b)
                dve.tensor_tensor_reduce(out=shifted[:, :], in0=logit[0:R, 0:L], in1=table[:, :], scale=-1.0, scalar=FLOOR,
                                         op0=ALU.add, op1=ALU.min, accum_out=nmax[:, b % 2:b % 2 + 1]).then_inc(shifted_ready, 1)
                if b + 1 < NB:
                    copy_keys(b + 1)
                dve.wait_ge(probs_ready, b + 1)
                dve.reciprocal(rinv[:, b % 2:b % 2 + 1], total[:, b % 2:b % 2 + 1]).then_inc(weighed, 1)
                dve.wait_ge(weighed, b + 1)
                dve.tensor_scalar(probs[:, :], probs[:, :], rinv[:, b % 2:b % 2 + 1], None, ALU.mult).then_inc(scaled, 1)
                dve.wait_ge(turned_p, b + 1)
                if b:
                    dve.wait_ge(out_ready, b)
                dve.tensor_copy(pT[:, 0:8, :], tpp[0][:, :].rearrange("p (t r) -> p t r", r=R)).then_inc(pT_ready, 1)
                dve.tensor_copy(pT[:, 8:10, :], tpp[1][:, 0:2 * R].rearrange("p (t r) -> p t r", r=R)).then_inc(pT_ready, 1)
                dve.tensor_copy(pT[0:NS, NT_K, :], tpp[1][0:NS, 2 * R:3 * R]).then_inc(pT_ready, 1)
                dve.wait_ge(out_ready, b + 1)
                src = outp[:, 0:64].rearrange("p (m two q) -> p m two q", m=4, two=2)
                for odd in range(2):
                    r = slice(odd * HD, (odd + 1) * HD)
                    dve.tensor_copy(keep.mixT[r, 4:8, SEQ + b * NS:SEQ + (b + 1) * NS], src[r, :, odd, :]).then_inc(mixed, 1)




class Norm:

    def __init__(self, p, keep):
        self.keep = keep
        self.stats = p.sb("stats", [P, 2, 2, 6])
        self.mv = p.sb("mv", [P, 2, 2])
        self.rstd = p.sb("rstd", [P, 2])
        self.g = p.sb("g", [P, D])
        self.b = p.sb("b", [P, D])
        self.params_in = p.sem("params_in")
        self.stat, self.aggr, self.root, self.inv, self.step, self.normed = (
            p.sem(n) for n in ("stat", "aggr", "root", "inv", "step", "normed"))
        self.turned, self.xT_even = p.sem("xT_turned"), p.sem("xT_out")

    def load(self, sp, g, b):
        for dst, src in ((self.g, g), (self.b, b)):
            sp.dma_start(dst[:, :], src[None, :].to_broadcast([P, D])).then_inc(self.params_in, 16)

    def vector(self, dve, t):
        k, w, s = self.keep, TILES[t][1], t % 2
        x = k.xtok[0:w, t, :]
        for h in range(2):
            dve.bn_stats(out=self.stats[0:w, s, h, :], in_=x[:, h * 512:(h + 1) * 512]).then_inc(self.stat, 1)
        dve.wait_ge(self.stat, 2 * t + 2)
        dve.bn_aggr(out=self.mv[0:w, s, :], in_=self.stats[0:w, s, :, :]).then_inc(self.aggr, 1)
        dve.wait_ge(self.root, t + 1)
        dve.reciprocal(self.rstd[0:w, s:s + 1], self.rstd[0:w, s:s + 1]).then_inc(self.inv, 1)
        dve.wait_ge(self.inv, t + 1)
        dve.tensor_scalar(x, x, self.mv[0:w, s, 0:1], self.rstd[0:w, s:s + 1], ALU.subtract, ALU.mult).then_inc(self.step, 1)
        dve.wait_ge(self.step, 2 * t + 1)
        dve.wait_ge(self.params_in, 32)
        dve.tensor_tensor(x, x, self.g[0:w, :], ALU.mult).then_inc(self.step, 1)
        dve.wait_ge(self.step, 2 * t + 2)
        dve.tensor_tensor(x, x, self.b[0:w, :], ALU.add).then_inc(self.normed, 1)

    def scalar(self, act, t):
        w, s = TILES[t][1], t % 2
        act.wait_ge(self.aggr, t + 1)
        if t >= 2:
            act.wait_ge(self.step, 2 * (t - 2) + 1)
        act.activation(self.rstd[0:w, s:s + 1], self.mv[0:w, s, 1:2], ACT.Sqrt, bias=self.keep.eps[0:w, :]).then_inc(self.root, 1)

    def turn(self, pe, banks):
        for t in range(NT):
            w = TILES[t][1]
            pe.wait_ge(self.normed, t + 1)
            for half in range(2):
                n = 2 * t + half
                if n >= 2:
                    pe.wait_ge(self.xT_even, n - 1)
                for i in range(4):
                    k = 4 * half + i
                    last = pe.transpose(banks[n % 2][:, i * P:i * P + w], self.keep.xtok[0:w, t, k * P:(k + 1) * P], self.keep.ident[0:w, 0:w])
                last.then_inc(self.turned, 1)

    def copy_turned(self, act, t, banks):
        lo, w = TILES[t]
        for half in range(2):
            n = 2 * t + half
            act.wait_ge(self.turned, n + 1)
            act.copy(self.keep.xT[:, 4 * half:4 * half + 4, lo:lo + w],
                     banks[n % 2][:, :].rearrange("p (k c) -> p k c", k=4)[:, :, 0:w]).then_inc(self.xT_even, 1)


def turn_mix_phase(nc, name, mix, keep):
    with phase(nc, name) as p:
        tps = [p.ps(f"tps{i}", [P, 512]) for i in range(4)]
        turned, mixT_ready = p.sem("turned"), p.sem("mixT_ready")
        block = p.body.enter_context(nc.Block())

        @block.tensor
        def _(pe):
            for k in range(KC):
                if k >= 4:
                    pe.wait_ge(mixT_ready, k - 3)
                for t in range(NQ):
                    last = pe.transpose(tps[k % 4][:, t * P:(t + 1) * P], mix[:, t, k * P:(k + 1) * P], keep.ident[:, :])
                last.then_inc(turned, 1)

        @block.scalar
        def _(act):
            for k in range(KC):
                act.wait_ge(turned, k + 1)
                act.copy(keep.mixT[:, k, 0:SEQ], tps[k % 4][:, :]).then_inc(mixT_ready, 1)


def output_phase(nc, name, w_out, g, b, keep):
    with phase(nc, name) as p:
        w = p.sb("w", [P, KC, D])
        w_in = [p.sem(f"w_in{k}") for k in range(KC)]
        product, summed = p.sem("product"), p.sem("summed")
        acc = [p.ps(f"acc{i}", [P, 512]) for i in range(4)]
        tps = [p.ps(f"tps{i}", [P, 512]) for i in range(2)]
        norm = Norm(p, keep)
        block = p.body.enter_context(nc.Block())

        @block.sync
        def _(sp):
            for k in range(KC):
                sp.dma_start(w[:, k, :], w_out[k * P:(k + 1) * P, :]).then_inc(w_in[k], 16)
            norm.load(sp, g, b)

        @block.tensor
        def _(pe):
            for t, (lo, m) in enumerate(TILES):
                for h in range(2):
                    n = 2 * t + h
                    if n >= 4:
                        pe.wait_ge(summed, n - 3)
                    for k in range(KC):
                        if n == 0:
                            pe.wait_ge(w_in[k], 16)
                        last = pe.matmul(acc[n % 4][0:m, :], keep.mixT[:, k, lo:lo + m], w[:, k, h * 512:(h + 1) * 512],
                                         start=(k == 0), stop=(k == KC - 1))
                    last.then_inc(product, 1)
            norm.turn(pe, tps)

        @block.scalar
        def _(act):
            for t in range(NT):
                norm.scalar(act, t)
                if t:
                    norm.copy_turned(act, t - 1, tps)
            norm.copy_turned(act, NT - 1, tps)

        @block.vector
        def _(dve):
            for t, (lo, m) in enumerate(TILES):
                for h in range(2):
                    n = 2 * t + h
                    dve.wait_ge(product, n + 1)
                    x = keep.xtok[0:m, t, h * 512:(h + 1) * 512]
                    dve.scalar_tensor_tensor(out=x, in0=x, scalar=ALPHA, in1=acc[n % 4][0:m, :], op0=ALU.mult, op1=ALU.add).then_inc(summed, 1)
                dve.wait_ge(summed, 2 * t + 2)
                norm.vector(dve, t)


def ffn_phase(nc, name, w_up, conv_w, conv_b, w_down, prev, g, b, p_tail, s_tail, y, keep):
    EXT = 2 + SEQ + NB * (2 + NS)
    CV = EXT - 2
    S0 = 2 + SEQ
    NR = 2 + 2 * NB
    LOOPS = NF // 2
    with phase(nc, name) as p:
        w = p.sb("w", [P, 2, KC, 256])
        ext = p.sb("ext", [P, 4, EXT])
        conv = p.sb("conv", [P, 4, CV])
        gelu = p.sb("gelu", [P, 2, CV])
        hid = p.sb("hid", [P, NF, T])
        wd = p.sb("wd", [P, 4, 2, 512])
        rows = p.sb("rows", [NR, 2 * D_FF])
        par_rows = p.sb("par_rows", [2 * NF, 4, P])
        par = p.sb("par", [P, 4, 2 * NF])
        par_slot = p.sb("par_slot", [P, 4, 4])
        prevT = p.sb("prevT", [P, 2 * NF, 2 * NB])
        tailT = p.sb("tailT", [P, 2 * NF, NR])
        acc = [p.ps(f"acc{i}", [P, 512]) for i in range(4)]
        acc_s = [p.ps(f"accs{i}", [P, 512]) for i in range(4)]
        w_in = [p.sem(f"w_in{i}") for i in range(2)]
        wd_in = [p.sem(f"wd_in{i}") for i in range(4)]
        (rows_in, par_turned, par_out, prefix_in, zeroed, up_done, main_out, small_out, tails_out, conv1, conv2, conv3, gelu_done,
         hid_done, wd_used, tail_turned, tail_out, product, summed, stored) = (p.sem(n) for n in (
             "rows_in", "par_turned", "par_out", "prefix_in", "zeroed", "up_done", "main_out", "small_out", "tails_out", "conv1",
             "conv2", "conv3", "gelu_done", "hid_done", "wd_used", "tail_turned", "tail_out", "product", "summed", "stored"))
        norm = Norm(p, keep)
        wv = w_up.rearrange("(k p) n -> p k n", p=P)
        last_of_half = NF // 2 - 1
        down_acc = acc + [acc_s[0]]
        block = p.body.enter_context(nc.Block())

        @block.sync
        def _(sp):
            sp.dma_start(rows[0:2 * NB, :], prev.rearrange("b r c -> (b r) c")).then_inc(rows_in, 16)
            sp.dma_start(par_rows[:, 0:3, :], conv_w.rearrange("j (n p) -> n j p", p=P)).then_inc(rows_in, 16)
            sp.dma_start(par_rows[:, 3, :], conv_b.rearrange("(n p) -> n p", p=P)).then_inc(rows_in, 16)
            with sp.Fori(0, LOOPS) as i:
                for s in range(2):
                    sp.wait_ge(up_done, i * 4 + (2 * s + 2))
                    for part in range(2):
                        src = wv[:, :, bass.ds(i * 2 * P + (s * P + part * D_FF), P)]
                        sp.dma_start(w[:, s, :, part * P:(part + 1) * P], src).then_inc(w_in[s], 16)
            norm.load(sp, g, b)
            for n in range(NF):
                h, f = divmod(n, NF // 2)
                if n == last_of_half + 4:
                    sp.wait_ge(product, NT)
                elif n >= 4:
                    sp.wait_ge(wd_used, n - 3 - (n > last_of_half + 4))
                src = w_down[2 * f * P:(2 * f + 2) * P, h * 512:(h + 1) * 512].rearrange("(f p) c -> p f c", p=P)
                sp.dma_start(wd[:, n % 4, :, :], src).then_inc(wd_in[n % 4], 16)
            sp.wait_ge(tail_out, NF // 2)
            sp.dma_start(p_tail, rows[0:2, :]).then_inc(stored, 16)
            sp.dma_start(s_tail, rows[2:NR, :]).then_inc(stored, 16)
            if y is not None:
                sp.wait_ge(norm.normed, NT)
                sp.dma_start(y[0].rearrange("b (i p) d -> p (b i) d", p=P), keep.xtok[:, 0:NQ, :]).then_inc(stored, 16)
                sp.dma_start(y[1].rearrange("b q d -> (b q) d"), keep.xtok[0:TS, NQ, :]).then_inc(stored, 16)
            sp.wait_ge(stored, 32 if y is None else 64)

        @block.gpsimd
        def _(pool):
            pool.memset(ext[:, :, 0:2], 0.0).then_inc(zeroed, 1)
            pool.wait_ge(zeroed, 1)
            pool.sem_inc(tails_out, 8)
            pool.wait_ge(par_out, 3)
            with pool.Fori(0, LOOPS) as i:
                for e in range(4):
                    n = i * 4 + e
                    blk = i * 2 + (e // 2 + (e % 2) * NF)
                    pool.wait_ge(conv3, n + 1)
                    pool.tensor_copy(ext[:, e, S0:EXT].rearrange("p (b c) -> p b c", b=NB)[:, :, 0:2],
                                     prevT[:, bass.ds(blk, 1), :].rearrange("p a (b r) -> p (a b) r", r=2)).then_inc(prefix_in, 1)
                    pool.tensor_copy(par_slot[:, e, :], par[:, :, bass.ds(blk, 1)].rearrange("p j a -> p (j a)")).then_inc(prefix_in, 1)
                for e in range(4):
                    n = i * 4 + e
                    blk = i * 2 + (e // 2 + (e % 2) * NF)
                    pool.wait_ge(main_out, n + 5)
                    pool.wait_ge(small_out, n + 5)
                    pool.tensor_copy(tailT[:, bass.ds(blk, 1), 0:2].rearrange("p a r -> p (a r)"), ext[:, e, SEQ:SEQ + 2]).then_inc(tails_out, 1)
                    pool.tensor_copy(tailT[:, bass.ds(blk, 1), 2:NR].rearrange("p a (b r) -> p (a b) r", r=2),
                                     ext[:, e, S0:EXT].rearrange("p (b c) -> p b c", b=NB)[:, :, NS:NS + 2]).then_inc(tails_out, 1)

        @block.tensor
        def _(pe):
            pe.wait_ge(rows_in, 48)
            for j in range(4):
                last = pe.transpose(acc_s[0][:, j * 2 * NF:(j + 1) * 2 * NF], par_rows[:, j, :], keep.ident[0:2 * NF, 0:2 * NF])
            last.then_inc(par_turned, 1)
            for h in range(2):
                for n in range(NF):
                    blk = h * NF + n
                    last = pe.transpose(acc_s[1 + h][:, n * 16:(n + 1) * 16], rows[0:16, blk * P:(blk + 1) * P], keep.ident[0:16, 0:16])
                last.then_inc(par_turned, 1)
            pe.wait_ge(par_out, 3)
            pe.sem_inc(up_done, 4)
            pe.sem_inc(main_out, 4)
            pe.sem_inc(small_out, 4)
            with pe.Fori(0, LOOPS) as i:
                for s in range(2):
                    pe.wait_ge(w_in[s], i * 32 + 32)
                    for part in range(2):
                        e = 2 * s + part
                        pe.wait_ge(main_out, i * 4 + (e + 1))
                        pe.wait_ge(small_out, i * 4 + (e + 1))
                        for k in range(KC):
                            pe.matmul(acc[e][:, :], w[:, s, k, part * P:(part + 1) * P], keep.xT[:, k, 0:SEQ], start=(k == 0), stop=(k == KC - 1))
                        for k in range(KC):
                            last = pe.matmul(acc_s[e][:, 0:TS], w[:, s, k, part * P:(part + 1) * P], keep.xT[:, k, SEQ:T], start=(k == 0), stop=(k == KC - 1))
                        last.then_inc(up_done, 1)
            pe.wait_ge(main_out, 4 + 2 * NF)
            pe.wait_ge(small_out, 4 + 2 * NF)
            pe.wait_ge(tails_out, 8 + 4 * NF)
            for n in range(NF // 2):
                if n >= 2:
                    pe.wait_ge(tail_out, n - 1)
                for i in range(4):
                    last = pe.transpose(acc_s[1 + n % 2][0:NR, i * P:(i + 1) * P], tailT[:, 4 * n + i, :], keep.ident[:, :])
                last.then_inc(tail_turned, 1)
            pe.wait_ge(hid_done, 4 + 2 * NF)
            for h in range(2):
                for f in range(NF):
                    n = h * (NF // 2) + f // 2
                    if f % 2 == 0:
                        pe.wait_ge(wd_in[n % 4], 16 * (n // 4 + 1))
                    for t, (lo, m) in enumerate(TILES):
                        if h and f == 0:
                            pe.wait_ge(summed, t + 1)
                        last = pe.matmul(down_acc[t][0:m, :], hid[:, f, lo:lo + m], wd[:, n % 4, f % 2, :], start=(f == 0), stop=(f == NF - 1))
                        if f == NF - 1:
                            last.then_inc(product, 1)
                    if f % 2 == 1 and f < NF - 1:
                        last.then_inc(wd_used, 1)
            pe.wait_ge(tail_out, NF // 2)
            norm.turn(pe, acc_s[1:3])

        @block.scalar
        def _(act):
            with act.Fori(0, LOOPS) as i:
                for s in range(2):
                    for e in (2 * s, 2 * s + 1):
                        act.wait_ge(up_done, i * 4 + (e + 5))
                        act.wait_ge(conv3, i * 4 + (e + 1))
                        act.wait_ge(tails_out, i * 8 + 2 * (e + 1))
                        act.copy(ext[:, e, 2:S0], acc[e][:, :]).then_inc(main_out, 1)
                    for e in (2 * s, 2 * s + 1):
                        act.wait_ge(main_out, i * 4 + (e + 5))
                        act.wait_ge(small_out, i * 4 + (e + 5))
                        act.wait_ge(prefix_in, i * 8 + 2 * (e + 1))
                        act.wait_ge(hid_done, i * 4 + 2 * (s + 1))
                        act.activation(conv[:, e, :], ext[:, e, 0:CV], ACT.Identity, scale=par_slot[:, e, 0:1], bias=par_slot[:, e, 3:4]).then_inc(conv1, 1)
                    act.wait_ge(conv3, i * 4 + (2 * s + 5))
                    act.activation(gelu[:, s, :], conv[:, 2 * s, :], ACT.Gelu_apprx_tanh).then_inc(gelu_done, 1)
            for n in range(NF // 2):
                act.wait_ge(tail_turned, n + 1)
                act.copy(rows[:, n * 512:(n + 1) * 512], acc_s[1 + n % 2][0:NR, :]).then_inc(tail_out, 1)
            for t in range(NT):
                norm.scalar(act, t)
                if t:
                    norm.copy_turned(act, t - 1, acc_s[1:3])
            norm.copy_turned(act, NT - 1, acc_s[1:3])

        @block.vector
        def _(dve):
            dve.wait_ge(par_turned, 1)
            dve.tensor_copy(par[:, :, :], acc_s[0][:, 0:8 * NF].rearrange("p (j n) -> p j n", j=4)).then_inc(par_out, 1)
            dve.sem_inc(conv3, 4)
            dve.sem_inc(hid_done, 4)
            for h in range(2):
                dve.wait_ge(par_turned, 2 + h)
                dve.tensor_copy(prevT[:, h * NF:(h + 1) * NF, :], acc_s[1 + h][:, 0:16 * NF].rearrange("p (n r) -> p n r", r=16)).then_inc(par_out, 1)
            with dve.Fori(0, LOOPS) as i:
                for s in range(2):
                    for e in (2 * s, 2 * s + 1):
                        dve.wait_ge(up_done, i * 4 + (e + 5))
                        dve.wait_ge(tails_out, i * 8 + 2 * (e + 1))
                        dve.tensor_copy(ext[:, e, S0:EXT].rearrange("p (b c) -> p b c", b=NB)[:, :, 2:2 + NS],
                                        acc_s[e][:, 0:TS].rearrange("p (b q) -> p b q", q=NS)).then_inc(small_out, 1)
                    for e in (2 * s, 2 * s + 1):
                        dve.wait_ge(conv1, i * 4 + (e + 1))
                        dve.scalar_tensor_tensor(out=conv[:, e, :], in0=ext[:, e, 1:1 + CV], scalar=par_slot[:, e, 1:2], in1=conv[:, e, :],
                                                 op0=ALU.mult, op1=ALU.add).then_inc(conv2, 1)
                        dve.wait_ge(conv2, i * 4 + (e + 1))
                        dve.scalar_tensor_tensor(out=conv[:, e, :], in0=ext[:, e, 2:2 + CV], scalar=par_slot[:, e, 2:3], in1=conv[:, e, :],
                                                 op0=ALU.mult, op1=ALU.add).then_inc(conv3, 1)
                    dve.wait_ge(conv3, i * 4 + (2 * s + 6))
                    dve.wait_ge(gelu_done, i * 2 + (s + 1))
                    f = i * 2 + s
                    dve.tensor_tensor(hid[:, bass.ds(f, 1), 0:SEQ].rearrange("p a t -> p (a t)"), gelu[:, s, 0:SEQ], conv[:, 2 * s + 1, 0:SEQ], ALU.mult).then_inc(hid_done, 1)
                    dve.tensor_tensor(hid[:, bass.ds(f, 1), SEQ:T].rearrange("p a (b q) -> p (a b) q", q=NS),
                                      sample_columns(gelu[:, s, :], S0), sample_columns(conv[:, 2 * s + 1, :], S0), ALU.mult).then_inc(hid_done, 1)
            for h in range(2):
                for t, (lo, m) in enumerate(TILES):
                    dve.wait_ge(product, h * NT + t + 1)
                    x = keep.xtok[0:m, t, h * 512:(h + 1) * 512]
                    dve.scalar_tensor_tensor(out=x, in0=x, scalar=ALPHA, in1=down_acc[t][0:m, :], op0=ALU.mult, op1=ALU.add).then_inc(summed, 1)
            dve.wait_ge(summed, 2 * NT)
            for t in range(NT):
                norm.vector(dve, t)


def sample_columns(row, start):
    a = row.ap
    return bass.AP(tensor=row.tensor, offset=row.offset + start, ap=[list(a[0]), [NS + 2, NB], [1, NS]])


def prompt_compressed_phase(nc, hT, tok, mix, io, keep):
    NC = SEQ // STRIDE - 1
    with phase(nc, "pcmp") as p:
        w1e = p.sb("w1e", [HD, 2, 32, HD])
        peT = p.sb("peT", [HD, 2, 32])
        b1 = p.sb("b1", [HD, 2])
        w2 = p.sb("w2", [HD, 2, HD])
        x = p.sb("x", [HD, 2, 2, SEQ])
        q = p.sb("q", [HD, N_HEADS, SEQ])
        hid = p.sb("hid", [HD, 2, 2, 32])
        kcT = p.sb("kcT", [HD, 2, 32])
        v_blk = p.sb("v_blk", [P, 2, 4, HD])
        mask = p.sb("mask", [P, NQ, 32])
        lg = p.sb("lg", [P, 2, N_HEADS, 32])
        pr = p.sb("pr", [P, 2, N_HEADS, 32])
        stat = p.sb("stat", [P, 2, 2, N_HEADS])
        pT = p.sb("pT", [P, 2, 512])
        psc = p.ps("psc", [P, 512])
        psh = p.ps("psh", [P, 512])
        psk = p.ps("psk", [P, 512])
        lgp = [p.ps(f"lgp{i}", [P, 512]) for i in range(2)]
        tps = p.ps("tps", [P, 512])
        outp = p.ps("outp", [P, 2 * 512])
        names = ("loaded", "gated", "const_sum", "const", "hidden", "activated", "keyed", "values", "cleared", "placed",
                 "scored", "soft", "exped", "weighed", "turned", "copied", "attended", "mixed")
        (loaded, gated, const_sum, const, hidden, activated, keyed, values, cleared, placed,
         scored, soft, exped, weighed, turned, copied, attended, mixed) = (p.sem(n) for n in names)
        block = p.body.enter_context(nc.Block())
        LOADS = 9

        @block.sync
        def _(sp):
            sp.dma_start(w1e[:, :, :, :], io["phi_w1"].rearrange("a j e f -> e a j f")).then_inc(loaded, 16)
            with nc.allow_non_contiguous_dma(reason="small transposed parameters"):
                for a in range(2):
                    sp.dma_start(peT[:, a, :], io["phi_pe"][a].rearrange("j e -> e j")).then_inc(loaded, 16)
                sp.dma_start(b1[:, :], io["phi_b1"].rearrange("a f -> f a")).then_inc(loaded, 16)
            sp.dma_start(w2[:, :, :], io["phi_w2"].rearrange("a f e -> f a e")).then_inc(loaded, 16)
            for a in range(2):
                sp.dma_start(x[:, a, :, :], hT[C_KV + a * P:C_KV + (a + 1) * P, 0:SEQ].rearrange("(g e) t -> e g t", e=HD)).then_inc(loaded, 16)
            sp.dma_start(q[:, :, :], hT[C_Q:C_Q + N_HEADS * HD, 0:SEQ].rearrange("(h e) t -> e h t", e=HD)).then_inc(loaded, 16)
            sp.dma_start(mask[:, :, :], io["c_cmp_mask"]).then_inc(loaded, 16)

        @block.tensor
        def _(pe):
            pe.wait_ge(loaded, 16 * LOADS)
            for a in range(2):
                for j in range(32):
                    last = pe.matmul(psc[0:HD, a:a + 1], w1e[:, a, j, :], peT[:, a, j:j + 1], start=(j == 0), stop=(j == 31))
                last.then_inc(const_sum, 1)
            for a in range(2):
                for j in range(32):
                    src = x[:, a, :, j:j + STRIDE * (NC - 1) + 1:STRIDE]
                    last = pe.matmul(psh[0:HD, a * 64:a * 64 + 2 * NC].rearrange("p (g c) -> p g c", g=2), w1e[:, a, j, :], src,
                                     start=(j == 0), stop=(j == 31))
                last.then_inc(hidden, 1)
            pe.wait_ge(activated, 2)
            pe.matmul(psk[0:HD, 0:2 * NC].rearrange("p (g c) -> p g c", g=2), w2[:, 0, :], hid[:, 0, :, 0:NC], start=True, stop=True).then_inc(keyed, 1)
            for g in range(2):
                pe.matmul(psk[0:NC, 128 + g * HD:128 + (g + 1) * HD], hid[:, 1, g, 0:NC], w2[:, 1, :], start=True, stop=True).then_inc(values, 1)
            pe.wait_ge(placed, 9)
            for i in range(NQ):
                if i >= 2:
                    pe.wait_ge(soft, 3 * (i - 2) + 1)
                for h in range(N_HEADS):
                    last = pe.matmul(lgp[i % 2][:, h * 32:(h + 1) * 32], q[:, h, i * P:(i + 1) * P], kcT[:, h // 8, :], start=True, stop=True)
                last.then_inc(scored, 1)
                pe.wait_ge(weighed, i + 1)
                if i:
                    pe.wait_ge(copied, i)
                for u in range(4):
                    last = pe.transpose(tps[:, u * P:(u + 1) * P], pr[:, i % 2, 4 * u:4 * u + 4, :].rearrange("p h c -> p (h c)"), keep.ident[:, :])
                last.then_inc(turned, 1)
                pe.wait_ge(copied, i + 1)
                if i:
                    pe.wait_ge(mixed, i)
                for u in range(4):
                    last = pe.matmul(outp[:, u * 256:(u + 1) * 256], pT[:, i % 2, u * P:(u + 1) * P],
                                     v_blk[:, u // 2, :, :].rearrange("p h e -> p (h e)"), start=True, stop=True)
                last.then_inc(attended, 1)

        @block.scalar
        def _(act):
            act.activation(keep.gate_tok[:, :, :], tok[:, 0:NQ, TC_G:TC], ACT.Exp, scale=-1.0).then_inc(gated, 1)
            act.wait_ge(const, 2)
            act.wait_ge(hidden, 2)
            for a in range(2):
                act.activation(hid[:, a, :, 0:NC], psh[0:HD, a * 64:a * 64 + 2 * NC].rearrange("p (g c) -> p g c", g=2),
                               ACT.Gelu_apprx_tanh, bias=keep.cmp_const[:, a:a + 1]).then_inc(activated, 1)
            for i in range(NQ):
                act.wait_ge(soft, 3 * i + 3)
                act.activation(pr[:, i % 2, :, :], lg[:, i % 2, :, :], ACT.Exp).then_inc(exped, 1)
                act.wait_ge(turned, i + 1)
                if i >= 2:
                    act.wait_ge(attended, i - 1)
                act.copy(pT[:, i % 2, :], tps[:, :]).then_inc(copied, 1)

        @block.vector
        def _(dve):
            dve.wait_ge(gated, 1)
            dve.tensor_scalar(keep.gate_tok[:, :, :], keep.gate_tok[:, :, :], 1.0, None, ALU.add).then_inc(gated, 1)
            dve.wait_ge(gated, 2)
            dve.reciprocal(keep.gate_tok[:, :, :], keep.gate_tok[:, :, :]).then_inc(gated, 1)
            dve.wait_ge(loaded, 16 * LOADS)
            dve.wait_ge(const_sum, 2)
            for a in range(2):
                dve.tensor_tensor(keep.cmp_const[:, a:a + 1], psc[0:HD, a:a + 1], b1[:, a:a + 1], ALU.add).then_inc(const, 1)
            dve.memset(kcT[:, :, :], 0.0).then_inc(cleared, 1)
            dve.memset(v_blk[:, :, :, :], 0.0).then_inc(cleared, 1)
            dve.wait_ge(cleared, 2)
            dve.wait_ge(keyed, 1)
            dve.wait_ge(values, 2)
            dve.tensor_copy(kcT[:, :, 0:NC], psk[0:HD, 0:2 * NC].rearrange("p (g c) -> p g c", g=2)).then_inc(placed, 1)
            for g in range(2):
                for u in range(4):
                    dve.tensor_copy(v_blk[32 * u:32 * u + NC, g, u, :], psk[0:NC, 128 + g * HD:128 + (g + 1) * HD]).then_inc(placed, 1)
            dve.wait_ge(gated, 3)
            for i in range(NQ):
                s = i % 2
                l, pv, mx, sm = lg[:, s, :, :], pr[:, s, :, :], stat[:, s, 0, :], stat[:, s, 1, :]
                dve.wait_ge(scored, i + 1)
                if i >= 2:
                    dve.wait_ge(exped, i - 1)
                dve.scalar_tensor_tensor(out=l, in0=lgp[s][:, :].rearrange("p (h c) -> p h c", h=N_HEADS), scalar=SCALE,
                                         in1=mask[:, i, None, :].to_broadcast([P, N_HEADS, 32]), op0=ALU.mult, op1=ALU.add).then_inc(soft, 1)
                dve.wait_ge(soft, 3 * i + 1)
                dve.tensor_reduce(mx, l, AX_X, ALU.max).then_inc(soft, 1)
                dve.wait_ge(soft, 3 * i + 2)
                dve.tensor_scalar(mx, mx, -FLOOR, None, ALU.max).then_inc(gated, 1)
                dve.wait_ge(gated, 4 + 3 * i)
                dve.tensor_tensor(l, l, mx[:, :, None].to_broadcast([P, N_HEADS, 32]), ALU.subtract).then_inc(soft, 1)
                dve.wait_ge(exped, i + 1)
                dve.tensor_reduce(sm, pv, AX_X, ALU.add).then_inc(gated, 1)
                dve.wait_ge(gated, 5 + 3 * i)
                dve.tensor_scalar(sm, sm, 1e-30, None, ALU.max).then_inc(gated, 1)
                dve.wait_ge(gated, 6 + 3 * i)
                dve.reciprocal(sm, sm).then_inc(cleared, 1)
                dve.wait_ge(cleared, 3 + 2 * i)
                dve.tensor_tensor(sm, keep.gate_tok[:, i, 0:N_HEADS], sm, ALU.mult).then_inc(cleared, 1)
                dve.wait_ge(cleared, 4 + 2 * i)
                dve.tensor_tensor(pv, pv, sm[:, :, None].to_broadcast([P, N_HEADS, 32]), ALU.mult).then_inc(weighed, 1)
                dve.wait_ge(attended, i + 1)
                dve.tensor_copy(mix[:, i, :], outp[:, :]).then_inc(mixed, 1)


def sample_c_phase(nc, hT, vec, cache_kv, state, new_kv, new_win, io, keep):
    rows_in_cache = cache_kv.rearrange("n (c j) s g e -> (n c) (j s g e)", j=STRIDE)
    R = N_HEADS * NS
    NC = NCH - 1
    LW = C_WIN + NS
    with phase(nc, "sc") as p:
        kv = p.sb("kv", [P, 2, STRIDE * 512])
        win = p.sb("win", [P, 2, 4, 256])
        w1 = p.sb("w1", [P, 2, 8, P])
        w2 = p.sb("w2", [HD, 2, HD])
        xT = keep.xT[:, :, :].rearrange("p k t -> p (k t)")[:, 0:4096].rearrange("p (a g m c) -> p a g m c", a=2, g=2, m=8)
        swap = p.sb("swap", [P, 2, 8, HD])
        hid = p.sb("hid", [HD, 2, 2, NC])
        h_next = h_sum = hid
        kcT = p.sb("kcT", [P, NC])
        vc = p.sb("vc", [NC, P])
        zeros = p.sb("zeros", [P, P])
        sc_cmp = p.sb("sc_cmp", [P, NC])
        pc = p.sb("pc", [P, NC])
        pcT = p.sb("pcT", [NC, P])
        imp = p.sb("imp", [16, P + 2])
        pair = p.sb("pair", [16, P])
        blocks = p.sb("blocks", [16, N_SEL])
        best = p.sb("best", [16, 2, 8])
        choice = p.sb("choice", [16, 2, N_SEL], BF16)
        spread = p.sb("spread", [16, R], BF16)
        q = p.sb("q", [HD, N_HEADS, TS])
        q_blk = p.sb("q_blk", [P, NB, R])
        k_new = p.sb("k_new", [P, 2, TS])
        v_new = p.sb("v_new", [NS, 2, 2, P])
        kT = p.sb("kT", [P, LS])
        kwT = p.sb("kwT", [P, LW])
        nat = kv[:, 1, 0:LS]
        nat_w = kv[:, 1, LS:LS + LW]
        table = p.sb("table", [R, LS])
        table_w = p.sb("table_w", [R, LW])
        gate = p.sb("gate", [R, 3, NB])
        shifted = p.sb("shifted", [R, LS])
        shifted_w = p.sb("shifted_w", [R, LW])
        pT = p.sb("pT", [P, STRIDE + 1, R])
        pwT = p.sb("pwT", [P, 5, R])
        nmax = p.sb("nmax", [R, 12])
        total = p.sb("total", [R, 4])
        wgt = p.sb("wgt", [R, 4])
        o = p.sb("o", [R, 3, HD])
        logit = [p.ps(f"logit{i}", [P, 512]) for i in range(3)]
        tps = [p.ps(f"tps{i}", [P, 512]) for i in range(2)]
        hps = p.ps("hps", [P, 512])
        cps = p.ps("cps", [P, 512])
        outp = p.ps("outp", [P, 512])
        names = ("loaded", "t_in", "zeroed", "built", "gated", "tabled", "h_done", "h_moved", "h_summed", "activated", "kc_done",
                 "kc_out", "cmp_scored", "cmp_shifted", "cmp_exped", "cmp_total", "cmp_normed", "imp_done", "imp_out", "paired",
                 "block_sums", "bonus", "picked", "marked", "chosen", "cmp_out", "kT_new", "kwT_new", "slc_max", "slc_exped",
                 "win_exped", "slc_out", "win_out", "weighed", "o_part", "o_ready", "o_turned", "mixed", "pcT_ready", "pT_ready",
                 "pwT_ready", "kT_ready", "kwT_ready", "xT_ready", "swapped", "inverted")
        m = {n: p.sem(n) for n in names}
        kv_in = keep.c_kv_in
        win_in = [p.sem(f"win_in{i}") for i in range(2)]
        tps_turned = [p.sem(f"tps_turned{i}") for i in range(2)]
        tps_out = [p.sem(f"tps_out{i}") for i in range(2)]
        scored = [p.sem(f"scored{i}") for i in range(3)]
        shifted_out = [p.sem(f"shifted_out{i}") for i in range(3)]

        turns, scores_order = [], []
        for b in range(-1, NB):
            if b + 1 < NB:
                turns += [("x", b + 1, i) for i in range(8)]
            if b >= 0:
                turns += [("k", b, i) for i in range(4)] + [("kw", b, 0)]
                scores_order += [("s", b, i) for i in range(5)] + [("w", b, i) for i in range(2)]
                turns += [("p", b, i) for i in range(5)] + [("pw", b, i) for i in range(2)]
            if b + 1 < NB:
                turns += [("pc", b + 1, 0)]
        turn_no = {g: n for n, g in enumerate(turns)}
        score_no = {g: n for n, g in enumerate(scores_order)}
        block = p.body.enter_context(nc.Block())
        LOADS = 8 + 3 * N_HEADS + 2 * NS

        @block.gpsimd
        def _(pool):
            for b in range(NB):
                if b == 1:
                    pool.wait_ge(m["tabled"], 4)
                if b >= 2:
                    pool.wait_ge(m["slc_out"], b - 1)
                pool.indirect_dma_start(out=kv[:, b % 2, :], out_offset=None, in_=rows_in_cache,
                                        in_offset=bass.IndirectOffsetOnAxis(ap=keep.chunk_row[:, b:b + 1], axis=0)).then_inc(kv_in[b % 2], 16)
                v = kv[:, b % 2, :].rearrange("c (m j r) -> c m j r", j=2, r=512)[:, :, :, 0:256].rearrange("c m j (a g e) -> c m j a g e", a=2, g=2)
                pool.wait_ge(kv_in[b % 2], 16 * (b // 2 + 1))
                if b:
                    pool.wait_ge(m["swapped"], 6 * b)
                for a in range(2):
                    pool.tensor_copy(swap[:, a, :, :], v[:, :, 0, a, 1, :]).then_inc(m["swapped"], 1)
                pool.wait_ge(m["swapped"], 6 * b + 2)
                for a in range(2):
                    pool.tensor_copy(v[:, :, 0, a, 1, :], v[:, :, 1, a, 0, :]).then_inc(m["swapped"], 1)
                pool.wait_ge(m["swapped"], 6 * b + 4)
                for a in range(2):
                    pool.tensor_copy(v[:, :, 1, a, 0, :], swap[:, a, :, :]).then_inc(m["swapped"], 1)

        @block.sync
        def _(sp):
            ld = m["loaded"]
            for a in range(2):
                for ab in range(2):
                    src = io["phi_w1"][a, 16 * ab:16 * (ab + 1)].rearrange("(m j) e f -> m (j e) f", j=2).rearrange("m p f -> p m f")
                    sp.dma_start(w1[:, a, :, ab * HD:(ab + 1) * HD], src).then_inc(ld, 16)
            sp.dma_start(w2[:, :, :], io["phi_w2"].rearrange("a f e -> f a e")).then_inc(ld, 16)
            sp.dma_start(q[:, :, :], hT[C_Q:C_Q + N_HEADS * HD, SEQ:T].rearrange("(h e) t -> e h t", e=HD)).then_inc(ld, 16)
            for a, s in enumerate((2, 4)):
                sp.dma_start(k_new[:, a, :], hT[C_KV + s * P:C_KV + (s + 1) * P, SEQ:T]).then_inc(ld, 16)
            with nc.allow_non_contiguous_dma(reason="gates, one per partition"):
                for br in range(3):
                    for h in range(N_HEADS):
                        sp.dma_start(gate[h * NS:(h + 1) * NS, br, :], hT[C_G + br * N_HEADS + h, SEQ:T].rearrange("(b q) -> q b", q=NS)).then_inc(ld, 16)
            sample_table(sp, nat, vec, KIND_FULL, 0, N_HEADS, 0, LS, ld)
            sample_table(sp, nat_w, vec, KIND_WIN, 0, N_HEADS, PAST - C_WIN, LW, ld)
            for b in range(NB):
                if b >= 2:
                    sp.wait_ge(m["win_out"], b - 1)
                sp.dma_start(v_new[:, 0, b % 2, :], new_kv[b, :, 3 * P:4 * P]).then_inc(win_in[b % 2], 16)
                sp.dma_start(v_new[:, 1, b % 2, :], new_win[b, :, P:2 * P]).then_inc(win_in[b % 2], 16)
                sp.dma_start(win[:, b % 2, :, :], state[b].rearrange("(c j) n -> c j n", j=4)).then_inc(win_in[b % 2], 16)

        @block.tensor
        def _(pe):
            pe.wait_ge(m["built"], 4)

            def turned(group, sources, width, dtype_rows=P):
                n = turn_no[group]
                if n >= 2:
                    pe.wait_ge(tps_out[n % 2], n // 2)
                for i, (src, rows) in enumerate(sources):
                    last = pe.transpose(tps[n % 2][0:rows, i * width:(i + 1) * width], src, keep.ident[:, :])
                last.then_inc(tps_turned[n % 2], 1)

            def cmp_keys(b):
                pe.wait_ge(m["swapped"], 6 * b + 6)
                for i in range(8):
                    a, g, f = i // 4, i // 2 % 2, i % 2
                    first = [(2 * (4 * f + u) + g) * 512 + a * P for u in range(4)]
                    turned(("x", b, i), [(kv[:, b % 2, c:c + P], P) for c in first], P)

            def cmp_hidden(b):
                pe.wait_ge(m["xT_ready"], 8 * (b + 1))
                if b:
                    pe.wait_ge(m["h_summed"], 2 * b)
                for a in range(2):
                    for u in range(8):
                        last = pe.matmul(hps[:, a * 256:(a + 1) * 256].rearrange("p (g c) -> p g c", g=2), w1[:, a, u, :],
                                         xT[:, a, :, u, :], start=(u == 0), stop=(u == 7))
                    last.then_inc(m["h_done"], 1)

            def cmp_final(b):
                pe.wait_ge(m["activated"], 2 * b + 2)
                if b:
                    pe.wait_ge(m["imp_out"], b)
                for g in range(2):
                    pe.matmul(cps[g * HD:(g + 1) * HD, 0:NC], w2[:, 0, :], hid[:, 0, g, :], start=True, stop=True)
                for g in range(2):
                    last = pe.matmul(cps[0:NC, 128 + g * HD:128 + (g + 1) * HD], hid[:, 1, g, :], w2[:, 1, :], start=True, stop=True)
                last.then_inc(m["kc_done"], 1)
                pe.wait_ge(m["kc_out"], 2 * b + 2)
                pe.matmul(cps[:, 256:256 + NC], q_blk[:, b, :], kcT[:, :], start=True, stop=True).then_inc(m["cmp_scored"], 1)

            def cmp_choice(b):
                pe.wait_ge(m["cmp_normed"], b + 1)
                pe.matmul(cps[0:16, 384:384 + NC], keep.group_sum[:, :], pc[:, :], start=True, stop=True).then_inc(m["imp_done"], 1)
                turned(("pc", b, 0), [(pc[:, :], NC)], P)
                pe.wait_ge(m["pcT_ready"], b + 1)
                if b:
                    pe.wait_ge(m["mixed"], 2 * b)
                pe.matmul(outp[:, 0:P], pcT[:, :], vc[:, :], start=True, stop=True).then_inc(m["cmp_out"], 1)

            def keys(b):
                for i in range(4):
                    turned(("k", b, i), [(kv[:, b % 2, (4 * i + u) * 512 + 256:(4 * i + u) * 512 + 384], P) for u in range(4)], P)
                pe.wait_ge(win_in[b % 2], 48 * (b // 2 + 1))
                turned(("kw", b, 0), [(win[:, b % 2, u, 0:P], P) for u in range(4)], P)

            def score_group(group, bank_cols, key_cols, pick):
                n = score_no[group]
                if n >= 3:
                    pe.wait_ge(shifted_out[n % 3], n // 3)
                mm = pe.matmul(logit[n % 3][:, 0:bank_cols], q_blk[:, group[1], :], key_cols, start=True, stop=pick is None)
                if pick is not None:
                    out = logit[n % 3][:, 0:bank_cols]
                    if bank_cols == 512:
                        out = out.rearrange("r (j k c) -> r j k c", j=4, c=4)
                    mm = pe.matmul(out, spread[:, :], pick, start=False, stop=True)
                mm.then_inc(scored[n % 3], 1)

            def scores(b):
                pe.wait_ge(m["chosen"], b + 1)
                for i in range(5):
                    if i == 4:
                        pe.wait_ge(m["kT_new"], b + 1)
                        pick = choice[:, b % 2, 32:33].to_broadcast([16, NS])
                        score_group(("s", b, 4), NS, kT[:, PAST:LS], pick)
                    else:
                        pe.wait_ge(m["kT_ready"], 4 * b + i + 1)
                        pick = choice[:, b % 2, None, 0:32, None].to_broadcast([16, 4, 32, 4])
                        score_group(("s", b, i), 512, kT[:, i * 512:(i + 1) * 512], pick)
                pe.wait_ge(m["kwT_ready"], b + 1)
                pe.wait_ge(m["kwT_new"], b + 1)
                score_group(("w", b, 0), 512, kwT[:, 0:512], None)
                score_group(("w", b, 1), NS, kwT[:, 512:LW], None)

            def turn_probs(b):
                pe.wait_ge(m["slc_exped"], b + 1)
                for i in range(4):
                    turned(("p", b, i), [(shifted[:, (4 * i + u) * P:(4 * i + u + 1) * P], P) for u in range(4)], P)
                turned(("p", b, 4), [(shifted[:, PAST:LS], NS)], P)
                pe.wait_ge(m["win_exped"], b + 1)
                turned(("pw", b, 0), [(shifted_w[:, u * P:(u + 1) * P], P) for u in range(4)], P)
                turned(("pw", b, 1), [(shifted_w[:, C_WIN:LW], NS)], P)

            def values(b):
                pe.wait_ge(m["pT_ready"], 5 * b + 5)
                if b:
                    pe.wait_ge(m["mixed"], 2 * b)
                for j in range(STRIDE):
                    pe.matmul(outp[:, 128:256], pT[:, j, :], kv[:, b % 2, j * 512 + 384:(j + 1) * 512], start=(j == 0), stop=False)
                pe.matmul(outp[:, 128:256], pT[0:NS, STRIDE, :], v_new[:, 0, b % 2, :], start=False, stop=True).then_inc(m["slc_out"], 1)
                pe.wait_ge(m["pwT_ready"], 2 * b + 2)
                for j in range(4):
                    pe.matmul(outp[:, 256:384], pwT[:, j, :], win[:, b % 2, j, P:2 * P], start=(j == 0), stop=False)
                pe.matmul(outp[:, 256:384], pwT[0:NS, 4, :], v_new[:, 1, b % 2, :], start=False, stop=True).then_inc(m["win_out"], 1)
                pe.wait_ge(m["o_ready"], b + 1)
                pe.transpose(outp[0:HD, 384:512], o[:, 2, :], keep.ident[:, :]).then_inc(m["o_turned"], 1)

            for b in range(-1, NB):
                if b + 1 < NB:
                    cmp_keys(b + 1)
                    cmp_hidden(b + 1)
                if b >= 0:
                    keys(b)
                    scores(b)
                if b + 1 < NB:
                    cmp_final(b + 1)
                if b >= 0:
                    turn_probs(b)
                    values(b)
                if b + 1 < NB:
                    cmp_choice(b + 1)

        @block.scalar
        def _(act):
            def turned(group, dst, src_of, done):
                n = turn_no[group]
                act.wait_ge(tps_turned[n % 2], n // 2 + 1)
                act.copy(dst, src_of(tps[n % 2])).then_inc(tps_out[n % 2], 1)
                act.wait_ge(tps_out[n % 2], n // 2 + 1)
                act.sem_inc(done, 1)

            act.wait_ge(m["loaded"], 16 * LOADS)
            act.activation(gate[:, :, :], gate[:, :, :], ACT.Exp, scale=-1.0).then_inc(m["gated"], 1)
            for b in range(-1, NB):
                if b + 1 < NB:
                    if b >= 0:
                        act.wait_ge(m["h_done"], 2 * (b + 1))
                    for i in range(8):
                        a, g, f = i // 4, i // 2 % 2, i % 2
                        turned(("x", b + 1, i), xT[:, a, g, 4 * f:4 * f + 4, :], lambda t: t[:, :].rearrange("p (m c) -> p m c", m=4), m["xT_ready"])
                if b >= 0:
                    if b:
                        act.wait_ge(m["slc_max"], b)
                    for i in range(4):
                        turned(("k", b, i), kT[:, i * 512:(i + 1) * 512], lambda t: t[:, :], m["kT_ready"])
                    act.copy(kT[:, PAST:LS], k_new[:, 0, b * NS:(b + 1) * NS]).then_inc(m["kT_new"], 1)
                    turned(("kw", b, 0), kwT[:, 0:C_WIN], lambda t: t[:, :], m["kwT_ready"])
                    act.copy(kwT[:, C_WIN:LW], k_new[:, 1, b * NS:(b + 1) * NS]).then_inc(m["kwT_new"], 1)
                if b + 1 < NB:
                    for a in range(2):
                        act.wait_ge(m["h_summed"], 2 * (b + 1) + a + 1)
                        act.activation(hid[:, a, :, :], h_sum[:, a, :, :], ACT.Gelu_apprx_tanh, bias=keep.cmp_const[:, a:a + 1]).then_inc(m["activated"], 1)
                if b >= 0:
                    act.wait_ge(m["weighed"], 2 * b + 1)
                    act.wait_ge(m["slc_max"], b + 1)
                    act.activation(shifted[:, :], shifted[:, :], ACT.Exp, bias=nmax[:, 8:9], scale=-1.0, accum_out=total[:, 0:1]).then_inc(m["slc_exped"], 1)
                    act.activation(shifted_w[:, :], shifted_w[:, :], ACT.Exp, bias=nmax[:, 9:10], scale=-1.0, accum_out=total[:, 1:2]).then_inc(m["win_exped"], 1)
                if b + 1 < NB:
                    act.wait_ge(m["cmp_shifted"], b + 2)
                    act.activation(pc[:, :], sc_cmp[:, :], ACT.Exp, bias=nmax[:, 10:11], scale=-1.0, accum_out=total[:, 2:3]).then_inc(m["cmp_exped"], 1)

        @block.vector
        def _(dve):
            dve.memset(q_blk[:, :, :], 0.0).then_inc(m["zeroed"], 1)
            dve.memset(zeros[:, :], 0.0).then_inc(m["zeroed"], 1)
            dve.memset(imp[:, :], 0.0).then_inc(m["zeroed"], 1)
            dve.memset(blocks[:, :], 0.0).then_inc(m["zeroed"], 1)
            dve.wait_ge(m["zeroed"], 4)
            dve.wait_ge(m["loaded"], 16 * LOADS)
            query_blocks(dve, q_blk, q, 2, N_HEADS // 2, m["built"])
            dve.tensor_copy(spread[:, :], keep.group_spread[:, :]).then_inc(m["built"], 1)
            dve.wait_ge(m["gated"], 1)
            dve.tensor_scalar(gate[:, :, :], gate[:, :, :], 1.0, None, ALU.add).then_inc(m["gated"], 1)
            dve.wait_ge(m["gated"], 2)
            dve.reciprocal(gate[:, :, :], gate[:, :, :]).then_inc(m["built"], 1)
            dve.tensor_copy(table[:, 0:PAST].rearrange("r (j c) -> r c j", j=STRIDE),
                            nat[:, 0:PAST].rearrange("r (c j) -> r c j", j=STRIDE)).then_inc(m["tabled"], 1)
            dve.tensor_copy(table[:, PAST:LS], nat[:, PAST:LS]).then_inc(m["tabled"], 1)
            dve.tensor_copy(table_w[:, 0:C_WIN].rearrange("r (j c) -> r c j", j=4),
                            nat_w[:, 0:C_WIN].rearrange("r (c j) -> r c j", j=4)).then_inc(m["tabled"], 1)
            dve.tensor_copy(table_w[:, C_WIN:LW], nat_w[:, C_WIN:LW]).then_inc(m["tabled"], 1)
            dve.wait_ge(m["tabled"], 4)
            dve.wait_ge(m["built"], 4)

            def shift(group, dst, bias, w, col):
                n = score_no[group]
                dve.wait_ge(scored[n % 3], n // 3 + 1)
                dve.tensor_tensor_reduce(out=dst, in0=logit[n % 3][:, 0:w], in1=bias, scale=-1.0, scalar=FLOOR,
                                         op0=ALU.add, op1=ALU.min, accum_out=nmax[:, col:col + 1]).then_inc(shifted_out[n % 3], 1)

            def hidden(b):
                for a in range(2):
                    ps = hps[:, a * 256:(a + 1) * 256].rearrange("p (g c) -> p g c", g=2)
                    dve.wait_ge(m["h_done"], 2 * b + 2)
                    if b:
                        dve.wait_ge(m["kc_done"], b)
                    dve.tensor_copy(h_next[:, a, :, :], ps[HD:P, :, 1:NCH]).then_inc(m["h_moved"], 1)
                    dve.wait_ge(m["h_moved"], 2 * b + a + 1)
                    dve.tensor_tensor(h_sum[:, a, :, :], ps[0:HD, :, 0:NC], h_next[:, a, :, :], ALU.add).then_inc(m["h_summed"], 1)

            def compressed(b):
                dve.wait_ge(m["kc_done"], b + 1)
                if b:
                    dve.wait_ge(m["cmp_out"], b)
                dve.tensor_copy(kcT[:, :], cps[:, 0:NC]).then_inc(m["kc_out"], 1)
                dve.tensor_copy(vc[:, :], cps[0:NC, 128:256]).then_inc(m["kc_out"], 1)
                dve.wait_ge(m["cmp_scored"], b + 1)
                dve.tensor_tensor_reduce(out=sc_cmp[:, :], in0=cps[:, 256:256 + NC], in1=zeros[:, 0:NC], scale=-1.0, scalar=FLOOR,
                                         op0=ALU.add, op1=ALU.min, accum_out=nmax[:, 10:11]).then_inc(m["cmp_shifted"], 1)

            def choose(b):
                dve.wait_ge(m["cmp_exped"], b + 1)
                dve.reciprocal(wgt[:, 2:3], total[:, 2:3]).then_inc(m["cmp_total"], 1)
                dve.wait_ge(m["cmp_total"], b + 1)
                dve.tensor_scalar(pc[:, :], pc[:, :], wgt[:, 2:3], None, ALU.mult).then_inc(m["cmp_normed"], 1)
                dve.wait_ge(m["imp_done"], b + 1)
                dve.tensor_copy(imp[:, 1:NC + 1], cps[0:16, 384:384 + NC]).then_inc(m["imp_out"], 1)
                n = turn_no[("pc", b, 0)]
                dve.wait_ge(tps_turned[n % 2], n // 2 + 1)
                dve.tensor_copy(pcT[:, :], tps[n % 2][0:NC, 0:P]).then_inc(tps_out[n % 2], 1)
                dve.wait_ge(tps_out[n % 2], n // 2 + 1)
                dve.sem_inc(m["pcT_ready"], 1)
                dve.wait_ge(m["imp_out"], b + 1)
                dve.tensor_tensor(pair[:, :], imp[:, 1:P + 1], imp[:, 0:P], ALU.add).then_inc(m["paired"], 1)
                dve.wait_ge(m["paired"], b + 1)
                dve.tensor_reduce(blocks[:, 0:32], pair[:, :].rearrange("r (k c) -> r k c", c=4), AX_X, ALU.add).then_inc(m["block_sums"], 1)
                dve.memset(blocks[:, 32:33], 0.0).then_inc(m["block_sums"], 1)
                dve.wait_ge(m["block_sums"], 2 * b + 2)
                dve.tensor_tensor(blocks[:, :], blocks[:, :], keep.sel_bonus[:, :], ALU.add).then_inc(m["bonus"], 1)
                for r in range(SEL_TOP // 8):
                    dve.wait_ge(m["bonus"], 3 * b + r + 1)
                    dve.max(best[:, r, :], blocks[:, :]).then_inc(m["picked"], 1)
                    dve.wait_ge(m["picked"], 2 * b + r + 1)
                    dve.match_replace(out=blocks[:, :], in_to_replace=best[:, r, :], in_values=blocks[:, :], imm_value=TAKEN).then_inc(m["bonus"], 1)
                dve.wait_ge(m["bonus"], 3 * b + 3)
                dve.tensor_scalar(choice[:, b % 2, :], blocks[:, :], TAKEN / 2, NEG, ALU.is_gt, ALU.mult).then_inc(m["chosen"], 1)

            def part(b, br, col, weight_col):
                for g in range(2):
                    r = slice(g * HD, (g + 1) * HD)
                    src = outp[r, col + g * HD:col + (g + 1) * HD]
                    if br == 0:
                        dve.tensor_scalar(o[r, 0, :], src, weight_col[r, :], None, ALU.mult).then_inc(m["o_part"], 1)
                    else:
                        dve.scalar_tensor_tensor(out=o[r, br, :], in0=src, scalar=weight_col[r, :], in1=o[r, br - 1, :],
                                                 op0=ALU.mult, op1=ALU.add).then_inc(m["o_part"], 1)

            for b in range(-1, NB):
                if b + 1 < NB:
                    hidden(b + 1)
                if b >= 0:
                    if b:
                        dve.wait_ge(m["slc_out"], b)
                    for i in range(4):
                        shift(("s", b, i), shifted[:, i * 512:(i + 1) * 512], table[:, i * 512:(i + 1) * 512], 512, i)
                    shift(("s", b, 4), shifted[:, PAST:LS], table[:, PAST:LS], NS, 4)
                    shift(("w", b, 0), shifted_w[:, 0:C_WIN], table_w[:, 0:C_WIN], 512, 5)
                    shift(("w", b, 1), shifted_w[:, C_WIN:LW], table_w[:, C_WIN:LW], NS, 6)
                    for i in range(3):
                        dve.wait_ge(shifted_out[i], len([g for g in scores_order[:7 * (b + 1)] if score_no[g] % 3 == i]))
                    dve.tensor_reduce(nmax[:, 8:9], nmax[:, 0:5], AX_X, ALU.min).then_inc(m["weighed"], 1)
                    dve.tensor_reduce(nmax[:, 9:10], nmax[:, 5:7], AX_X, ALU.min).then_inc(m["slc_max"], 1)
                if b + 1 < NB:
                    compressed(b + 1)
                if b >= 0:
                    for i in range(5):
                        rows, cnt = (P, 4) if i < 4 else (NS, 1)
                        n = turn_no[("p", b, i)]
                        dve.wait_ge(tps_turned[n % 2], n // 2 + 1)
                        dve.tensor_copy(pT[0:rows, 4 * i:4 * i + cnt, :], tps[n % 2][0:rows, 0:cnt * P].rearrange("p (j r) -> p j r", j=cnt)).then_inc(tps_out[n % 2], 1)
                        dve.wait_ge(tps_out[n % 2], n // 2 + 1)
                        dve.sem_inc(m["pT_ready"], 1)
                    for i in range(2):
                        rows, cnt = (P, 4) if i < 1 else (NS, 1)
                        n = turn_no[("pw", b, i)]
                        dve.wait_ge(tps_turned[n % 2], n // 2 + 1)
                        dve.tensor_copy(pwT[0:rows, 4 * i:4 * i + cnt, :], tps[n % 2][0:rows, 0:cnt * P].rearrange("p (j r) -> p j r", j=cnt)).then_inc(tps_out[n % 2], 1)
                        dve.wait_ge(tps_out[n % 2], n // 2 + 1)
                        dve.sem_inc(m["pwT_ready"], 1)
                    dve.wait_ge(m["win_exped"], b + 1)
                    dve.reciprocal(wgt[:, 0:2], total[:, 0:2]).then_inc(m["inverted"], 1)
                    dve.wait_ge(m["inverted"], b + 1)
                    dve.tensor_tensor(wgt[:, 0:2], gate[:, 1:3, b], wgt[:, 0:2], ALU.mult).then_inc(m["weighed"], 1)
                    dve.wait_ge(m["weighed"], 2 * b + 2)
                    dve.wait_ge(m["win_out"], b + 1)
                    part(b, 0, 0, gate[:, 0, b:b + 1])
                    dve.wait_ge(m["o_part"], 6 * b + 2)
                    part(b, 1, 128, wgt[:, 0:1])
                    dve.wait_ge(m["o_part"], 6 * b + 4)
                    part(b, 2, 256, wgt[:, 1:2])
                    dve.wait_ge(m["o_part"], 6 * b + 6)
                    dve.sem_inc(m["o_ready"], 1)
                    dve.wait_ge(m["o_turned"], b + 1)
                    src = outp[0:HD, 384:512].rearrange("e (h two q) -> e h two q", two=2, q=NS)
                    for odd in range(2):
                        dve.tensor_copy(keep.mixT[odd * HD:(odd + 1) * HD, :, SEQ + b * NS:SEQ + (b + 1) * NS], src[:, :, odd, :]).then_inc(m["mixed"], 1)
                if b + 1 < NB:
                    choose(b + 1)


class Keep:
    pass


def build(nc, io):
    keep, dram = Keep(), Keep()
    dram.vec_up = nc.dram_tensor("vec_up", [3, N_HEADS, LU], F32, kind="Internal").ap()
    dram.hT_ab = nc.dram_tensor("hT_ab", [AB_COLS, T], F32, kind="Internal").ap()
    dram.hT_c = nc.dram_tensor("hT_c", [C_COLS, T], F32, kind="Internal").ap()
    dram.vec = nc.dram_tensor("vec", [3, N_HEADS, LV], F32, kind="Internal").ap()
    with ExitStack() as ctx:
        def sb(name, shape, dt=F32):
            return ctx.enter_context(nc.sbuf_tensor(name, shape, dt))

        keep.xtok = sb("xtok", [P, NT, D])
        keep.xT = sb("xT", [P, KC, T])
        keep.mixT = sb("mixT", [P, KC, T])
        keep.ident = sb("ident", [P, P])
        keep.ident_bf = sb("ident_bf", [P, P], BF16)
        keep.causal = sb("causal", [P, P])
        keep.chunk_row = sb("chunk_row", [P, NB], I32)
        keep.eps = sb("eps", [P, 1])
        copied = ctx.enter_context(nc.semaphore("state_copied"))
        const_in = ctx.enter_context(nc.semaphore("const_in"))
        keep.kidx_in = [ctx.enter_context(nc.semaphore(f"kidx_in{b}")) for b in range(NB)]
        keep.a_kv_in = [ctx.enter_context(nc.semaphore(f"a_kv_in{i}")) for i in range(2)]
        keep.c_kv_in = [ctx.enter_context(nc.semaphore(f"c_kv_in{i}")) for i in range(2)]
        consts = [("same_token", [P, 16]), ("pick_row", [TS, NB, TS]), ("new_causal", [TS, NS]), ("group_sum", [P, 16]),
                  ("group_spread", [16, P]), ("sel_bonus", [16, N_SEL])]
        held = {name: sb(name, shape) for name, shape in consts}
        keep.same_token, keep.pick_row, keep.new_causal = held["same_token"], held["pick_row"], held["new_causal"]
        keep.group_sum, keep.group_spread, keep.sel_bonus = held["group_sum"], held["group_spread"], held["sel_bonus"]
        keep.gate_tok = sb("gate_tok", [P, NQ, 48])
        keep.cmp_const = sb("cmp_const", [HD, 2])

        for b in range(NB):
            nc.gpsimd.dma_start(io["o_s_b_kv"][b, 0:PAST - NS, :], io["state_b_kv"][b, NS:PAST, :]).then_inc(copied, 16)
        nc.gpsimd.dma_start(io["o_s_c_win"][:, 0:C_WIN - NS, :], io["state_c_kv"][:, NS:C_WIN, :]).then_inc(copied, 16)
        for name, shape in consts:
            whole = tuple(slice(0, n) for n in shape)
            nc.sync.dma_start(held[name][whole], io["c_" + name]).then_inc(const_in, 16)
        nc.vector.memset(keep.eps[:, :], LN_EPS)
        nc.sync.wait_ge(const_in, 16 * len(consts))

        setup_phase(nc, io, keep, dram)
        project_phase(nc, "proj_ab", io["w_in_ab"], AB_COLS, dram.hT_ab, keep)
        with ExitStack() as ab:
            tok = ab.enter_context(nc.sbuf_tensor("tok_ab", [P, NT, TAB], F32))
            sel_mask = ab.enter_context(nc.sbuf_tensor("sel_mask", [TS, LS], BF16))
            token_major_phase(nc, "tok_ab", dram.hT_ab, [(A_K, 256, TA_K), (A_KI, 72, TA_KI), (B_K, 1024, TB_K)], tok, [
                (io["o_p_a_kv"].rearrange("(i p) c -> p i c", p=P), tok[:, 0:NQ, 0:256]),
                (io["o_p_a_kidx"].rearrange("(i p) c -> p i c", p=P), tok[:, 0:NQ, TA_KI:TA_W]),
                (io["o_p_b_kv"][3 * SEQ:, :].rearrange("(i p) c -> p i c", p=P), tok[:, 0:NQ, TB_K:TAB]),
                (io["o_s_a_kv"].rearrange("b q c -> (b q) c"), tok[0:TS, NQ, 0:256]),
                (io["o_s_a_kidx"].rearrange("b q c -> (b q) c"), tok[0:TS, NQ, TA_KI:TA_W]),
            ] + [(io["o_s_b_kv"][b, PAST - NS:PAST, :], tok[b * NS:(b + 1) * NS, NQ, TB_K:TAB]) for b in range(NB)], keep)
            sample_indexer_phase(nc, dram.hT_ab, io["cache_a_kidx"], io, sel_mask, keep)
            with ExitStack() as pr:
                mix = pr.enter_context(nc.sbuf_tensor("mix_ab", [P, NQ, D], F32))
                sel_bias = pr.enter_context(nc.sbuf_tensor("sel_bias", [P, NQ - 1, SEQ], BF16))
                prompt_indexer_phase(nc, dram.hT_ab, tok, sel_bias, keep)
                prompt_attention_phase(nc, "pab", [
                    dict(heads=H_A, q=A_Q, k=A_K, kv=2, v=TA_V, kind=KIND_FULL, h0=0, out=0, sel=sel_bias, gate=None),
                    dict(heads=H_B, q=B_Q, k=B_K, kv=H_B, v=TB_V, kind=KIND_DIL, h0=8, out=512, sel=None, gate=None),
                ], dram.hT_ab, dram.vec_up, tok, mix, keep)
                turn_mix_phase(nc, "mix_ab_turn", mix, keep)
            sample_a_phase(nc, dram.hT_ab, dram.vec, io["cache_a_kv"], io["o_s_a_kv"], io, sel_mask, keep)
        sample_b_phase(nc, dram.hT_ab, dram.vec, io["state_b_kv"], io["o_s_b_kv"][:, PAST - NS:PAST, :], io, keep)
        output_phase(nc, "out_ab", io["w_out_ab"], io["ln1_g"][0], io["ln1_b"][0], keep)
        ffn_phase(nc, "ffn0", io["ffn_up"][0], io["ffn_conv_w"][0], io["ffn_conv_b"][0], io["ffn_down"][0], io["state_ffn"][0],
                  io["ln2_g"][0], io["ln2_b"][0], io["o_p_ffn"][0], io["o_s_ffn"][0], None, keep)

        project_phase(nc, "proj_c", io["w_in_c"], C_COLS, dram.hT_c, keep)
        with ExitStack() as c:
            tok = c.enter_context(nc.sbuf_tensor("tok_c", [P, NT, TC], F32))
            mix = c.enter_context(nc.sbuf_tensor("mix_c", [P, NQ, D], F32))
            token_major_phase(nc, "tok_c", dram.hT_c, [(C_KV, 768, 0), (C_G, 48, TC_G)], tok, [
                (io["o_p_c_kv"].rearrange("(i p) c -> p i c", p=P), tok[:, 0:NQ, 0:512]),
                (io["o_p_c_win"].rearrange("(i p) c -> p i c", p=P), tok[:, 0:NQ, 512:768]),
                (io["o_s_c_kv"].rearrange("b q c -> (b q) c"), tok[0:TS, NQ, 0:512]),
            ] + [(io["o_s_c_win"][b, C_WIN - NS:C_WIN, :], tok[b * NS:(b + 1) * NS, NQ, 512:768]) for b in range(NB)], keep)
            prompt_compressed_phase(nc, dram.hT_c, tok, mix, io, keep)
            prompt_attention_phase(nc, "pc", [
                dict(heads=N_HEADS, q=C_Q, k=C_KV + 2 * P, kv=2, v=3 * P, kind=KIND_FULL, h0=0, out=0, sel=None, gate=N_HEADS),
                dict(heads=N_HEADS, q=C_Q, k=C_KV + 4 * P, kv=2, v=5 * P, kind=KIND_WIN, h0=0, out=0, sel=None, gate=2 * N_HEADS),
            ], dram.hT_c, dram.vec_up, tok, mix, keep)
            turn_mix_phase(nc, "mix_c_turn", mix, keep)
        sample_c_phase(nc, dram.hT_c, dram.vec, io["cache_c_kv"], io["state_c_kv"], io["o_s_c_kv"],
                       io["o_s_c_win"][:, C_WIN - NS:C_WIN, :], io, keep)
        output_phase(nc, "out_c", io["w_out_c"], io["ln1_g"][1], io["ln1_b"][1], keep)
        ffn_phase(nc, "ffn1", io["ffn_up"][1], io["ffn_conv_w"][1], io["ffn_conv_b"][1], io["ffn_down"][1], io["state_ffn"][1],
                  io["ln2_g"][1], io["ln2_b"][1], io["o_p_ffn"][1], io["o_s_ffn"][1], (io["o_y_prompt"], io["o_y_sample"]), keep)
        nc.sync.wait_ge(copied, 16 * (NB + 1))


def t5_buckets(dist):
    n = np.maximum(dist, 0)
    nf = np.maximum(n, 1).astype(np.float32)
    far = 16 + (np.log(nf / np.float32(16)) / np.float32(np.log(8.0)) * np.float32(16)).astype(np.int32)
    return np.where(n < 16, n, np.minimum(far, 31))


def distance_rows(dist):
    rows = np.zeros((33, 3, len(dist)), np.float32)
    rows[t5_buckets(dist), :, np.arange(len(dist))] = 1.0
    held = sum(((dist >= 0) & (dist <= w) & (dist % d == 0)).astype(np.float64) for w, d in B_WINDOWS)
    rows[32, KIND_FULL] = np.where(dist >= 0, 0.0, NEG)
    rows[32, KIND_WIN] = np.where((dist >= 0) & (dist < C_WIN), 0.0, NEG)
    rows[32, KIND_DIL] = np.where(held > 0, np.log(np.maximum(held, 1.0)), NEG)
    return rows


def shape_constants():
    onehot, onehot_up = distance_rows(FAR - np.arange(LV)), distance_rows(np.arange(LU) + 1 - P)
    i = np.arange(P)
    j2hq = np.arange(P)
    bq = np.arange(TS)
    pick = np.zeros((TS, NB, TS), np.float32)
    for b in range(NB):
        pick[:, b, :] = (bq[:, None] // NS == b) & (bq[:, None] % NS == np.arange(TS)[None, :] % NS)
    group = (j2hq[:, None] // 64 == np.arange(16)[None, :] // NS) & (j2hq[:, None] % NS == np.arange(16)[None, :] % NS)
    cmp_mask = np.full((P, NQ, 32), NEG, np.float32)
    for t in range(NQ):
        pos = t * P + i[:, None]
        cmp_mask[:, t, 0:31] = np.where(np.arange(31)[None, :] * STRIDE + 2 * STRIDE - 1 <= pos, 0.0, NEG)
    blk = np.arange(N_SEL)
    cur = PAST // 64
    return {
        "c_ident": np.eye(P, dtype=np.float32),
        "c_causal": np.where(i[None, :] <= i[:, None], 0.0, NEG).astype(np.float32),
        "c_onehot": onehot,
        "c_onehot_up": onehot_up,
        "c_same_token": group.astype(np.float32),
        "c_group_sum": group.astype(np.float32),
        "c_group_spread": np.ascontiguousarray(group.T).astype(np.float32),
        "c_pick_row": pick,
        "c_new_causal": np.where(np.arange(NS)[None, :] <= bq[:, None] % NS, 0.0, NEG).astype(np.float32),
        "c_cmp_mask": cmp_mask,
        "c_sel_bonus": np.tile(np.where((blk == 0) | (blk == cur) | (blk == cur - 1), SEL_BONUS, 0.0), (16, 1)).astype(np.float32),
    }


VIEWS = {
    "x_prompt": (1, SEQ, D), "x_sample": (NB, NS, D), "cache_a_kv": (160, PAGE, 2, 2, HD), "cache_a_kidx": (160, PAGE, HD),
    "cache_c_kv": (160, PAGE, 4, 2, HD), "state_b_kv": (NB, PAST, D), "state_c_kv": (NB, C_WIN, 256),
    "state_ffn": (2, NB, 2, 2 * D_FF), "page_table": (NB, 16), "rel_bias": (32, 16), "w_in_ab": (D, AB_COLS), "w_out_ab": (D, D),
    "w_in_c": (D, C_COLS), "w_out_c": (D, D), "phi_pe": (2, 32, HD), "phi_w1": (2, 32, HD, HD), "phi_b1": (2, HD),
    "phi_w2": (2, HD, HD), "ln1_g": (2, D), "ln1_b": (2, D), "ln2_g": (2, D), "ln2_b": (2, D), "ffn_up": (2, D, 2 * D_FF),
    "ffn_conv_w": (2, CONV_W, 2 * D_FF), "ffn_conv_b": (2, 2 * D_FF), "ffn_down": (2, D_FF, D),
}
OUTS = [
    ("y_prompt", (1, SEQ, D), (1, SEQ, D)), ("y_sample", (NB, NS, D), (NB, NS, D)),
    ("p_a_kv", (SEQ, 256), (1, 1, SEQ, 2, 2, HD)), ("p_a_kidx", (SEQ, HD), (1, 1, SEQ, HD)),
    ("p_b_kv", (PAST, D), (1, 1, PAST, 2, 8, HD)), ("p_c_kv", (SEQ, 512), (1, 1, SEQ, 4, 2, HD)),
    ("p_c_win", (SEQ, 256), (1, 1, C_WIN, 2, 2, HD)), ("p_ffn", (2, 2, 2 * D_FF), (2, 1, 2, 2 * D_FF)),
    ("s_a_kv", (NB, NS, 256), (1, NB, NS, 2, 2, HD)), ("s_a_kidx", (NB, NS, HD), (1, NB, NS, HD)),
    ("s_b_kv", (NB, PAST, D), (1, NB, PAST, 2, 8, HD)), ("s_c_kv", (NB, NS, 512), (1, NB, NS, 4, 2, HD)),
    ("s_c_win", (NB, C_WIN, 256), (1, NB, C_WIN, 2, 2, HD)), ("s_ffn", (2, 2 * NB, 2 * D_FF), (2, NB, 2, 2 * D_FF)),
]


def kernel(**inputs):
    import concourse.bacc as bacc
    from concourse.bass_utils import run_bass_kernel_spmd

    nc = bacc.Bacc("TRN2", target_bir_lowering=False, num_devices=1)
    arrays, io = {}, {}
    for name, shape in VIEWS.items():
        arrays[name] = np.ascontiguousarray(inputs[name]).reshape(shape)
    arrays.update(shape_constants())
    for name, a in arrays.items():
        io[name] = nc.dram_tensor(name, list(a.shape), mybir.dt.from_np(a.dtype), kind="ExternalInput").ap()
    for name, view, _ in OUTS:
        io["o_" + name] = nc.dram_tensor("out_" + name, list(view), F32, kind="ExternalOutput").ap()
    build(nc, io)
    r = run_bass_kernel_spmd(nc, [arrays], core_ids=[0]).results[0]
    return tuple(r["out_" + name].reshape(shape) for name, _, shape in OUTS)
```

```python
from contextlib import ExitStack, contextmanager

import concourse.bass as bass
import numpy as np
from concourse import mybir

F32 = mybir.dt.float32
BF16 = mybir.dt.bfloat16
F32R = mybir.dt.float32r
I32 = mybir.dt.int32
ALU = mybir.AluOpType
ACT = mybir.ActivationFunctionType
AX_X = mybir.AxisListType.X

P = 128
D = 1024
KC = D // P
SEQ = 512
NQ = SEQ // P
NB, NS = 8, 8
TS = NB * NS
T = SEQ + TS
TH = T // 2
TILES = [(i * P, P) for i in range(NQ)] + [(SEQ, TS)]
NT = len(TILES)
PAST = 2048
PAGE = 128
LS = PAST + NS
HD = 64
STRIDE = 16
NCH = PAST // STRIDE
N_HEADS = 16
H_A = H_IDX = H_B = 8
AB_COLS = 2888
C_COLS = 1840
B_WINDOWS = ((128, 1), (512, 4), (2048, 16))
C_WIN = 512
DSA_TOP_PROMPT = 128
DSA_TOP_SAMPLE = 256
N_SEL = 33
SEL_TOP = 16
SEL_BONUS = 1e3
D_FF = 2816
NF = D_FF // P
CONV_W = 3
ALPHA = 4 ** 0.25
LN_EPS = 1e-5
SCALE = HD ** -0.5
IDX_SCALE = HD ** -0.5 * H_IDX ** -0.5
NEG = -1e30
FLOOR = 1e29
TAKEN = -3e38
A_Q, A_K, A_V, A_QI, A_KI, A_W, B_Q, B_K, B_V = 0, 512, 640, 768, 1280, 1344, 1352, 1864, 2376
C_Q, C_KV, C_G = 0, 1024, 1792
TA_K, TA_V, TA_KI, TA_W, TB_K, TB_V, TAB = 0, 128, 256, 320, 328, 840, 1352
TC_G, TC = 768, 816
FAR = 2056
LV = FAR + P
LU = SEQ + 2 * P
KIND_FULL, KIND_WIN, KIND_DIL = 0, 1, 2


class Phase:

    def __init__(self, nc, ctx, name):
        self.nc, self.ctx, self.name, self.sems = nc, ctx, name, []
        self.body = ExitStack()

    def sb(self, name, shape, dt=F32):
        return self.ctx.enter_context(self.nc.sbuf_tensor(f"{self.name}_{name}", shape, dt))

    def ps(self, name, shape, dt=F32):
        return self.ctx.enter_context(self.nc.psum_tensor(f"{self.name}_{name}", shape, dt))

    def sem(self, name):
        s = self.ctx.enter_context(self.nc.semaphore(f"{self.name}_{name}"))
        self.sems.append(s)
        return s


@contextmanager
def phase(nc, name):
    with ExitStack() as ctx:
        p = Phase(nc, ctx, name)
        with p.body:
            yield p
        for s in p.sems:
            nc.gpsimd.sem_clear(s)
        nc.all_engine_barrier()


def setup_phase(nc, io, keep, dram):
    with phase(nc, "setup") as p:
        onehot = p.sb("onehot", [33, 3, LV])
        onehot_up = p.sb("onehot_up", [33, 3, LU])
        tabx = p.sb("tabx", [33, N_HEADS])
        vec_sb = p.sb("vec", [N_HEADS, 3, LV])
        vec_up = p.sb("vec_up", [N_HEADS, 3, LU])
        rep8 = p.sb("rep8", [P, 1], I32)
        pages = p.sb("pages", [P, NB], I32)
        zero = keep.zero
        acc = [p.ps(f"acc{i}", [P, 512]) for i in range(4)]
        xps = [p.ps(f"xps{i}", [P, 512]) for i in range(4)]
        loaded, x_in, ones_set, vec_ready, vec_out, stored = (
            p.sem(n) for n in ("loaded", "x_in", "ones_set", "vec_ready", "vec_out", "stored"))
        x_high = p.sem("x_high")
        x_ready, x_out, iota_done, rem_done, idx_done, zero_set, cast_done = (
            p.sem(n) for n in ("x_ready", "x_out", "iota_done", "rem_done", "idx_done", "zero_set", "cast_done"))
        ranges = [(onehot, vec_sb, k, c, min(512, LV - c)) for k in range(3) for c in range(0, LV, 512)]
        ranges += [(onehot_up, vec_up, k, c, min(512, LU - c)) for k in range(3) for c in range(0, LU, 512)]
        block = p.body.enter_context(nc.Block())

        @block.sync
        def _(sp):
            sp.dma_start(keep.xtok[:, 0:NQ, :], io["x_prompt"].rearrange("b (i p) d -> p (b i) d", p=P)).then_inc(x_in, 16)
            sp.dma_start(keep.xtok[0:TS, NQ, :], io["x_sample"].rearrange("b q d -> (b q) d")).then_inc(x_in, 16)
            sp.dma_start(keep.ident[:, :], io["c_ident"]).then_inc(x_in, 16)
            sp.dma_start(onehot[:, :, :], io["c_onehot"]).then_inc(loaded, 16)
            sp.dma_start(onehot_up[:, :, :], io["c_onehot_up"]).then_inc(loaded, 16)
            sp.dma_start(tabx[0:32, :], io["rel_bias"]).then_inc(loaded, 16)
            sp.dma_start(keep.causal[:, :], io["c_causal"]).then_inc(loaded, 16)
            with nc.allow_non_contiguous_dma(reason="one page number for each of a page's 8 chunks"):
                pt = io["page_table"]
                for b in range(NB):
                    sp.dma_start(pages[:, b:b + 1],
                                 bass.AP(tensor=pt.tensor, offset=16 * b, ap=[[1, 16], [0, 8], [1, 1]])).then_inc(loaded, 16)
            sp.wait_ge(vec_out, len(ranges))
            sp.dma_start(dram.vec.rearrange("k h m -> h k m"), vec_sb[:, :, :]).then_inc(stored, 16)
            sp.dma_start(dram.vec_up.rearrange("k h m -> h k m"), vec_up[:, :, :]).then_inc(stored, 16)
            sp.wait_ge(stored, 32)
            sp.wait_ge(loaded, 16 * (4 + NB))
            sp.wait_ge(zero_set, 1)

        @block.gpsimd
        def _(pool):
            pool.iota(rep8[:, :], pattern=[[0, 1]], base=0, channel_multiplier=1).then_inc(iota_done, 1)
            pool.memset(zero[:, :], 0.0).then_inc(zero_set, 1)

        @block.tensor
        def _(pe):
            pe.wait_ge(x_in, 48)
            n = 0
            for k in range(KC):
                for t0, tn in ((0, NQ), (NQ, 1)):
                    if n >= 4:
                        pe.wait_ge(x_out, n - 3)
                    for t in range(t0, t0 + tn):
                        w = TILES[t][1]
                        last = pe.transpose(xps[n % 4][:, (t - t0) * P:(t - t0) * P + w],
                                            keep.xtok[0:w, t, k * P:(k + 1) * P], keep.ident[0:w, 0:w])
                    last.then_inc(x_ready, 1)
                    n += 1
            pe.wait_ge(ones_set, 1)
            pe.wait_ge(loaded, 16 * (4 + NB))
            for n, (source, dest, k, c, w) in enumerate(ranges):
                if n >= 4:
                    pe.wait_ge(vec_out, n - 3)
                pe.matmul(acc[n % 4][0:N_HEADS, 0:w], tabx[:, :], source[:, k, c:c + w],
                          start=True, stop=True).then_inc(vec_ready, 1)

        @block.scalar
        def _(act):
            n = 0
            for k in range(KC):
                for t0, w in ((0, SEQ), (SEQ, TS)):
                    act.wait_ge(x_ready, n + 1)
                    act.copy(keep.xh[:, k, t0:t0 + w], xps[n % 4][:, 0:w]).then_inc(x_high, 1)
                    n += 1

        @block.vector
        def _(dve):
            dve.memset(tabx[32:33, :], 1.0).then_inc(ones_set, 1)
            dve.wait_ge(iota_done, 1)
            dve.tensor_single_scalar(rep8[:, :], rep8[:, :], 7, ALU.bitwise_and).then_inc(rem_done, 1)
            dve.wait_ge(rem_done, 1)
            dve.wait_ge(loaded, 16 * (4 + NB))
            for b in range(NB):
                dve.scalar_tensor_tensor(out=keep.chunk_row[:, b:b + 1], in0=pages[:, b:b + 1], scalar=8.0,
                                         in1=rep8[:, :], op0=ALU.mult, op1=ALU.add).then_inc(idx_done, 1)
            dve.wait_ge(x_in, 48)
            dve.tensor_copy(keep.ident_bf[:, :], keep.ident[:, :]).then_inc(cast_done, 1)
            n = 0
            for k in range(KC):
                for t0, w in ((0, SEQ), (SEQ, TS)):
                    dve.wait_ge(x_high, n + 1)
                    low_part(dve, keep.xl[:, k, t0:t0 + w], xps[n % 4][:, 0:w], keep.xh[:, k, t0:t0 + w]).then_inc(x_out, 1)
                    n += 1
            for n, (source, dest, k, c, w) in enumerate(ranges):
                dve.wait_ge(vec_ready, n + 1)
                dve.tensor_copy(dest[:, k, c:c + w], acc[n % 4][0:N_HEADS, 0:w]).then_inc(vec_out, 1)


def low_part(dve, low, whole, high):
    return dve.tensor_tensor(low, whole, high.bitcast(F32), ALU.subtract)


def split_product(pe, out, wh, wl, xh, xl, first, last):
    for weights, moving, start, stop in ((wh, xh, first, False), (wh, xl, False, False), (wl, xh, False, last)):
        for o, x in zip(out, moving):
            done = pe.matmul(o, weights, x, start=start, stop=stop)
    return done


def halves(x, k):
    return x[:, k, 0:TH], x[:, k, TH:T]


def project_phase(nc, name, w_in, cols, hT, keep, late_stores=()):
    groups, tail = cols // 256, cols % 256
    loops = groups // 2
    assert groups == 2 * loops + 1 and 0 < tail <= P
    with phase(nc, name) as p:
        w = p.sb("w", [P, 2, KC, 256])
        wh = p.sb("wh", [P, 2, KC, 256], F32R)
        wl = p.sb("wl", [P, 2, KC, 256], F32R)
        stage = p.sb("stage", [P, 4, T])
        acc = [[p.ps(f"acc{i}_{h}", [P, 512]) for h in range(2)] for i in range(4)]
        w_loaded = [p.sem(f"w_loaded{i}") for i in range(2)]
        high, low, stored = p.sem("w_high"), p.sem("w_low"), p.sem("stored")
        done, copied0, copied1 = p.sem("done"), p.sem("copied0"), p.sem("copied1")
        st_free = [p.sem(f"st_free{i}") for i in range(4)]
        wv = w_in.rearrange("(k p) n -> p k n", p=P)
        blocks = 4 * loops
        rest_blocks = [(2 * loops * 256, P), (2 * loops * 256 + P, P), (groups * 256, tail)]
        block = p.body.enter_context(nc.Block())

        @block.sync
        def _(sp):
            with sp.Fori(0, loops) as i:
                for s in range(2):
                    sp.wait_ge(low, i * 2 + (s + 1))
                    sp.dma_start(w[:, s, :, :], wv[:, :, bass.ds(i * 512 + s * 256, 256)]).then_inc(w_loaded[s], 16)
            for s, cw in ((0, 256), (1, tail)):
                c0 = (2 * loops + s) * 256
                sp.wait_ge(low, 2 * loops + s + 1)
                sp.dma_start(w[:, s, :, 0:cw], wv[:, :, c0:c0 + cw]).then_inc(w_loaded[s], 16)
            for dst, src in late_stores:
                sp.dma_start(dst, src).then_inc(stored, 16)
            if late_stores:
                sp.wait_ge(stored, 16 * len(late_stores))

        def column_block(pe, n, s, lo, slot):
            pe.wait_ge(copied0, n + 1)
            pe.wait_ge(copied1, n + 1)
            out = (acc[slot][0][:, 0:TH], acc[slot][1][:, 0:TH])
            for k in range(KC):
                last = split_product(pe, out, wh[:, s, k, lo:lo + P], wl[:, s, k, lo:lo + P], halves(keep.xh, k), halves(keep.xl, k),
                                     k == 0, k == KC - 1)
            last.then_inc(done, 1)

        @block.tensor
        def _(pe):
            pe.sem_inc(done, 4)
            pe.sem_inc(copied0, 4)
            pe.sem_inc(copied1, 4)
            with pe.Fori(0, loops) as i:
                for s in range(2):
                    pe.wait_ge(low, i * 2 + (s + 3))
                    for j in range(2):
                        column_block(pe, i * 4 + 2 * s + j, s, j * P, 2 * s + j)
            pe.wait_ge(low, 2 * loops + 3)
            for j in range(2):
                column_block(pe, blocks + j, 0, j * P, j)
            pe.wait_ge(low, 2 * loops + 4)
            column_block(pe, blocks + 2, 1, 0, 2)

        def split_high(act, g, i, s):
            act.wait_ge(w_loaded[s], i * 16 + 16)
            act.wait_ge(done, g * 2 + 2)
            act.copy(wh[:, s, :, :], w[:, s, :, :]).then_inc(high, 1)

        def split_low(dve, g, s):
            dve.wait_ge(high, g + 1)
            low_part(dve, wl[:, s, :, :], w[:, s, :, :], wh[:, s, :, :]).then_inc(low, 1)

        @block.scalar
        def _(act):
            for slot in range(4):
                act.sem_inc(st_free[slot], 16)

            def evacuate(n, i, slot, row, m):
                act.wait_ge(done, n + 5)
                act.wait_ge(st_free[slot], i * 16 + 16)
                act.copy(stage[0:m, slot, 0:TH], acc[slot][0][0:m, 0:TH]).then_inc(copied0, 1)
                act.wait_ge(copied0, n + 5)
                act.wait_ge(copied1, n + 5)
                act.dma_start(hT[bass.ds(row, m), :], stage[0:m, slot, :]).then_inc(st_free[slot], 16)

            for s in range(2):
                split_high(act, s, 0, s)
            with act.Fori(0, loops) as i:
                for s in range(2):
                    for j in range(2):
                        evacuate(i * 4 + 2 * s + j, i, 2 * s + j, i * 512 + (2 * s + j) * P, P)
                    split_high(act, i * 2 + (s + 2), i + 1, s)
            for r, (c0, m) in enumerate(rest_blocks):
                evacuate(blocks + r, loops, r, c0, m)
            for slot in range(4):
                act.wait_ge(st_free[slot], 16 + 16 * len(range(slot, blocks + len(rest_blocks), 4)))

        @block.vector
        def _(dve):
            dve.sem_inc(low, 2)

            def evacuate(n, i, slot, m):
                dve.wait_ge(done, n + 5)
                dve.wait_ge(st_free[slot], i * 16 + 16)
                dve.tensor_copy(stage[0:m, slot, TH:T], acc[slot][1][0:m, 0:TH]).then_inc(copied1, 1)

            for s in range(2):
                split_low(dve, s, s)
            with dve.Fori(0, loops) as i:
                for s in range(2):
                    for j in range(2):
                        evacuate(i * 4 + 2 * s + j, i, 2 * s + j, P)
                    split_low(dve, i * 2 + (s + 2), s)
            for r, (c0, m) in enumerate(rest_blocks):
                evacuate(blocks + r, loops, r, m)


def token_major_phase(nc, name, hT, pieces, tok, stores, keep):
    chunks = [(r0 + o, min(P, n - o), c0 + o) for r0, n, c0 in pieces for o in range(0, n, P)]
    with phase(nc, name) as p:
        rows = p.sb("rows", [P, len(chunks), T])
        tp = [p.ps(f"tp{i}", [P, 512]) for i in range(4)]
        turned, out_done = p.sem("turned"), p.sem("out_done")
        row_sem = [p.sem(f"row_in{i}") for i in range(len(chunks))]
        block = p.body.enter_context(nc.Block())

        @block.sync
        def _(sp):
            for i, (r0, n, _) in enumerate(chunks):
                sp.dma_start(rows[0:n, i, :], hT[r0:r0 + n, :]).then_inc(row_sem[i], 16)
            sp.wait_ge(out_done, 2 * len(chunks))
            for dst, src in stores:
                sp.dma_start(dst, src).then_inc(keep.pending, 16)
            keep.pending_count += 16 * len(stores)

        @block.tensor
        def _(pe):
            for i, (_, n, _) in enumerate(chunks):
                pe.wait_ge(row_sem[i], 16)
                for half, (t0, tn) in enumerate(((0, NQ), (NQ, 1))):
                    u = 2 * i + half
                    if u >= 4:
                        pe.wait_ge(out_done, u - 3)
                    for t in range(t0, t0 + tn):
                        lo, w = TILES[t]
                        last = pe.transpose(tp[u % 4][0:w, (t - t0) * P:(t - t0) * P + n], rows[0:n, i, lo:lo + w],
                                            keep.ident[0:n, 0:n])
                    last.then_inc(turned, 1)

        @block.vector
        def _(dve):
            for i, (_, n, c0) in enumerate(chunks):
                for half in range(2):
                    u = 2 * i + half
                    dve.wait_ge(turned, u + 1)
                    if half == 0:
                        src = tp[u % 4][:, :].rearrange("p (t c) -> p t c", t=NQ)[:, :, 0:n]
                        dve.tensor_copy(tok[:, 0:NQ, c0:c0 + n], src).then_inc(out_done, 1)
                    else:
                        dve.tensor_copy(tok[0:TS, NQ, c0:c0 + n], tp[u % 4][0:TS, 0:n]).then_inc(out_done, 1)


class PromptSelection:

    ROUNDS = DSA_TOP_PROMPT // 8

    def __init__(self, p, pscore, bias):
        self.pscore, self.bias = pscore, bias
        self.score = p.sb("score", [P, NQ - 1, SEQ])
        self.best = p.sb("best", [P, 2, 8])
        self.loaded, self.picked, self.marked, self.biased = (p.sem(n) for n in ("score_in", "picked", "marked", "biased"))

    def load(self, sp):
        for i in range(1, NQ):
            L = (i + 1) * P
            sp.dma_start(self.score[:, i - 1, 0:L], self.pscore[:, i - 1, 0:L]).then_inc(self.loaded, 16)

    def round(self, dve, n):
        i, r = divmod(n, self.ROUNDS)
        s, best = self.score[:, i, 0:(i + 2) * P], self.best[:, n % 2, :]
        if n == 0:
            dve.wait_ge(self.loaded, 16 * (NQ - 1))
        else:
            dve.wait_ge(self.marked, n)
        dve.max(best, s).then_inc(self.picked, 1)
        dve.wait_ge(self.picked, n + 1)
        dve.match_replace(out=s, in_to_replace=best, in_values=s, imm_value=TAKEN).then_inc(self.marked, 1)
        if r == self.ROUNDS - 1:
            dve.wait_ge(self.marked, n + 1)
            dve.tensor_scalar(self.bias[:, i, 0:(i + 2) * P], s, TAKEN / 2, NEG, ALU.is_gt, ALU.mult).then_inc(self.biased, 1)


def prompt_indexer_phase(nc, hT, tok, pscore, keep):
    with phase(nc, "pidx") as p:
        qi = p.sb("qi", [HD, H_IDX, SEQ])
        ki = p.sb("ki", [HD, SEQ])
        relu = p.sb("relu", [P, 3, SEQ])
        score = p.sb("score", [P, 3, 2, SEQ])
        dots = [p.ps(f"dots{i}", [P, SEQ]) for i in range(4)]
        loaded, dot_done, relu_done, summed, stored = (p.sem(n) for n in ("loaded", "dot_done", "relu_done", "summed", "stored"))
        steps = [(i, h) for i in range(1, NQ) for h in range(H_IDX)]
        block = p.body.enter_context(nc.Block())

        @block.sync
        def _(sp):
            sp.dma_start(qi[:, :, :], hT[A_QI:A_QI + H_IDX * HD, 0:SEQ].rearrange("(h e) t -> e h t", e=HD)).then_inc(loaded, 16)
            sp.dma_start(ki[:, :], hT[A_KI:A_KI + HD, 0:SEQ]).then_inc(loaded, 16)
            for i in range(1, NQ):
                L = (i + 1) * P
                sp.wait_ge(summed, len(steps) + i)
                sp.dma_start(pscore[:, i - 1, 0:L], score[:, i - 1, (H_IDX - 1) % 2, 0:L]).then_inc(stored, 16)
            sp.wait_ge(stored, 16 * (NQ - 1))

        @block.tensor
        def _(pe):
            pe.wait_ge(loaded, 32)
            for n, (i, h) in enumerate(steps):
                if n >= 4:
                    pe.wait_ge(relu_done, n - 3)
                L = (i + 1) * P
                pe.matmul(dots[n % 4][:, 0:L], qi[:, h, i * P:(i + 1) * P], ki[:, 0:L], start=True, stop=True).then_inc(dot_done, 1)

        @block.scalar
        def _(act):
            for n, (i, h) in enumerate(steps):
                L = (i + 1) * P
                act.wait_ge(dot_done, n + 1)
                if n >= 3:
                    act.wait_ge(summed, n - 2)
                act.activation(relu[:, n % 3, 0:L], dots[n % 4][:, 0:L], ACT.Relu, scale=IDX_SCALE).then_inc(relu_done, 1)

        @block.vector
        def _(dve):
            for n, (i, h) in enumerate(steps):
                L = (i + 1) * P
                w = tok[:, i, TA_W + h:TA_W + h + 1]
                dve.wait_ge(relu_done, n + 1)
                if h:
                    dve.wait_ge(summed, n)
                    dve.scalar_tensor_tensor(out=score[:, i - 1, h % 2, 0:L], in0=relu[:, n % 3, 0:L], scalar=w,
                                             in1=score[:, i - 1, (h + 1) % 2, 0:L], op0=ALU.mult, op1=ALU.add).then_inc(summed, 1)
                else:
                    dve.tensor_scalar(score[:, i - 1, 0, 0:L], relu[:, n % 3, 0:L], w, None, ALU.mult).then_inc(summed, 1)
            dve.wait_ge(summed, len(steps))
            last = (H_IDX - 1) % 2
            for i in range(1, NQ):
                s = score[:, i - 1, last, i * P:(i + 1) * P]
                dve.tensor_tensor(s, s, keep.causal[:, :], ALU.add).then_inc(summed, 1)


def prompt_attention_phase(nc, name, branches, heads, hT, vec_up, tok, keep, tok_loads=(), sel_bias=None):
    with phase(nc, name) as p:
        kmax = max(b["kv"] for b in branches)
        parts = len(heads[0][2])
        per_head = NQ * parts
        added = branches[0]["gate"] is not None
        table = p.sb("table", [P, 2 * parts, 4, SEQ + P])
        kT = p.sb("kT", [HD, len(branches), kmax, SEQ])
        q = p.sb("q", [HD, 3, SEQ])
        shifted = p.sb("shifted", [P, 4, SEQ])
        probs = p.sb("probs", [P, 4, SEQ])
        pT = p.sb("pT", [P, 2, SEQ])
        nmax = p.sb("nmax", [P, 4])
        total = p.sb("total", [P, 4])
        weight = p.sb("weight", [P, 4])
        logit = [p.ps(f"logit{i}", [P, SEQ]) for i in range(4)]
        tps = [p.ps(f"tps{i}", [P, SEQ]) for i in range(2)]
        out = [p.ps(f"out{i}", [P, SEQ]) for i in range(2)]
        names = ("logit_ready", "shifted_ready", "probs_ready", "turned", "pT_ready0", "pT_ready1", "out_ready",
                 "weighed", "scaled", "mixed", "k_scaled")
        logit_ready, shifted_ready, probs_ready, turned, pT0, pT1, out_ready, weighed, scaled, mixed, k_scaled = (p.sem(n) for n in names)
        pT_ready = [pT0, pT1]
        k_in, v_in = p.sem("k_in"), p.sem("v_in")
        q_in = [p.sem(f"q_in{i}") for i in range(3)]
        t_in = [p.sem(f"table_in{i}") for i in range(2 * parts)]
        steps = [(n, i, part) for n in range(len(heads)) for i in range(NQ) for part in range(parts)]
        S = len(steps)
        block = p.body.enter_context(nc.Block())

        @block.sync
        def _(sp):
            for br, b in enumerate(branches):
                rows = hT[b["k"]:b["k"] + b["kv"] * HD, 0:SEQ].rearrange("(g e) t -> e g t", e=HD)
                sp.dma_start(kT[:, br, 0:b["kv"], :], rows).then_inc(k_in, 16)
            for n, (q_row, place, members) in enumerate(heads):
                if n == 1:
                    for dst, src in tok_loads:
                        sp.dma_start(dst, src).then_inc(v_in, 16)
                if n % 4 == 0:
                    g = n // 4
                    if g >= 2:
                        sp.wait_ge(shifted_ready, 4 * per_head * (g - 1))
                    for part, (br, h) in enumerate(members):
                        slot = (g % 2) * parts + part
                        head0 = (branches[br]["kind"] * N_HEADS + branches[br]["h0"] + h) * LU
                        sp.dma_start(table[:, slot, :, :], bass.AP(tensor=vec_up.tensor, offset=head0,
                                                                   ap=[[1, P], [LU, 4], [1, SEQ + P]])).then_inc(t_in[slot], 16)
                if n >= 3:
                    sp.wait_ge(logit_ready, per_head * (n - 2))
                sp.dma_start(q[:, n % 3, :], hT[q_row:q_row + HD, 0:SEQ]).then_inc(q_in[n % 3], 16)

        @block.tensor
        def _(pe):
            def scores(s):
                n, i, part = steps[s]
                br, h = heads[n][2][part]
                b = branches[br]
                L = (i + 1) * P
                if i == 0 and part == 0:
                    pe.wait_ge(q_in[n % 3], 16 * (n // 3 + 1))
                if i == 0 and h == 0:
                    pe.wait_ge(k_scaled, br + 1)
                if s >= 4:
                    pe.wait_ge(shifted_ready, s - 3)
                sel = b["sel"] and i > 0
                g = h // (b["heads"] // b["kv"])
                mm = pe.matmul(logit[s % 4][:, 0:L], q[:, n % 3, i * P:(i + 1) * P], kT[:, br, g, 0:L], start=True, stop=not sel)
                if sel:
                    mm = pe.matmul(logit[s % 4][:, 0:L], keep.ident_bf[:, :], sel_bias[:, i - 1, 0:L], start=False, stop=True)
                mm.then_inc(logit_ready, 1)

            def turn(s):
                i = steps[s][1]
                pe.wait_ge(scaled, s + 1)
                if s >= 2:
                    pe.wait_ge(pT_ready[s % 2], s // 2)
                for kt in range(i + 1):
                    last = pe.transpose(tps[s % 2][:, kt * P:(kt + 1) * P], probs[:, s % 4, kt * P:(kt + 1) * P], keep.ident[:, :])
                last.then_inc(turned, 1)

            def values(s):
                n, i, part = steps[s]
                br, h = heads[n][2][part]
                b = branches[br]
                g = h // (b["heads"] // b["kv"])
                half = heads[n][1] % 2
                if s == 0 and tok_loads:
                    pe.wait_ge(v_in, 16 * len(tok_loads))
                pe.wait_ge(pT_ready[s % 2], s // 2 + 1)
                if n >= 2 and i == 0 and part == 0:
                    pe.wait_ge(mixed, n - 1)
                for kt in range(i + 1):
                    v = tok[:, kt, b["v"] + g * HD:b["v"] + (g + 1) * HD]
                    last = pe.matmul(out[n % 2][half * HD:(half + 1) * HD, i * P:(i + 1) * P], v, pT[:, s % 2, kt * P:(kt + 1) * P],
                                     start=(part == 0 and kt == 0), stop=(part == parts - 1 and kt == i))
                last.then_inc(out_ready, 1)

            for s in range(S + 3):
                if s < S:
                    scores(s)
                if 2 <= s < S + 2:
                    turn(s - 2)
                if s >= 3:
                    values(s - 3)

        @block.scalar
        def _(act):
            for br, b in enumerate(branches):
                act.wait_ge(k_in, 16 * len(branches))
                act.mul(kT[:, br, 0:b["kv"], :], kT[:, br, 0:b["kv"], :], SCALE).then_inc(k_scaled, 1)

            def copy_turned(s):
                L = (steps[s][1] + 1) * P
                act.wait_ge(turned, s + 1)
                if s >= 2:
                    act.wait_ge(out_ready, s - 1)
                act.copy(pT[:, s % 2, 0:L], tps[s % 2][:, 0:L]).then_inc(pT_ready[s % 2], 1)

            for s in range(S + 2):
                if s < S:
                    L = (steps[s][1] + 1) * P
                    act.wait_ge(shifted_ready, s + 1)
                    if s >= 4:
                        act.wait_ge(turned, s - 3)
                        act.wait_ge(weighed, s - 3)
                    act.activation(probs[:, s % 4, 0:L], shifted[:, s % 4, 0:L], ACT.Exp, bias=nmax[:, s % 4:s % 4 + 1], scale=-1.0,
                                   accum_out=total[:, s % 4:s % 4 + 1]).then_inc(probs_ready, 1)
                if s >= 2 and s % 2 == 0:
                    copy_turned(s - 2)

        @block.vector
        def _(dve):
            def shift(s):
                n, i, part = steps[s]
                L = (i + 1) * P
                slot = (n // 4 % 2) * parts + part
                dve.wait_ge(logit_ready, s + 1)
                if n % 4 == 0 and i == 0:
                    dve.wait_ge(t_in[slot], 16 * (n // 8 + 1))
                if s >= 4:
                    dve.wait_ge(probs_ready, s - 3)
                row = table[:, slot, n % 4, 0:L]
                bias = bass.AP(tensor=row.tensor, offset=row.offset + L - 1, ap=[list(row.ap[0]), [-1, L]])
                dve.tensor_tensor_reduce(out=shifted[:, s % 4, 0:L], in0=logit[s % 4][:, 0:L], in1=bias, scale=-1.0, scalar=FLOOR,
                                         op0=ALU.add, op1=ALU.min, accum_out=nmax[:, s % 4:s % 4 + 1]).then_inc(shifted_ready, 1)

            def copy_turned(s):
                L = (steps[s][1] + 1) * P
                dve.wait_ge(turned, s + 1)
                if s >= 2:
                    dve.wait_ge(out_ready, s - 1)
                dve.tensor_copy(pT[:, s % 2, 0:L], tps[s % 2][:, 0:L]).then_inc(pT_ready[s % 2], 1)

            def weigh(s):
                n, i, part = steps[s]
                L = (i + 1) * P
                br, h = heads[n][2][part]
                gate = branches[br]["gate"]
                dve.wait_ge(probs_ready, s + 1)
                if s >= 4:
                    dve.wait_ge(scaled, s - 3)
                w, t = weight[:, s % 4:s % 4 + 1], total[:, s % 4:s % 4 + 1]
                e = probs[:, s % 4, 0:L]
                dve.reciprocal(w, t).then_inc(weighed, 1)
                dve.wait_ge(weighed, s + 1)
                if gate is None:
                    dve.tensor_scalar(e, e, w, None, ALU.mult).then_inc(scaled, 1)
                else:
                    dve.tensor_scalar(e, e, w, keep.gate_tok[:, i, gate + h:gate + h + 1], ALU.mult, ALU.mult).then_inc(scaled, 1)

            def mix_in(n):
                place = heads[n][1]
                rows = slice(place % 2 * HD, (place % 2 + 1) * HD)
                dst, src = keep.mixT[rows, place // 2, 0:SEQ], out[n % 2][rows, :]
                dve.wait_ge(out_ready, per_head * (n + 1))
                if added:
                    dve.tensor_tensor(dst, src, dst, ALU.add).then_inc(mixed, 1)
                else:
                    dve.tensor_copy(dst, src).then_inc(mixed, 1)

            for s in range(S + 5):
                if s < S:
                    shift(s)
                if 1 <= s <= S:
                    weigh(s - 1)
                if 2 <= s < S + 2 and s % 2 == 1:
                    copy_turned(s - 2)
                if s >= 5 and (s - 4) % per_head == 0:
                    mix_in((s - 4) // per_head - 1)


class SampleSelection:

    ROUNDS = DSA_TOP_SAMPLE // 8

    def __init__(self, p, score):
        self.score = score
        self.best = p.sb("best", [TS, 2, 8])
        self.picked, self.marked = p.sem("picked"), p.sem("marked")

    def round(self, dve, r):
        score, best = self.score, self.best[:, r % 2, :]
        if r:
            dve.wait_ge(self.marked, r)
        dve.max(best, score[:, :]).then_inc(self.picked, 1)
        dve.wait_ge(self.picked, r + 1)
        dve.match_replace(out=score[:, :], in_to_replace=best, in_values=score[:, :], imm_value=TAKEN).then_inc(self.marked, 1)


def mask_from_marks(dve, score, sel_mask, masked):
    dve.tensor_scalar(sel_mask[:, 0:PAST].rearrange("r (j c) -> r j c", j=STRIDE),
                      score[:, 0:PAST].rearrange("r (c j) -> r j c", j=STRIDE), TAKEN / 2, NEG, ALU.is_gt, ALU.mult).then_inc(masked, 1)
    dve.tensor_scalar(sel_mask[:, PAST:LS], score[:, PAST:LS], TAKEN / 2, NEG, ALU.is_gt, ALU.mult).then_inc(masked, 1)


def sample_indexer_phase(nc, hT, cache_kidx, io, score, keep):
    rows_in_cache = cache_kidx.rearrange("n (c j) e -> (n c) (j e)", j=STRIDE)
    with phase(nc, "sidx") as p:
        kidx = p.sb("kidx", [P, NB, STRIDE * HD])
        kT = p.sb("kT", [P, 2, NCH * 8])
        relu = p.sb("relu", [P, 2, NCH * 8])
        part = p.sb("part", [16, 2, NCH * 8])
        q = p.sb("q", [HD, H_IDX, TS])
        q_blk = p.sb("q_blk", [P, NB, P])
        k_new = p.sb("k_new", [HD, TS])
        w_col = p.sb("w_col", [P, NB])
        w_sel = p.sb("w_sel", [P, NB, 16])
        relu_new = p.sb("relu_new", [TS, NB, NS])
        new_part = p.sb("new_part", [NS, NB, NS])
        raw = p.sb("raw", [TS, LS])
        tps = [p.ps(f"tps{i}", [P, 512]) for i in range(2)]
        dots = [p.ps(f"dots{i}", [P, 512]) for i in range(2)]
        sums = [p.ps(f"sums{i}", [P, 512]) for i in range(2)]
        dots_new = p.ps("dots_new", [P, 512])
        sums_new = p.ps("sums_new", [P, 512])
        (loaded, zeroed, built, turned, kT_ready, dot_done, relu_done, sum_done, part_done, new_dots, new_relu, new_sums,
         new_out, stored, natural) = (p.sem(n) for n in (
             "loaded", "zeroed", "built", "turned", "kT_ready", "dot_done", "relu_done", "sum_done", "part_done", "new_dots",
             "new_relu", "new_sums", "new_out", "stored", "natural"))
        kidx_in = keep.kidx_in
        parts_out = [p.sem(f"parts_out{i}") for i in range(2)]
        halves = [(b, f) for b in range(NB) for f in range(2)]
        block = p.body.enter_context(nc.Block())

        def load_weights(e, j2, h):
            r = j2 * TS + h * NS
            e.dma_start(w_col[r:r + NS, :], hT[A_W + h, SEQ:T].rearrange("(b q) -> q b", q=NS)).then_inc(loaded, 16)

        @block.gpsimd
        def _(pool):
            for b in range(NB):
                pool.indirect_dma_start(out=kidx[:, b, :], out_offset=None, in_=rows_in_cache,
                                        in_offset=bass.IndirectOffsetOnAxis(ap=keep.chunk_row[:, b:b + 1], axis=0)).then_inc(kidx_in[b], 16)

        @block.sync
        def _(sp):
            sp.dma_start(q[:, :, :], hT[A_QI:A_QI + H_IDX * HD, SEQ:T].rearrange("(h e) t -> e h t", e=HD)).then_inc(loaded, 16)
            sp.dma_start(k_new[:, :], hT[A_KI:A_KI + HD, SEQ:T]).then_inc(loaded, 16)
            with nc.allow_non_contiguous_dma(reason="indexer weights, one per partition"):
                for j2 in range(2):
                    for h in range(H_IDX // 2):
                        load_weights(sp, j2, h)
            sp.wait_ge(new_out, 1)
            for b in range(NB):
                sp.dma_start(raw[b * NS:(b + 1) * NS, PAST:LS], new_part[:, b, :]).then_inc(stored, 16)
            for b in range(NB):
                sp.wait_ge(part_done, 2 * (b + 1))
                for j2 in range(2):
                    sp.dma_start(raw[b * NS:(b + 1) * NS, j2 * 1024:(j2 + 1) * 1024],
                                 part[j2 * NS:(j2 + 1) * NS, b % 2, :]).then_inc(parts_out[b % 2], 16)
            sp.wait_ge(keep.pending, keep.pending_count)

        @block.tensor
        def _(pe):
            pe.wait_ge(built, 3)
            for b in range(NB):
                pe.matmul(dots_new[0:TS, b * NS:(b + 1) * NS], q_blk[0:HD, b, 0:TS], k_new[:, b * NS:(b + 1) * NS],
                          start=True, stop=True).then_inc(new_dots, 1)
            pe.wait_ge(new_relu, 1)
            for b in range(NB):
                pe.matmul(sums_new[0:NS, b * NS:(b + 1) * NS], w_sel[0:TS, b, 0:NS], relu_new[:, b, :], start=True, stop=True).then_inc(new_sums, 1)

            def turn(n):
                b, f = halves[n]
                if f == 0:
                    pe.wait_ge(kidx_in[b], 16)
                if n >= 2:
                    pe.wait_ge(kT_ready, n - 1)
                for m in range(4):
                    j = 2 * (4 * f + m)
                    last = pe.transpose(tps[n % 2][:, m * P:(m + 1) * P], kidx[:, b, j * HD:(j + 2) * HD], keep.ident[:, :])
                last.then_inc(turned, 1)

            def dot(n):
                b, f = halves[n]
                pe.wait_ge(kT_ready, n + 1)
                if n >= 2:
                    pe.wait_ge(relu_done, n - 1)
                pe.matmul(dots[n % 2][:, :], q_blk[:, b, :], kT[:, b % 2, f * 512:(f + 1) * 512], start=True, stop=True).then_inc(dot_done, 1)

            def head_sum(n):
                b, f = halves[n]
                pe.wait_ge(relu_done, n + 1)
                if n >= 2:
                    pe.wait_ge(part_done, n - 1)
                pe.matmul(sums[n % 2][0:16, :], w_sel[:, b, :], relu[:, b % 2, f * 512:(f + 1) * 512], start=True, stop=True).then_inc(sum_done, 1)

            N = len(halves)
            for n in range(N + 2):
                if n < N:
                    turn(n)
                if 1 <= n <= N:
                    dot(n - 1)
                if n >= 2:
                    head_sum(n - 2)

        @block.scalar
        def _(act):
            with nc.allow_non_contiguous_dma(reason="indexer weights, one per partition"):
                for j2 in range(2):
                    for h in range(H_IDX // 2, H_IDX):
                        load_weights(act, j2, h)
            act.wait_ge(new_dots, NB)
            act.activation(relu_new[:, :, :], dots_new[0:TS, 0:TS].rearrange("p (b t) -> p b t", b=NB), ACT.Relu, scale=IDX_SCALE).then_inc(new_relu, 1)
            for n, (b, f) in enumerate(halves):
                act.wait_ge(dot_done, n + 1)
                if n >= 4:
                    act.wait_ge(sum_done, n - 3)
                act.activation(relu[:, b % 2, f * 512:(f + 1) * 512], dots[n % 2][:, :], ACT.Relu, scale=IDX_SCALE).then_inc(relu_done, 1)

        @block.vector
        def _(dve):
            dve.memset(q_blk[:, :, :], 0.0).then_inc(zeroed, 1)
            dve.wait_ge(zeroed, 1)
            dve.wait_ge(loaded, 16 * (2 + 2 * H_IDX))
            src = q[:, :, :].rearrange("e h (b q) -> e b h q", q=NS)
            for j2 in range(2):
                dst = q_blk[j2 * HD:(j2 + 1) * HD, :, j2 * TS:(j2 + 1) * TS].rearrange("e b (h q) -> e b h q", q=NS)
                dve.tensor_copy(dst, src).then_inc(built, 1)
            for b in range(NB):
                last = dve.tensor_scalar(w_sel[:, b, :], keep.same_token[:, :], w_col[:, b:b + 1], None, ALU.mult)
            last.then_inc(built, 1)
            dve.wait_ge(new_sums, NB)
            dve.tensor_copy(new_part[:, :, :], sums_new[0:NS, 0:TS].rearrange("p (b t) -> p b t", b=NB)).then_inc(new_out, 1)
            N = len(halves)
            for n in range(N + 2):
                if n < N:
                    b, f = halves[n]
                    dve.wait_ge(turned, n + 1)
                    if n >= 4:
                        dve.wait_ge(dot_done, n - 3)
                    dve.tensor_copy(kT[:, b % 2, f * 512:(f + 1) * 512], tps[n % 2][:, :]).then_inc(kT_ready, 1)
                if n >= 2:
                    b, f = halves[n - 2]
                    dve.wait_ge(sum_done, n - 1)
                    if b >= 2:
                        dve.wait_ge(parts_out[b % 2], 32 * (b // 2))
                    dve.tensor_copy(part[:, b % 2, f * 512:(f + 1) * 512], sums[n % 2][0:16, :]).then_inc(part_done, 1)
            for i in range(2):
                dve.wait_ge(parts_out[i], 32 * NB // 2)
            dve.wait_ge(stored, 16 * NB)
            dve.tensor_copy(score[:, 0:PAST].rearrange("r (c m s) -> r s m c", s=2, m=8),
                            raw[:, 0:PAST].rearrange("r (s m c) -> r s m c", s=2, m=8)).then_inc(natural, 1)
            dve.tensor_tensor(score[:, PAST:LS], raw[:, PAST:LS], keep.new_causal[0:TS, :], ALU.add).then_inc(natural, 1)


def query_blocks(dve, dst, src, groups, heads_per_group, done):
    for g in range(groups):
        h0, n = g * heads_per_group, heads_per_group
        out = dst[g * HD:(g + 1) * HD, :, h0 * NS:(h0 + n) * NS].rearrange("e b (h q) -> e b h q", q=NS)
        dve.tensor_scalar(out, src[:, h0:h0 + n, :].rearrange("e h (b q) -> e b h q", q=NS), SCALE, None, ALU.mult).then_inc(done, 1)


def sample_table(sp, dst, vec, kind, h0, heads, lo, n, done):
    for q in range(NS):
        first = (kind * N_HEADS + h0) * LV + FAR - PAST - q + lo
        sp.dma_start(dst[q:(heads - 1) * NS + q + 1:NS, :], bass.AP(tensor=vec.tensor, offset=first, ap=[[LV, heads], [1, n]])).then_inc(done, 16)


def sample_a_phase(nc, hT, vec, cache_kv, new_kv, io, score, pscore, sel_bias, keep):
    rows_in_cache = cache_kv.rearrange("n (c j) s g e -> (n c) (j s g e)", j=STRIDE)
    R = H_A * NS
    with phase(nc, "sa") as p:
        kv = p.sb("kv", [P, 3, STRIDE * 256])
        sel_mask = p.sb("sel_mask", [TS, LS], BF16)
        masked = p.sem("masked")
        kT = p.sb("kT", [P, 2, LS])
        k_new = p.sb("k_new", [P, TS])
        v_new = p.sb("v_new", [NS, NB, P])
        q = p.sb("q", [HD, H_A, TS])
        q_blk = p.sb("q_blk", [P, NB, R])
        nat = p.sb("nat", [R, LS])
        table = p.sb("table", [R, LS])
        pick = p.sb("pick", [TS, NB, R], BF16)
        shifted = p.sb("shifted", [R, LS])
        probs = p.sb("probs", [R, LS])
        pT = p.sb("pT", [P, STRIDE + 1, R])
        o = p.sb("o", [R, 2, HD])
        nmax = p.sb("nmax", [R, 2])
        total = p.sb("total", [R, 2])
        rinv = p.sb("rinv", [R, 2])
        logit = p.ps("logit", [P, 5 * 512])
        tps = [p.ps(f"tps{i}", [P, 512]) for i in range(2)]
        outp = p.ps("outp", [P, 512])
        (loaded, t_in, zeroed, built, tabled, turned_k, kT_ready, kT_new, logit_ready, shifted_ready, probs_ready, turned_p,
         pT_ready, out_ready, weighed, o_ready, o_turned, mixed) = (p.sem(n) for n in (
             "loaded", "t_in", "zeroed", "built", "tabled", "turned_k", "kT_ready", "kT_new", "logit_ready", "shifted_ready",
             "probs_ready", "turned_p", "pT_ready", "out_ready", "weighed", "o_ready", "o_turned", "mixed"))
        kv_in = keep.a_kv_in
        selection = PromptSelection(p, pscore, sel_bias)
        third = (NQ - 1) * selection.ROUNDS // NB // 3

        def select(dve, b, part):
            for r in range(part * third, (part + 1) * third):
                selection.round(dve, 3 * third * b + r)

        block = p.body.enter_context(nc.Block())

        @block.gpsimd
        def _(pool):
            for b in range(NB):
                if b == 1:
                    pool.wait_ge(t_in, 16 * NS)
                if b >= 3:
                    pool.wait_ge(out_ready, b - 2)
                pool.indirect_dma_start(out=kv[:, b % 3, :], out_offset=None, in_=rows_in_cache,
                                        in_offset=bass.IndirectOffsetOnAxis(ap=keep.chunk_row[:, b:b + 1], axis=0)).then_inc(kv_in[b % 3], 16)

        @block.sync
        def _(sp):
            sp.dma_start(q[:, :, :], hT[A_Q:A_Q + H_A * HD, SEQ:T].rearrange("(h e) t -> e h t", e=HD)).then_inc(loaded, 16)
            sp.dma_start(k_new[:, :], hT[A_K:A_K + P, SEQ:T]).then_inc(loaded, 16)
            sp.dma_start(v_new[:, :, :], new_kv[:, :, P:2 * P].rearrange("b q c -> q b c")).then_inc(loaded, 16)
            sample_table(sp, nat, vec, KIND_FULL, 0, H_A, 0, LS, t_in)
            selection.load(sp)

        @block.tensor
        def _(pe):
            def keys(b):
                pe.wait_ge(kv_in[b % 3], 16 * (b // 3 + 1))
                for m in range(4):
                    n = 4 * b + m
                    if n >= 2:
                        pe.wait_ge(kT_ready, n - 1)
                    if m < 2 and b >= 2:
                        pe.wait_ge(pT_ready, 3 * (b - 1))
                    for i in range(4):
                        j = 4 * m + i
                        last = pe.transpose(tps[n % 2][:, i * P:(i + 1) * P], kv[:, b % 3, j * 256:j * 256 + P], keep.ident[:, :])
                    last.then_inc(turned_k, 1)

            def scores(b):
                if b == 0:
                    pe.wait_ge(built, 3)
                    pe.wait_ge(masked, 2)
                pe.wait_ge(kT_ready, 4 * b + 4)
                pe.wait_ge(kT_new, b + 1)
                if b:
                    pe.wait_ge(shifted_ready, b)
                for c in range(0, LS, 512):
                    w = min(512, LS - c)
                    pe.matmul(logit[0:R, c:c + w], q_blk[:, b, :], kT[:, b % 2, c:c + w], start=True, stop=False)
                    last = pe.matmul(logit[0:R, c:c + w], pick[:, b, :], sel_mask[:, c:c + w], start=False, stop=True)
                last.then_inc(logit_ready, 1)

            def turn(b):
                pe.wait_ge(probs_ready, b + 1)
                for m in range(3):
                    if m == 0:
                        pe.wait_ge(kT_ready, min(4 * b + 8, 4 * NB))
                    if m == 2:
                        pe.wait_ge(pT_ready, 3 * b + 1)
                    n = 8 if m < 2 else 1
                    for i in range(n):
                        j = 8 * m + i
                        w = P if m < 2 else NS
                        last = pe.transpose(tps[m % 2][0:w, i * R:(i + 1) * R], probs[:, j * P:j * P + w], keep.ident[0:R, 0:R])
                    last.then_inc(turned_p, 1)

            def values(b):
                pe.wait_ge(pT_ready, 3 * b + 3)
                if b:
                    pe.wait_ge(mixed, 2 * b)
                for j in range(STRIDE):
                    pe.matmul(outp[0:R, 0:P], pT[:, j, :], kv[:, b % 3, j * 256 + P:(j + 1) * 256], start=(j == 0), stop=False)
                pe.matmul(outp[0:R, 0:P], pT[0:NS, STRIDE, :], v_new[:, b, :], start=False, stop=True).then_inc(out_ready, 1)

            def turn_out(b):
                pe.wait_ge(o_ready, 2 * b + 2)
                pe.transpose(outp[0:HD, 256:256 + R], o[:, b % 2, :], keep.ident[0:R, 0:R]).then_inc(o_turned, 1)

            keys(0)
            for b in range(NB):
                scores(b)
                if b:
                    turn_out(b - 1)
                if b + 1 < NB:
                    keys(b + 1)
                turn(b)
                values(b)
            turn_out(NB - 1)

        @block.scalar
        def _(act):
            def copy_keys(b):
                if b >= 2:
                    act.wait_ge(logit_ready, b - 1)
                for m in range(4):
                    act.wait_ge(turned_k, 4 * b + m + 1)
                    act.copy(kT[:, b % 2, m * 512:(m + 1) * 512], tps[m % 2][:, :]).then_inc(kT_ready, 1)
                if b == 0:
                    act.wait_ge(loaded, 48)
                act.copy(kT[:, b % 2, PAST:LS], k_new[:, b * NS:(b + 1) * NS]).then_inc(kT_new, 1)

            copy_keys(0)
            for b in range(NB):
                if b + 1 < NB:
                    copy_keys(b + 1)
                act.wait_ge(shifted_ready, b + 1)
                if b:
                    act.wait_ge(turned_p, 3 * b)
                if b >= 2:
                    act.wait_ge(weighed, b - 1)
                act.activation(probs[:, :], shifted[:, :], ACT.Exp, bias=nmax[:, b % 2:b % 2 + 1], scale=-1.0,
                               accum_out=total[:, b % 2:b % 2 + 1]).then_inc(probs_ready, 1)

        @block.vector
        def _(dve):
            mask_from_marks(dve, score, sel_mask, masked)
            dve.memset(q_blk[:, :, :], 0.0).then_inc(zeroed, 1)
            dve.wait_ge(zeroed, 1)
            dve.wait_ge(loaded, 48)
            query_blocks(dve, q_blk, q, 2, H_A // 2, built)
            dve.tensor_copy(pick[:, :, :], keep.pick_row[:, :, :]).then_inc(built, 1)
            dve.wait_ge(t_in, 16 * NS)
            dve.tensor_copy(table[:, 0:PAST].rearrange("r (j c) -> r c j", j=STRIDE),
                            nat[:, 0:PAST].rearrange("r (c j) -> r c j", j=STRIDE)).then_inc(tabled, 1)
            dve.tensor_copy(table[:, PAST:LS], nat[:, PAST:LS]).then_inc(tabled, 1)
            dve.wait_ge(tabled, 2)

            def mix_in(b):
                dve.wait_ge(o_turned, b + 1)
                src = outp[0:HD, 256:256 + R].rearrange("e (h two q) -> e h two q", two=2, q=NS)
                for odd in range(2):
                    dve.tensor_copy(keep.mixT[odd * HD:(odd + 1) * HD, 0:4, SEQ + b * NS:SEQ + (b + 1) * NS], src[:, :, odd, :]).then_inc(mixed, 1)

            for b in range(NB):
                dve.wait_ge(logit_ready, b + 1)
                if b:
                    dve.wait_ge(probs_ready, b)
                dve.tensor_tensor_reduce(out=shifted[:, :], in0=logit[0:R, 0:LS], in1=table[:, :], scale=-1.0, scalar=FLOOR,
                                         op0=ALU.add, op1=ALU.min, accum_out=nmax[:, b % 2:b % 2 + 1]).then_inc(shifted_ready, 1)
                if b:
                    mix_in(b - 1)
                select(dve, b, 0)
                for m in range(3):
                    dve.wait_ge(turned_p, 3 * b + m + 1)
                    if b:
                        dve.wait_ge(out_ready, b)
                    if m < 2:
                        dve.tensor_copy(pT[:, 8 * m:8 * m + 8, :], tps[m % 2][:, :].rearrange("p (j r) -> p j r", r=R)).then_inc(pT_ready, 1)
                    else:
                        dve.tensor_copy(pT[0:NS, STRIDE, :], tps[0][0:NS, 0:R]).then_inc(pT_ready, 1)
                dve.reciprocal(rinv[:, b % 2:b % 2 + 1], total[:, b % 2:b % 2 + 1]).then_inc(weighed, 1)
                select(dve, b, 1)
                dve.wait_ge(weighed, b + 1)
                dve.wait_ge(out_ready, b + 1)
                if b >= 2:
                    dve.wait_ge(o_turned, b - 1)
                for g in range(2):
                    r = slice(g * 32, (g + 1) * 32)
                    dve.tensor_scalar(o[r, b % 2, :], outp[r, g * HD:(g + 1) * HD], rinv[r, b % 2:b % 2 + 1], None, ALU.mult).then_inc(o_ready, 1)
                select(dve, b, 2)
            mix_in(NB - 1)


def sample_b_phase(nc, hT, vec, state, new_kv, io, score, keep):
    R = H_B * NS
    NT_K = 10
    L = NT_K * P + NS
    with phase(nc, "sb") as p:
        k = p.sb("k", [P, 2, NT_K, 512])
        v = p.sb("v", [P, 2, NT_K, 512])
        kT = p.sb("kT", [P, 4, L])
        k_new = p.sb("k_new", [P, 4, TS])
        v_new = p.sb("v_new", [NS, 2, 512])
        q = p.sb("q", [HD, H_B, TS])
        q_blk = p.sb("q_blk", [P, NB, 4, R])
        nat = p.sb("nat", [R, LS])
        table = p.sb("table", [R, L])
        shifted = p.sb("shifted", [R, L])
        probs = shifted
        pT = p.sb("pT", [P, NT_K + 1, R])
        o = p.sb("o", [R, 512])
        nmax = p.sb("nmax", [R, 2])
        total = p.sb("total", [R, 2])
        rinv = p.sb("rinv", [R, 2])
        logit = p.ps("logit", [P, 3 * 512])
        tps = [p.ps(f"tps{i}", [P, 512]) for i in range(2)]
        tpp = [p.ps(f"tpp{i}", [P, 512]) for i in range(2)]
        outp = p.ps("outp", [P, 512])
        (loaded, t_in, zeroed, built, tabled, turned_k, kT_even, kT_odd, kT_new, logit_ready, shifted_ready, probs_ready, weighed,
         scaled, turned_p, pT_ready, out_ready, o_turned, mixed) = (p.sem(n) for n in (
             "loaded", "t_in", "zeroed", "built", "tabled", "turned_k", "kT_even", "kT_odd", "kT_new", "logit_ready",
             "shifted_ready", "probs_ready", "weighed", "scaled", "turned_p", "pT_ready", "out_ready", "o_turned", "mixed"))
        kT_ready = [kT_even, kT_odd]
        k_in = [p.sem(f"k_in{i}") for i in range(2)]
        v_in = [p.sem(f"v_in{i}") for i in range(2)]
        selection = SampleSelection(p, score)

        def select(dve, b, part):
            each = selection.ROUNDS // (2 * NB)
            for r in range(each):
                selection.round(dve, (2 * b + part) * each + r)

        block = p.body.enter_context(nc.Block())

        def load(sp, dst, b, col, done):
            chunks = state[b].rearrange("(g r) c -> g r c", r=STRIDE)
            sp.dma_start(dst[:, b % 2, 0:8, :], chunks[:, 0:8, col:col + 512]).then_inc(done, 16)
            late = bass.AP(tensor=state.tensor, offset=(b * PAST + 96 * STRIDE + 8) * D + col,
                           ap=[[STRIDE * D, 32], [2 * D, 4], [D, 2], [1, 512]])
            sp.dma_start(dst[:, b % 2, 8:10, :], late).then_inc(done, 16)

        @block.sync
        def _(sp):
            sp.dma_start(q[:, :, :], hT[B_Q:B_Q + H_B * HD, SEQ:T].rearrange("(h e) t -> e h t", e=HD)).then_inc(loaded, 16)
            sp.dma_start(k_new[:, :, :], hT[B_K:B_K + 4 * P, SEQ:T].rearrange("(m e) t -> e m t", e=P)).then_inc(loaded, 16)
            for b in range(NB):
                if b >= 2:
                    sp.wait_ge(turned_k, NT_K * (b - 1))
                load(sp, k, b, 0, k_in[b % 2])
                if b == 0:
                    sample_table(sp, nat, vec, KIND_DIL, 8, H_B, 0, LS, t_in)
                if b >= 2:
                    sp.wait_ge(out_ready, b - 1)
                load(sp, v, b, 512, v_in[b % 2])
                sp.dma_start(v_new[:, b % 2, :], new_kv[b, :, 512:1024]).then_inc(v_in[b % 2], 16)

        @block.tensor
        def _(pe):
            def keys(b):
                pe.wait_ge(k_in[b % 2], 32 * (b // 2 + 1))
                for t in range(NT_K):
                    n = NT_K * b + t
                    if n >= 2:
                        pe.wait_ge(kT_ready[n % 2], n // 2)
                    for m in range(4):
                        last = pe.transpose(tps[n % 2][:, m * P:(m + 1) * P], k[:, b % 2, t, m * P:(m + 1) * P], keep.ident[:, :])
                    last.then_inc(turned_k, 1)

            def scores(b):
                if b == 0:
                    pe.wait_ge(built, 8)
                for i in range(2):
                    pe.wait_ge(kT_ready[i], NT_K // 2 * (b + 1))
                pe.wait_ge(kT_new, b + 1)
                if b:
                    pe.wait_ge(shifted_ready, b)
                for c in range(0, L, 512):
                    w = min(512, L - c)
                    for m in range(4):
                        last = pe.matmul(logit[0:R, c:c + w], q_blk[:, b, m, :], kT[:, m, c:c + w], start=(m == 0), stop=(m == 3))
                last.then_inc(logit_ready, 1)

            def turn(b):
                pe.wait_ge(probs_ready, b + 1)
                if b:
                    pe.wait_ge(pT_ready, 3 * b)
                    pe.wait_ge(mixed, 2 * b)
                for t in range(NT_K + 1):
                    w = P if t < NT_K else NS
                    last = pe.transpose(tpp[t // 8][0:w, (t % 8) * R:(t % 8 + 1) * R], probs[:, t * P:t * P + w], keep.ident[0:R, 0:R])
                last.then_inc(turned_p, 1)

            def values(b):
                pe.wait_ge(pT_ready, 3 * b + 3)
                pe.wait_ge(v_in[b % 2], 48 * (b // 2 + 1))
                if b:
                    pe.wait_ge(scaled, b)
                for t in range(NT_K):
                    pe.matmul(outp[0:R, :], pT[:, t, :], v[:, b % 2, t, :], start=(t == 0), stop=False)
                pe.matmul(outp[0:R, :], pT[0:NS, NT_K, :], v_new[:, b % 2, :], start=False, stop=True).then_inc(out_ready, 1)

            def turn_out(b):
                pe.wait_ge(scaled, b + 1)
                for m in range(4):
                    last = pe.transpose(tpp[1][:, 256 + m * R:256 + (m + 1) * R], o[:, m * P:(m + 1) * P], keep.ident[0:R, 0:R])
                last.then_inc(o_turned, 1)

            keys(0)
            for b in range(NB):
                scores(b)
                if b:
                    turn_out(b - 1)
                if b + 1 < NB:
                    keys(b + 1)
                turn(b)
                values(b)
            turn_out(NB - 1)

        def copy_key_tile(eng, copy, b, t):
            n = NT_K * b + t
            eng.wait_ge(turned_k, n + 1)
            if b:
                eng.wait_ge(logit_ready, b)
            copy(kT[:, :, t * P:(t + 1) * P], tps[n % 2][:, :].rearrange("p (m c) -> p m c", m=4)).then_inc(kT_ready[n % 2], 1)

        @block.scalar
        def _(act):
            act.wait_ge(loaded, 32)

            def copy_keys(b):
                for t in range(0, NT_K, 2):
                    copy_key_tile(act, act.copy, b, t)
                act.copy(kT[:, :, NT_K * P:L], k_new[:, :, b * NS:(b + 1) * NS]).then_inc(kT_new, 1)

            copy_keys(0)
            for b in range(NB):
                if b + 1 < NB:
                    copy_keys(b + 1)
                act.wait_ge(shifted_ready, b + 1)
                if b:
                    act.wait_ge(turned_p, b)
                if b >= 2:
                    act.wait_ge(weighed, b - 1)
                act.activation(probs[:, :], shifted[:, :], ACT.Exp, bias=nmax[:, b % 2:b % 2 + 1], scale=-1.0,
                               accum_out=total[:, b % 2:b % 2 + 1]).then_inc(probs_ready, 1)

        @block.vector
        def _(dve):
            select(dve, 0, 0)
            dve.memset(q_blk[:, :, :, :], 0.0).then_inc(zeroed, 1)
            dve.wait_ge(zeroed, 1)
            dve.wait_ge(loaded, 32)
            for h in range(H_B):
                dst = q_blk[(h % 2) * HD:(h % 2 + 1) * HD, :, h // 2, h * NS:(h + 1) * NS]
                dve.tensor_scalar(dst, q[:, h, :].rearrange("e (b q) -> e b q", q=NS), SCALE, None, ALU.mult).then_inc(built, 1)
            dve.wait_ge(t_in, 16 * NS)
            dve.tensor_copy(table[:, 0:8 * P].rearrange("r (t g) -> r t g", t=8),
                            nat[:, 0:PAST].rearrange("r (g t) -> r t g", t=STRIDE)[:, 0:8, :]).then_inc(tabled, 1)
            for t in range(2):
                dst = table[:, (8 + t) * P:(9 + t) * P].rearrange("r (g s) -> r g s", s=4)
                src = nat[:, 96 * STRIDE:PAST].rearrange("r (g h s t) -> r t h g s", h=2, s=4, t=2)[:, t, 1, :, :]
                dve.tensor_copy(dst, src).then_inc(tabled, 1)
            dve.tensor_copy(table[:, NT_K * P:L], nat[:, PAST:LS]).then_inc(tabled, 1)
            dve.wait_ge(tabled, 4)

            def copy_keys(b):
                for t in range(1, NT_K, 2):
                    copy_key_tile(dve, dve.tensor_copy, b, t)

            def mix_in(b):
                dve.wait_ge(o_turned, b + 1)
                for odd in range(2):
                    r = slice(odd * HD, (odd + 1) * HD)
                    first = tpp[1][r, 256 + odd * NS:512]
                    src = bass.AP(tensor=first.tensor, offset=first.offset, ap=[list(first.ap[0]), [R + 2 * NS, 4], [1, NS]])
                    dve.tensor_copy(keep.mixT[r, 4:8, SEQ + b * NS:SEQ + (b + 1) * NS], src).then_inc(mixed, 1)

            copy_keys(0)
            for b in range(NB):
                dve.wait_ge(logit_ready, b + 1)
                if b:
                    dve.wait_ge(probs_ready, b)
                dve.tensor_tensor_reduce(out=shifted[:, :], in0=logit[0:R, 0:L], in1=table[:, :], scale=-1.0, scalar=FLOOR,
                                         op0=ALU.add, op1=ALU.min, accum_out=nmax[:, b % 2:b % 2 + 1]).then_inc(shifted_ready, 1)
                if b:
                    mix_in(b - 1)
                if b + 1 < NB:
                    copy_keys(b + 1)
                dve.wait_ge(turned_p, b + 1)
                if b:
                    dve.wait_ge(out_ready, b)
                dve.tensor_copy(pT[:, 0:8, :], tpp[0][:, :].rearrange("p (t r) -> p t r", r=R)).then_inc(pT_ready, 1)
                dve.tensor_copy(pT[:, 8:10, :], tpp[1][:, 0:2 * R].rearrange("p (t r) -> p t r", r=R)).then_inc(pT_ready, 1)
                dve.tensor_copy(pT[0:NS, NT_K, :], tpp[1][0:NS, 2 * R:3 * R]).then_inc(pT_ready, 1)
                dve.wait_ge(probs_ready, b + 1)
                dve.reciprocal(rinv[:, b % 2:b % 2 + 1], total[:, b % 2:b % 2 + 1]).then_inc(weighed, 1)
                select(dve, b, 1)
                dve.wait_ge(weighed, b + 1)
                dve.wait_ge(out_ready, b + 1)
                if b:
                    dve.wait_ge(o_turned, b)
                dve.tensor_scalar(o[:, :], outp[0:R, :], rinv[:, b % 2:b % 2 + 1], None, ALU.mult).then_inc(scaled, 1)
                if b + 1 < NB:
                    select(dve, b + 1, 0)
            mix_in(NB - 1)


class Norm:

    def __init__(self, p, keep):
        self.keep = keep
        self.stats = p.sb("stats", [P, NT, 2, 6])
        self.mv = p.sb("mv", [P, NT, 2])
        self.rstd = p.sb("rstd", [P, NT])
        self.shift = p.sb("shift", [P, NT])
        self.g = p.sb("g", [P, D])
        self.b = p.sb("b", [P, D])
        self.params_in = p.sem("params_in")
        self.stat, self.aggr, self.root, self.inv, self.shifted, self.scaled, self.gained, self.normed_left, self.normed_right = (
            p.sem(n) for n in ("stat", "aggr", "root", "inv", "shifted", "scaled", "gained", "normed_left", "normed_right"))
        self.turned, self.high, self.low = p.sem("x_turned"), p.sem("x_high"), p.sem("x_low")

    def load(self, sp, g, b):
        for dst, src in ((self.g, g), (self.b, b)):
            sp.dma_start(dst[:, :], src[None, :].to_broadcast([P, D])).then_inc(self.params_in, 16)

    def statistics(self, dve, t, h):
        w = TILES[t][1]
        dve.bn_stats(out=self.stats[0:w, t, h, :], in_=self.keep.xtok[0:w, t, h * 512:(h + 1) * 512]).then_inc(self.stat, 1)

    def aggregate(self, dve, t, stats_done):
        w = TILES[t][1]
        dve.wait_ge(self.stat, stats_done)
        dve.bn_aggr(out=self.mv[0:w, t, :], in_=self.stats[0:w, t, :, :]).then_inc(self.aggr, 1)

    def factors(self, dve, t):
        w = TILES[t][1]
        r = self.rstd[0:w, t:t + 1]
        dve.wait_ge(self.root, t + 1)
        dve.reciprocal(r, r).then_inc(self.inv, 1)
        dve.wait_ge(self.inv, t + 1)
        dve.scalar_tensor_tensor(out=self.shift[0:w, t:t + 1], in0=self.mv[0:w, t, 0:1], scalar=-1.0, in1=r,
                                 op0=ALU.mult, op1=ALU.mult).then_inc(self.shifted, 1)

    def gain(self, dve, t):
        w = TILES[t][1]
        x = self.keep.xtok[0:w, t, :]
        dve.wait_ge(self.params_in, 32)
        dve.wait_ge(self.scaled, t + 1)
        dve.tensor_tensor(x, x, self.g[0:w, :], ALU.mult).then_inc(self.gained, 1)
        dve.wait_ge(self.gained, t + 1)
        dve.tensor_tensor(x[:, 0:640], x[:, 0:640], self.b[0:w, 0:640], ALU.add).then_inc(self.normed_left, 1)

    def root_of(self, act, t):
        w = TILES[t][1]
        act.wait_ge(self.aggr, t + 1)
        act.activation(self.rstd[0:w, t:t + 1], self.mv[0:w, t, 1:2], ACT.Sqrt, bias=self.keep.eps[0:w, :]).then_inc(self.root, 1)

    def scale(self, act, t):
        w = TILES[t][1]
        x = self.keep.xtok[0:w, t, :]
        act.wait_ge(self.shifted, t + 1)
        act.activation(x, x, ACT.Identity, scale=self.rstd[0:w, t:t + 1], bias=self.shift[0:w, t:t + 1]).then_inc(self.scaled, 1)

    def bias(self, pool):
        for t in range(NT):
            w = TILES[t][1]
            x = self.keep.xtok[0:w, t, 640:D]
            pool.wait_ge(self.gained, t + 1)
            pool.tensor_tensor(x, x, self.b[0:w, 640:D], ALU.add).then_inc(self.normed_right, 1)

    def wait(self, e, t):
        e.wait_ge(self.normed_left, t + 1)
        e.wait_ge(self.normed_right, t + 1)

    def turn(self, pe, t, banks):
        w = TILES[t][1]
        self.wait(pe, t)
        for half in range(2):
            n = 2 * t + half
            if n >= 2:
                pe.wait_ge(self.low, n - 1)
            for i in range(4):
                k = 4 * half + i
                last = pe.transpose(banks[n % 2][:, i * P:i * P + w], self.keep.xtok[0:w, t, k * P:(k + 1) * P], self.keep.ident[0:w, 0:w])
            last.then_inc(self.turned, 1)

    def high_part(self, act, t, banks):
        lo, w = TILES[t]
        for half in range(2):
            n = 2 * t + half
            act.wait_ge(self.turned, n + 1)
            act.copy(self.keep.xh[:, 4 * half:4 * half + 4, lo:lo + w],
                     banks[n % 2][:, :].rearrange("p (k c) -> p k c", k=4)[:, :, 0:w]).then_inc(self.high, 1)

    def low_part(self, dve, t, banks):
        lo, w = TILES[t]
        for half in range(2):
            n = 2 * t + half
            dve.wait_ge(self.high, n + 1)
            low_part(dve, self.keep.xl[:, 4 * half:4 * half + 4, lo:lo + w],
                     banks[n % 2][:, :].rearrange("p (k c) -> p k c", k=4)[:, :, 0:w],
                     self.keep.xh[:, 4 * half:4 * half + 4, lo:lo + w]).then_inc(self.low, 1)


def turn_mix_phase(nc, name, mix, keep):
    with phase(nc, name) as p:
        tps = [p.ps(f"tps{i}", [P, 512]) for i in range(4)]
        turned, mixT_ready = p.sem("turned"), p.sem("mixT_ready")
        block = p.body.enter_context(nc.Block())

        @block.tensor
        def _(pe):
            for k in range(KC):
                if k >= 4:
                    pe.wait_ge(mixT_ready, k - 3)
                for t in range(NQ):
                    last = pe.transpose(tps[k % 4][:, t * P:(t + 1) * P], mix[:, t, k * P:(k + 1) * P], keep.ident[:, :])
                last.then_inc(turned, 1)

        @block.scalar
        def _(act):
            for k in range(KC):
                act.wait_ge(turned, k + 1)
                act.copy(keep.mixT[:, k, 0:SEQ], tps[k % 4][:, :]).then_inc(mixT_ready, 1)


def output_phase(nc, name, w_out, g, b, keep):
    MT = KC * T + P - TS
    with phase(nc, name) as p:
        w = p.sb("w", [P, 4, D])
        wh = p.sb("wh", [P, KC, D], F32R)
        wl = p.sb("wl", [P, KC, D], F32R)
        mh = p.sb("mh", [P, MT], F32R)
        ml = p.sb("ml", [P, MT], F32R)
        w_in = [p.sem(f"w_in{k}") for k in range(KC)]
        product, summed, high, low = (p.sem(n) for n in ("product", "summed", "high", "low"))
        acc = [p.ps(f"acc{i}", [P, 512]) for i in range(6)]
        tps = [p.ps(f"tps{i}", [P, 512]) for i in range(2)]
        norm = Norm(p, keep)
        block = p.body.enter_context(nc.Block())
        groups = ((0, 1), (2, 3), (4,))
        mixed = keep.mixT[:, :, :].rearrange("p k t -> p (k t)")

        @block.sync
        def _(sp):
            for k in range(KC):
                if k >= 4:
                    sp.wait_ge(low, 2 * (k - 4) + 3)
                sp.dma_start(w[:, k % 4, :], w_out[k * P:(k + 1) * P, :]).then_inc(w_in[k], 16)
            norm.load(sp, g, b)

        @block.tensor
        def _(pe):
            for group in groups:
                for k in range(KC):
                    if group[0] == 0:
                        pe.wait_ge(low, 2 * k + 3)
                    for t in group:
                        tile = slice(k * T + t * P, k * T + (t + 1) * P)
                        for h in range(2):
                            n = 2 * t + h
                            if n >= 6 and k == 0:
                                pe.wait_ge(summed, n - 5)
                            cols, o = slice(h * 512, (h + 1) * 512), acc[n % 6][:, :]
                            pe.matmul(o, mh[:, tile], wh[:, k, cols], start=(k == 0), stop=False)
                            pe.matmul(o, mh[:, tile], wl[:, k, cols], start=False, stop=False)
                            last = pe.matmul(o, ml[:, tile], wh[:, k, cols], start=False, stop=(k == KC - 1))
                            if k == KC - 1:
                                last.then_inc(product, 1)
                if group[0] == 2:
                    for t in range(2):
                        norm.turn(pe, t, tps)
            for t in range(2, NT):
                norm.turn(pe, t, tps)

        @block.scalar
        def _(act):
            act.copy(mh[:, KC * T:MT], mixed[:, 0:MT - KC * T]).then_inc(high, 1)
            for k in range(KC):
                r = slice(k * T, (k + 1) * T)
                act.copy(mh[:, r], mixed[:, r]).then_inc(high, 1)
                act.wait_ge(w_in[k], 16)
                act.copy(wh[:, k, :], w[:, k % 4, :]).then_inc(high, 1)
            for group in groups:
                for t in group:
                    norm.root_of(act, t)
                for t in group:
                    norm.scale(act, t)
                    if t >= 2:
                        norm.high_part(act, t - 2, tps)
            for t in range(NT - 2, NT):
                norm.high_part(act, t, tps)

        @block.gpsimd
        def _(pool):
            norm.bias(pool)

        @block.vector
        def _(dve):
            dve.wait_ge(high, 1)
            low_part(dve, ml[:, KC * T:MT], mixed[:, 0:MT - KC * T], mh[:, KC * T:MT]).then_inc(low, 1)
            for k in range(KC):
                r = slice(k * T, (k + 1) * T)
                dve.wait_ge(high, 2 * k + 2)
                low_part(dve, ml[:, r], mixed[:, r], mh[:, r]).then_inc(low, 1)
                dve.wait_ge(high, 2 * k + 3)
                low_part(dve, wl[:, k, :], w[:, k % 4, :], wh[:, k, :]).then_inc(low, 1)
            for group in groups:
                for t in group:
                    m = TILES[t][1]
                    for h in range(2):
                        n = 2 * t + h
                        dve.wait_ge(product, n + 1)
                        x = keep.xtok[0:m, t, h * 512:(h + 1) * 512]
                        dve.scalar_tensor_tensor(out=x, in0=x, scalar=ALPHA, in1=acc[n % 6][0:m, :], op0=ALU.mult, op1=ALU.add).then_inc(summed, 1)
                for t in group:
                    for h in range(2):
                        dve.wait_ge(summed, 2 * t + h + 1)
                        norm.statistics(dve, t, h)
                    norm.aggregate(dve, t, 2 * t + 2)
                for t in group:
                    norm.factors(dve, t)
                for t in group:
                    norm.gain(dve, t)
                    if t >= 2:
                        norm.low_part(dve, t - 2, tps)
            for t in range(NT - 2, NT):
                norm.low_part(dve, t, tps)


class StateCopy:

    ROWS = (PAST - NS) // (NF // 2)

    def __init__(self, io, half, copied):
        self.src_b, self.dst_b, self.src_c, self.dst_c = io["state_b_kv"], io["o_s_b_kv"], io["state_c_kv"], io["o_s_c_win"]
        self.b, self.copied, self.before = slice(half * NB // 2, (half + 1) * NB // 2), copied, half * 16 * (NF // 2 + 2)

    def step(self, e, i):
        e.dma_start(self.dst_b[self.b, bass.ds(i * self.ROWS, self.ROWS), :],
                    self.src_b[self.b, bass.ds(i * self.ROWS + NS, self.ROWS), :]).then_inc(self.copied, 16)

    def rest(self, e):
        done = self.ROWS * (NF // 2)
        e.dma_start(self.dst_b[self.b, done:PAST - NS, :], self.src_b[self.b, NS + done:PAST, :]).then_inc(self.copied, 16)
        e.dma_start(self.dst_c[self.b, 0:C_WIN - NS, :], self.src_c[self.b, NS:C_WIN, :]).then_inc(self.copied, 16)

    def wait(self, e):
        e.wait_ge(self.copied, self.before + 16 * (NF // 2 + 2))


def ffn_phase(nc, name, w_up, conv_w, conv_b, w_down, prev, g, b, p_tail, s_tail, y, state_copy, keep):
    EXT = 2 + SEQ + NB * (2 + NS)
    CV = EXT - 2
    S0 = 2 + SEQ
    NR = 2 + 2 * NB
    LOOPS = NF // 2
    PD = SEQ + P
    with phase(nc, name) as p:
        w = p.sb("w", [P, 2, KC, 256])
        wh = p.sb("wh", [P, 2, KC, 256], F32R)
        wl = p.sb("wl", [P, 2, KC, 256], F32R)
        wd, wdh, wdl = (t[:, :, :, :].rearrange("p s k c -> p (s k c)").rearrange("p (n f c) -> p n f c", n=4, f=2) for t in (w, wh, wl))
        hh, hl = (t[:, :, :].rearrange("p k t -> p (k t)")[:, 0:6 * PD].rearrange("p (s f t) -> p s f t", s=3, f=2) for t in (keep.xh, keep.xl))
        ext = p.sb("ext", [P, 4, EXT])
        scratch = keep.mixT[:, :, :].rearrange("p k t -> p (k t)")
        conv = scratch[:, 0:4 * CV].rearrange("p (e c) -> p e c", e=4)
        gelu = scratch[:, 4 * CV:6 * CV].rearrange("p (e c) -> p e c", e=2)
        hid = p.sb("hid", [P, NF, T])
        rows = hid[0:2 * NB, :, :].rearrange("r n t -> r (n t)")[:, 0:2 * D_FF]
        tail_rows = p.sb("tail_rows", [NR, 2, 512])
        par_rows = p.sb("par_rows", [2 * NF, 4, P])
        par = p.sb("par", [P, 4, 2 * NF])
        par_slot = p.sb("par_slot", [P, 4, 4])
        prevT = p.sb("prevT", [P, 2 * NF, 2 * NB])
        tailT = p.sb("tailT", [P, 2 * NF, NR])
        acc = [p.ps(f"acc{i}", [P, 512]) for i in range(4)]
        acc2 = [p.ps(f"acc2_{i}", [P, 512]) for i in range(4)]
        w_in = [p.sem(f"w_in{i}") for i in range(2)]
        wd_in = [p.sem(f"wd_in{i}") for i in range(4)]
        (rows_in, par_turned, par_out, prefix_in, zeroed, up_done, main_out, small_out, tails_out, conv1, conv2, conv3, gelu_done,
         hid_done, wd_used, tail_turned, tail_out, product, summed, stored) = (p.sem(n) for n in (
             "rows_in", "par_turned", "par_out", "prefix_in", "zeroed", "up_done", "main_out", "small_out", "tails_out", "conv1",
             "conv2", "conv3", "gelu_done", "hid_done", "wd_used", "tail_turned", "tail_out", "product", "summed", "stored"))
        w_high, w_low, d_high, d_low = (p.sem(n) for n in ("w_high", "w_low", "d_high", "d_low"))
        tail_stored = [p.sem(f"tail_stored{i}") for i in range(2)]
        norm = Norm(p, keep)
        wv = w_up.rearrange("(k p) n -> p k n", p=P)
        last_of_half = NF // 2 - 1
        down_acc = acc + [acc2[0]]
        block = p.body.enter_context(nc.Block())

        @block.sync
        def _(sp):
            sp.dma_start(rows, prev.rearrange("b r c -> (b r) c")).then_inc(rows_in, 16)
            sp.dma_start(par_rows[:, 0:3, :], conv_w.rearrange("j (n p) -> n j p", p=P)).then_inc(rows_in, 16)
            sp.dma_start(par_rows[:, 3, :], conv_b.rearrange("(n p) -> n p", p=P)).then_inc(rows_in, 16)
            with sp.Fori(0, LOOPS) as i:
                for s in range(2):
                    sp.wait_ge(w_low, i * 2 + (s + 1))
                    for part in range(2):
                        src = wv[:, :, bass.ds(i * 2 * P + (s * P + part * D_FF), P)]
                        sp.dma_start(w[:, s, :, part * P:(part + 1) * P], src).then_inc(w_in[s], 16)
            norm.load(sp, g, b)
            for n in range(NF):
                h, f = divmod(n, NF // 2)
                if n == 0:
                    sp.wait_ge(w_low, 2 + NF)
                if n >= 4:
                    sp.wait_ge(d_low, 2 * (n - 4) + 2)
                src = w_down[2 * f * P:(2 * f + 2) * P, h * 512:(h + 1) * 512].rearrange("(f p) c -> p f c", p=P)
                sp.dma_start(wd[:, n % 4, :, :], src).then_inc(wd_in[n % 4], 16)
            if y is not None:
                for t in range(NQ):
                    norm.wait(sp, t)
                    sp.dma_start(y[0][0, t * P:(t + 1) * P, :], keep.xtok[:, t, :]).then_inc(stored, 16)
                norm.wait(sp, NT - 1)
                sp.dma_start(y[1].rearrange("b q d -> (b q) d"), keep.xtok[0:TS, NQ, :]).then_inc(stored, 16)
                sp.wait_ge(stored, 16 * NT)

        @block.gpsimd
        def _(pool):
            pool.memset(ext[:, :, 0:2], 0.0).then_inc(zeroed, 1)
            pool.wait_ge(zeroed, 1)
            pool.sem_inc(tails_out, 8)
            pool.wait_ge(par_out, 3)
            with pool.Fori(0, LOOPS) as i:
                for e in range(4):
                    n = i * 4 + e
                    blk = i * 2 + (e // 2 + (e % 2) * NF)
                    pool.wait_ge(conv3, n + 1)
                    pool.tensor_copy(ext[:, e, S0:EXT].rearrange("p (b c) -> p b c", b=NB)[:, :, 0:2],
                                     prevT[:, bass.ds(blk, 1), :].rearrange("p a (b r) -> p (a b) r", r=2)).then_inc(prefix_in, 1)
                    pool.tensor_copy(par_slot[:, e, :], par[:, :, bass.ds(blk, 1)].rearrange("p j a -> p (j a)")).then_inc(prefix_in, 1)
                for e in range(4):
                    n = i * 4 + e
                    blk = i * 2 + (e // 2 + (e % 2) * NF)
                    pool.wait_ge(main_out, n + 5)
                    pool.wait_ge(small_out, n * 2 + 10)
                    pool.tensor_copy(tailT[:, bass.ds(blk, 1), 0:2].rearrange("p a r -> p (a r)"), ext[:, e, SEQ:SEQ + 2]).then_inc(tails_out, 1)
                    pool.tensor_copy(tailT[:, bass.ds(blk, 1), 2:NR].rearrange("p a (b r) -> p (a b) r", r=2),
                                     ext[:, e, S0:EXT].rearrange("p (b c) -> p b c", b=NB)[:, :, NS:NS + 2]).then_inc(tails_out, 1)

            norm.bias(pool)

        @block.tensor
        def _(pe):
            pe.sem_inc(up_done, 4)
            pe.sem_inc(main_out, 4)
            pe.sem_inc(small_out, 8)
            pe.wait_ge(rows_in, 48)
            for j in range(4):
                last = pe.transpose(acc2[0][:, j * 2 * NF:(j + 1) * 2 * NF], par_rows[:, j, :], keep.ident[0:2 * NF, 0:2 * NF])
            last.then_inc(par_turned, 1)
            for h in range(2):
                for n in range(NF):
                    blk = h * NF + n
                    last = pe.transpose(acc2[1 + h][:, n * 16:(n + 1) * 16], rows[0:16, blk * P:(blk + 1) * P], keep.ident[0:16, 0:16])
                last.then_inc(par_turned, 1)
            pe.wait_ge(par_out, 3)
            with pe.Fori(0, LOOPS) as i:
                for s in range(2):
                    pe.wait_ge(w_low, i * 2 + (s + 3))
                    for part in range(2):
                        e = 2 * s + part
                        pe.wait_ge(main_out, i * 4 + (e + 1))
                        pe.wait_ge(small_out, i * 8 + 2 * (e + 1))
                        out, cols = (acc[e][:, 0:TH], acc2[e][:, 0:TH]), slice(part * P, (part + 1) * P)
                        for k in range(KC):
                            last = split_product(pe, out, wh[:, s, k, cols], wl[:, s, k, cols], halves(keep.xh, k), halves(keep.xl, k),
                                                 k == 0, k == KC - 1)
                        last.then_inc(up_done, 1)
            pe.wait_ge(main_out, 4 + 2 * NF)
            pe.wait_ge(small_out, 8 + 4 * NF)
            pe.wait_ge(tails_out, 8 + 4 * NF)

            def turn_tail(n):
                if n >= 2:
                    pe.wait_ge(tail_out, n - 1)
                for i in range(4):
                    last = pe.transpose(acc2[1 + n % 2][0:NR, i * P:(i + 1) * P], tailT[:, 4 * n + i, :], keep.ident[:, :])
                last.then_inc(tail_turned, 1)

            for n in range(NF):
                h, f2 = divmod(n, NF // 2)
                pe.wait_ge(d_low, 2 * n + 2)
                for j in range(2):
                    f = 2 * f2 + j
                    for t in range(NT):
                        if h and f == 0:
                            pe.wait_ge(summed, t + 1)
                        tile = slice(t * P, (t + 1) * P)
                        wide, part = (wdh[:, n % 4, j, :], wdl[:, n % 4, j, :]), (hh[:, n % 3, j, tile], hl[:, n % 3, j, tile])
                        pe.matmul(down_acc[t][:, :], part[0], wide[0], start=(f == 0), stop=False)
                        pe.matmul(down_acc[t][:, :], part[0], wide[1], start=False, stop=False)
                        last = pe.matmul(down_acc[t][:, :], part[1], wide[0], start=False, stop=(f == NF - 1))
                        if f == NF - 1:
                            last.then_inc(product, 1)
                if f2 < NF // 2 - 1:
                    last.then_inc(wd_used, 1)
                if n < NF // 2:
                    turn_tail(n)
            pe.wait_ge(tail_out, NF // 2)
            if y is None:
                for t in range(NT):
                    norm.turn(pe, t, acc2[1:3])

        def down_slot_free(e, n):
            m = n - 3
            if m == last_of_half:
                e.wait_ge(product, NT)
            elif m >= 0:
                e.wait_ge(wd_used, m + 1 - (m > last_of_half))
            else:
                e.wait_ge(up_done, 4 + 2 * NF)

        def split_high(act, g, i, s):
            act.wait_ge(w_in[s], i * 32 + 32)
            act.wait_ge(up_done, g * 2 + 2)
            act.copy(wh[:, s, :, :], w[:, s, :, :]).then_inc(w_high, 1)

        def split_low(dve, g, s):
            dve.wait_ge(w_high, g + 1)
            low_part(dve, wl[:, s, :, :], w[:, s, :, :], wh[:, s, :, :]).then_inc(w_low, 1)

        @block.scalar
        def _(act):
            act.wait_ge(up_done, 4)
            for s in range(2):
                split_high(act, s, 0, s)

            def step(i, ahead):
                state_copy.step(act, i)
                for s in range(2):
                    for e in (2 * s, 2 * s + 1):
                        act.wait_ge(up_done, i * 4 + (e + 5))
                        act.wait_ge(conv3, i * 4 + (e + 1))
                        act.wait_ge(tails_out, i * 8 + 2 * (e + 1))
                        act.copy(ext[:, e, 2:2 + TH], acc[e][:, 0:TH]).then_inc(main_out, 1)
                    if ahead:
                        split_high(act, i * 2 + (s + 2), i + 1, s)
                    for e in (2 * s, 2 * s + 1):
                        act.wait_ge(main_out, i * 4 + (e + 5))
                        act.wait_ge(small_out, i * 8 + 2 * (e + 5))
                        act.wait_ge(prefix_in, i * 8 + 2 * (e + 1))
                        act.wait_ge(hid_done, i * 4 + 2 * (s + 1))
                        act.activation(conv[:, e, :], ext[:, e, 0:CV], ACT.Identity, scale=par_slot[:, e, 0:1], bias=par_slot[:, e, 3:4]).then_inc(conv1, 1)
                    act.wait_ge(conv3, i * 4 + (2 * s + 5))
                    act.activation(gelu[:, s, :], conv[:, 2 * s, :], ACT.Gelu_apprx_tanh).then_inc(gelu_done, 1)

            with act.Fori(0, LOOPS - 1) as i:
                step(i, True)
            step(LOOPS - 1, False)
            state_copy.rest(act)
            act.wait_ge(hid_done, 4 + 2 * NF)
            for n in range(NF):
                f2 = n % (NF // 2)
                down_slot_free(act, n)
                act.copy(hh[:, n % 3, :, 0:T], hid[:, 2 * f2:2 * f2 + 2, :]).then_inc(d_high, 1)
                act.wait_ge(wd_in[n % 4], 16 * (n // 4 + 1))
                act.copy(wdh[:, n % 4, :, :], wd[:, n % 4, :, :]).then_inc(d_high, 1)
                if 3 <= n < NF // 2 + 3:
                    m = n - 3
                    act.wait_ge(tail_turned, m + 1)
                    if m >= 2:
                        act.wait_ge(tail_stored[m % 2], 32 * (m // 2))
                    act.copy(tail_rows[:, m % 2, :], acc2[1 + m % 2][0:NR, :]).then_inc(tail_out, 1)
                    act.wait_ge(tail_out, m + 1)
                    act.dma_start(p_tail[:, m * 512:(m + 1) * 512], tail_rows[0:2, m % 2, :]).then_inc(tail_stored[m % 2], 16)
                    act.dma_start(s_tail[:, m * 512:(m + 1) * 512], tail_rows[2:NR, m % 2, :]).then_inc(tail_stored[m % 2], 16)
            for t in range(NT):
                norm.root_of(act, t)
            for t in range(NT):
                norm.scale(act, t)
                if t >= 2 and y is None:
                    norm.high_part(act, t - 2, acc2[1:3])
            if y is None:
                for t in range(NT - 2, NT):
                    norm.high_part(act, t, acc2[1:3])
            state_copy.wait(act)
            for m in range(2):
                act.wait_ge(tail_stored[m], 32 * len(range(m, NF // 2, 2)))

        @block.vector
        def _(dve):
            dve.sem_inc(w_low, 2)
            dve.sem_inc(conv3, 4)
            dve.sem_inc(hid_done, 4)
            dve.wait_ge(par_turned, 1)
            dve.tensor_copy(par[:, :, :], acc2[0][:, 0:8 * NF].rearrange("p (j n) -> p j n", j=4)).then_inc(par_out, 1)
            for h in range(2):
                dve.wait_ge(par_turned, 2 + h)
                dve.tensor_copy(prevT[:, h * NF:(h + 1) * NF, :], acc2[1 + h][:, 0:16 * NF].rearrange("p (n r) -> p n r", r=16)).then_inc(par_out, 1)
            for s in range(2):
                split_low(dve, s, s)

            def step(i, ahead):
                for s in range(2):
                    for e in (2 * s, 2 * s + 1):
                        dve.wait_ge(up_done, i * 4 + (e + 5))
                        dve.wait_ge(tails_out, i * 8 + 2 * (e + 1))
                        dve.tensor_copy(ext[:, e, 2 + TH:S0], acc2[e][:, 0:SEQ - TH]).then_inc(small_out, 1)
                        dve.tensor_copy(ext[:, e, S0:EXT].rearrange("p (b c) -> p b c", b=NB)[:, :, 2:2 + NS],
                                        acc2[e][:, SEQ - TH:TH].rearrange("p (b q) -> p b q", q=NS)).then_inc(small_out, 1)
                    if ahead:
                        split_low(dve, i * 2 + (s + 2), s)
                    for e in (2 * s, 2 * s + 1):
                        dve.wait_ge(conv1, i * 4 + (e + 1))
                        dve.scalar_tensor_tensor(out=conv[:, e, :], in0=ext[:, e, 1:1 + CV], scalar=par_slot[:, e, 1:2], in1=conv[:, e, :],
                                                 op0=ALU.mult, op1=ALU.add).then_inc(conv2, 1)
                        dve.wait_ge(conv2, i * 4 + (e + 1))
                        dve.scalar_tensor_tensor(out=conv[:, e, :], in0=ext[:, e, 2:2 + CV], scalar=par_slot[:, e, 2:3], in1=conv[:, e, :],
                                                 op0=ALU.mult, op1=ALU.add).then_inc(conv3, 1)
                    dve.wait_ge(conv3, i * 4 + (2 * s + 6))
                    dve.wait_ge(gelu_done, i * 2 + (s + 1))
                    f = i * 2 + s
                    dve.tensor_tensor(hid[:, bass.ds(f, 1), 0:SEQ].rearrange("p a t -> p (a t)"), gelu[:, s, 0:SEQ], conv[:, 2 * s + 1, 0:SEQ], ALU.mult).then_inc(hid_done, 1)
                    dve.tensor_tensor(hid[:, bass.ds(f, 1), SEQ:T].rearrange("p a (b q) -> p (a b) q", q=NS),
                                      sample_columns(gelu[:, s, :], S0), sample_columns(conv[:, 2 * s + 1, :], S0), ALU.mult).then_inc(hid_done, 1)

            def take_in(h, t):
                m = TILES[t][1]
                dve.wait_ge(product, h * NT + t + 1)
                x = keep.xtok[0:m, t, h * 512:(h + 1) * 512]
                dve.scalar_tensor_tensor(out=x, in0=x, scalar=ALPHA, in1=down_acc[t][0:m, :], op0=ALU.mult, op1=ALU.add).then_inc(summed, 1)

            with dve.Fori(0, LOOPS - 1) as i:
                step(i, True)
            step(LOOPS - 1, False)
            for n in range(NF):
                f2 = n % (NF // 2)
                if n == last_of_half + 3:
                    for t in range(NT):
                        take_in(0, t)
                if last_of_half + 3 < n <= last_of_half + 3 + NT:
                    t = n - last_of_half - 4
                    dve.wait_ge(summed, t + 1)
                    norm.statistics(dve, t, 0)
                dve.wait_ge(d_high, 2 * n + 1)
                low_part(dve, hl[:, n % 3, :, 0:T], hid[:, 2 * f2:2 * f2 + 2, :], hh[:, n % 3, :, 0:T]).then_inc(d_low, 1)
                dve.wait_ge(d_high, 2 * n + 2)
                low_part(dve, wdl[:, n % 4, :, :], wd[:, n % 4, :, :], wdh[:, n % 4, :, :]).then_inc(d_low, 1)
            for t in range(NT):
                take_in(1, t)
                dve.wait_ge(summed, NT + t + 1)
                norm.statistics(dve, t, 1)
                norm.aggregate(dve, t, NT + t + 1)
            for t in range(NT):
                norm.factors(dve, t)
            for t in range(NT):
                norm.gain(dve, t)
                if t >= 2 and y is None:
                    norm.low_part(dve, t - 2, acc2[1:3])
            if y is None:
                for t in range(NT - 2, NT):
                    norm.low_part(dve, t, acc2[1:3])


def sample_columns(row, start):
    a = row.ap
    return bass.AP(tensor=row.tensor, offset=row.offset + start, ap=[list(a[0]), [NS + 2, NB], [1, NS]])


def prompt_compressed_phase(nc, hT, tok, mix, io, keep):
    NC = SEQ // STRIDE - 1
    with phase(nc, "pcmp") as p:
        w1e = p.sb("w1e", [HD, 2, 32, HD])
        peT = p.sb("peT", [HD, 2, 32])
        b1 = p.sb("b1", [HD, 2])
        w2 = p.sb("w2", [HD, 2, HD])
        x = p.sb("x", [HD, 2, 2, SEQ])
        q = p.sb("q", [HD, N_HEADS, SEQ])
        hid = p.sb("hid", [HD, 2, 2, 32])
        kcT = p.sb("kcT", [HD, 2, 32])
        v_blk = p.sb("v_blk", [P, 2, 4, HD])
        mask = p.sb("mask", [P, NQ, 32])
        lg = p.sb("lg", [P, 2, N_HEADS, 32])
        pr = p.sb("pr", [P, 2, N_HEADS, 32])
        stat = p.sb("stat", [P, 2, 2, N_HEADS])
        pT = p.sb("pT", [P, 2, 512])
        psc = p.ps("psc", [P, 512])
        psh = p.ps("psh", [P, 512])
        psk = p.ps("psk", [P, 512])
        lgp = [p.ps(f"lgp{i}", [P, 512]) for i in range(2)]
        tps = p.ps("tps", [P, 512])
        outp = p.ps("outp", [P, 2 * 512])
        names = ("loaded", "gated", "const_sum", "const", "hidden", "activated", "keyed", "values", "cleared", "placed",
                 "scored", "soft", "exped", "weighed", "turned", "copied", "attended", "mixed")
        (loaded, gated, const_sum, const, hidden, activated, keyed, values, cleared, placed,
         scored, soft, exped, weighed, turned, copied, attended, mixed) = (p.sem(n) for n in names)
        block = p.body.enter_context(nc.Block())
        LOADS = 6
        w1_in = [p.sem(f"w1_in{a}") for a in range(2)]

        @block.sync
        def _(sp):
            with nc.allow_non_contiguous_dma(reason="small transposed parameters"):
                for a in range(2):
                    sp.dma_start(w1e[:, a, :, :], io["phi_w1"][a].rearrange("j e f -> e j f")).then_inc(w1_in[a], 16)
                    sp.dma_start(peT[:, a, :], io["phi_pe"][a].rearrange("j e -> e j")).then_inc(w1_in[a], 16)
                sp.dma_start(b1[:, :], io["phi_b1"].rearrange("a f -> f a")).then_inc(loaded, 16)
            sp.dma_start(w2[:, :, :], io["phi_w2"].rearrange("a f e -> f a e")).then_inc(loaded, 16)
            for a in range(2):
                sp.dma_start(x[:, a, :, :], hT[C_KV + a * P:C_KV + (a + 1) * P, 0:SEQ].rearrange("(g e) t -> e g t", e=HD)).then_inc(loaded, 16)
            sp.dma_start(q[:, :, :], hT[C_Q:C_Q + N_HEADS * HD, 0:SEQ].rearrange("(h e) t -> e h t", e=HD)).then_inc(loaded, 16)
            sp.dma_start(mask[:, :, :], io["c_cmp_mask"]).then_inc(loaded, 16)
            sp.wait_ge(keep.pending, keep.pending_count)

        @block.tensor
        def _(pe):
            for a in range(2):
                pe.wait_ge(w1_in[a], 32)
                for j in range(32):
                    last = pe.matmul(psc[0:HD, a:a + 1], w1e[:, a, j, :], peT[:, a, j:j + 1], start=(j == 0), stop=(j == 31))
                last.then_inc(const_sum, 1)
            pe.wait_ge(loaded, 16 * LOADS)
            for a in range(2):
                for j in range(32):
                    src = x[:, a, :, j:j + STRIDE * (NC - 1) + 1:STRIDE]
                    last = pe.matmul(psh[0:HD, a * 64:a * 64 + 2 * NC].rearrange("p (g c) -> p g c", g=2), w1e[:, a, j, :], src,
                                     start=(j == 0), stop=(j == 31))
                last.then_inc(hidden, 1)
            pe.wait_ge(activated, 2)
            pe.matmul(psk[0:HD, 0:2 * NC].rearrange("p (g c) -> p g c", g=2), w2[:, 0, :], hid[:, 0, :, 0:NC], start=True, stop=True).then_inc(keyed, 1)
            for g in range(2):
                pe.matmul(psk[0:NC, 128 + g * HD:128 + (g + 1) * HD], hid[:, 1, g, 0:NC], w2[:, 1, :], start=True, stop=True).then_inc(values, 1)
            pe.wait_ge(placed, 9)

            def scores(i):
                if i >= 2:
                    pe.wait_ge(soft, 3 * (i - 2) + 1)
                for h in range(N_HEADS):
                    last = pe.matmul(lgp[i % 2][:, h * 32:(h + 1) * 32], q[:, h, i * P:(i + 1) * P], kcT[:, h // 8, :], start=True, stop=True)
                last.then_inc(scored, 1)

            scores(0)
            for i in range(NQ):
                if i + 1 < NQ:
                    scores(i + 1)
                pe.wait_ge(weighed, i + 1)
                if i:
                    pe.wait_ge(copied, i)
                for u in range(4):
                    last = pe.transpose(tps[:, u * P:(u + 1) * P], pr[:, i % 2, 4 * u:4 * u + 4, :].rearrange("p h c -> p (h c)"), keep.ident[:, :])
                last.then_inc(turned, 1)
                pe.wait_ge(copied, i + 1)
                if i:
                    pe.wait_ge(mixed, i)
                for u in range(4):
                    last = pe.matmul(outp[:, u * 256:(u + 1) * 256], pT[:, i % 2, u * P:(u + 1) * P],
                                     v_blk[:, u // 2, :, :].rearrange("p h e -> p (h e)"), start=True, stop=True)
                last.then_inc(attended, 1)

        @block.scalar
        def _(act):
            act.activation(keep.gate_tok[:, :, :], tok[:, 0:NQ, TC_G:TC], ACT.Exp, scale=-1.0).then_inc(gated, 1)
            act.wait_ge(const, 2)
            act.wait_ge(hidden, 2)
            for a in range(2):
                act.activation(hid[:, a, :, 0:NC], psh[0:HD, a * 64:a * 64 + 2 * NC].rearrange("p (g c) -> p g c", g=2),
                               ACT.Gelu_apprx_tanh, bias=keep.cmp_const[:, a:a + 1]).then_inc(activated, 1)
            for i in range(NQ):
                act.wait_ge(soft, 3 * i + 3)
                act.activation(pr[:, i % 2, :, :], lg[:, i % 2, :, :], ACT.Exp).then_inc(exped, 1)
                act.wait_ge(turned, i + 1)
                if i >= 2:
                    act.wait_ge(attended, i - 1)
                act.copy(pT[:, i % 2, :], tps[:, :]).then_inc(copied, 1)

        @block.vector
        def _(dve):
            dve.wait_ge(gated, 1)
            dve.tensor_scalar(keep.gate_tok[:, :, :], keep.gate_tok[:, :, :], 1.0, None, ALU.add).then_inc(gated, 1)
            dve.wait_ge(gated, 2)
            dve.reciprocal(keep.gate_tok[:, :, :], keep.gate_tok[:, :, :]).then_inc(gated, 1)
            dve.wait_ge(loaded, 16 * LOADS)
            dve.wait_ge(const_sum, 2)
            for a in range(2):
                dve.tensor_tensor(keep.cmp_const[:, a:a + 1], psc[0:HD, a:a + 1], b1[:, a:a + 1], ALU.add).then_inc(const, 1)
            dve.memset(kcT[:, :, :], 0.0).then_inc(cleared, 1)
            dve.memset(v_blk[:, :, :, :], 0.0).then_inc(cleared, 1)
            dve.wait_ge(cleared, 2)
            dve.wait_ge(keyed, 1)
            dve.wait_ge(values, 2)
            dve.tensor_copy(kcT[:, :, 0:NC], psk[0:HD, 0:2 * NC].rearrange("p (g c) -> p g c", g=2)).then_inc(placed, 1)
            for g in range(2):
                for u in range(4):
                    dve.tensor_copy(v_blk[32 * u:32 * u + NC, g, u, :], psk[0:NC, 128 + g * HD:128 + (g + 1) * HD]).then_inc(placed, 1)
            def mix_in(i):
                dve.wait_ge(attended, i + 1)
                dve.tensor_copy(mix[:, i, :], outp[:, :]).then_inc(mixed, 1)

            dve.wait_ge(gated, 3)
            for i in range(NQ):
                s = i % 2
                l, pv, mx, sm = lg[:, s, :, :], pr[:, s, :, :], stat[:, s, 0, :], stat[:, s, 1, :]
                dve.wait_ge(scored, i + 1)
                if i >= 2:
                    dve.wait_ge(exped, i - 1)
                dve.scalar_tensor_tensor(out=l, in0=lgp[s][:, :].rearrange("p (h c) -> p h c", h=N_HEADS), scalar=SCALE,
                                         in1=mask[:, i, None, :].to_broadcast([P, N_HEADS, 32]), op0=ALU.mult, op1=ALU.add).then_inc(soft, 1)
                dve.wait_ge(soft, 3 * i + 1)
                dve.tensor_reduce(mx, l, AX_X, ALU.max).then_inc(soft, 1)
                dve.wait_ge(soft, 3 * i + 2)
                dve.tensor_scalar(mx, mx, -FLOOR, None, ALU.max).then_inc(gated, 1)
                dve.wait_ge(gated, 4 + 3 * i)
                dve.tensor_tensor(l, l, mx[:, :, None].to_broadcast([P, N_HEADS, 32]), ALU.subtract).then_inc(soft, 1)
                dve.wait_ge(exped, i + 1)
                dve.tensor_reduce(sm, pv, AX_X, ALU.add).then_inc(gated, 1)
                dve.wait_ge(gated, 5 + 3 * i)
                dve.tensor_scalar(sm, sm, 1e-30, None, ALU.max).then_inc(gated, 1)
                dve.wait_ge(gated, 6 + 3 * i)
                dve.reciprocal(sm, sm).then_inc(cleared, 1)
                dve.wait_ge(cleared, 3 + 2 * i)
                dve.tensor_tensor(sm, keep.gate_tok[:, i, 0:N_HEADS], sm, ALU.mult).then_inc(cleared, 1)
                dve.wait_ge(cleared, 4 + 2 * i)
                dve.tensor_tensor(pv, pv, sm[:, :, None].to_broadcast([P, N_HEADS, 32]), ALU.mult).then_inc(weighed, 1)
                if i:
                    mix_in(i - 1)
            mix_in(NQ - 1)


def sample_c_phase(nc, hT, vec, cache_kv, state, new_kv, new_win, io, keep):
    rows_in_cache = cache_kv.rearrange("n (c j) s g e -> (n c) (j s g e)", j=STRIDE)
    R = N_HEADS * NS
    NC = NCH - 1
    LW = C_WIN + NS
    with phase(nc, "sc") as p:
        kv = p.sb("kv", [P, 2, STRIDE * 512])
        win = p.sb("win", [P, 2, 4, 256])
        w1 = p.sb("w1", [P, 2, 8, P])
        w2 = p.sb("w2", [HD, 2, HD])
        xT = p.sb("xT", [P, 2, 2, 8, P])
        hid = p.sb("hid", [HD, 2, 2, NC])
        h_next = h_sum = hid
        kcT = p.sb("kcT", [P, NC])
        vc = p.sb("vc", [NC, P])
        zeros = p.sb("zeros", [P, P])
        sc_cmp = p.sb("sc_cmp", [P, NC])
        pc = p.sb("pc", [P, NC])
        pcT = p.sb("pcT", [NC, P])
        imp = p.sb("imp", [16, P + 2])
        pair = p.sb("pair", [16, P])
        blocks = p.sb("blocks", [16, N_SEL])
        best = p.sb("best", [16, 2, 8])
        choice = p.sb("choice", [16, 2, N_SEL], BF16)
        spread = p.sb("spread", [16, R], BF16)
        q = p.sb("q", [HD, N_HEADS, TS])
        q_blk = p.sb("q_blk", [P, NB, R])
        k_new = p.sb("k_new", [P, 2, TS])
        v_new = p.sb("v_new", [NS, 2, 2, P])
        kT = p.sb("kT", [P, LS])
        kwT = p.sb("kwT", [P, LW])
        nat = kv[:, 1, 0:LS]
        nat_w = kv[:, 1, LS:LS + LW]
        table = p.sb("table", [R, LS])
        table_w = p.sb("table_w", [R, LW])
        gate = p.sb("gate", [R, 3, NB])
        shifted = p.sb("shifted", [R, LS])
        shifted_w = p.sb("shifted_w", [R, LW])
        pT = p.sb("pT", [P, STRIDE + 1, R])
        pwT = p.sb("pwT", [P, 5, R])
        nmax = p.sb("nmax", [R, 12])
        total = p.sb("total", [R, 4])
        wgt = p.sb("wgt", [R, 4])
        o = p.sb("o", [R, 3, HD])
        logit = [p.ps(f"logit{i}", [P, 512]) for i in range(3)]
        tps = [p.ps(f"tps{i}", [P, 512]) for i in range(2)]
        hps = p.ps("hps", [P, 512])
        cps = p.ps("cps", [P, 512])
        outp = p.ps("outp", [P, 512])
        names = ("loaded", "t_in", "zeroed", "built", "gated", "tabled", "h_done", "h_moved", "h_summed", "activated", "kc_done",
                 "kc_out", "cmp_scored", "cmp_shifted", "cmp_exped", "cmp_total", "cmp_normed", "imp_done", "imp_out", "paired",
                 "block_sums", "bonus", "picked", "marked", "chosen", "cmp_out", "kT_new", "kwT_new", "slc_max", "slc_exped",
                 "win_exped", "slc_out", "win_out", "weighed", "o_part", "o_ready", "o_turned", "mixed", "pcT_ready", "pT_ready",
                 "pwT_ready", "kT_ready", "kwT_ready", "inverted", "w1_in")
        m = {n: p.sem(n) for n in names}
        kv_in = keep.c_kv_in
        win_in = [p.sem(f"win_in{i}") for i in range(2)]
        tps_turned = [p.sem(f"tps_turned{i}") for i in range(2)]
        tps_out = [p.sem(f"tps_out{i}") for i in range(2)]
        scored = [p.sem(f"scored{i}") for i in range(3)]
        shifted_out = [p.sem(f"shifted_out{i}") for i in range(3)]

        turns, scores_order = [], []
        for b in range(-1, NB):
            if b >= 0:
                turns += [("k", b, i) for i in range(4)] + [("kw", b, 0)]
                scores_order += [("s", b, i) for i in range(5)] + [("w", b, i) for i in range(2)]
            if b + 1 < NB:
                turns += [("x", b + 1, i) for i in range(8)]
            if b >= 0:
                turns += [("p", b, i) for i in range(5)] + [("pw", b, i) for i in range(2)]
            if b + 1 < NB:
                turns += [("pc", b + 1, 0)]
        turn_no = {g: n for n, g in enumerate(turns)}

        def out_count(n):
            return sum(2 if turns[u][0] == "x" else 1 for u in range(n % 2, n + 1, 2))

        score_no = {g: n for n, g in enumerate(scores_order)}
        block = p.body.enter_context(nc.Block())
        LOADS = 4 + 3 * NB + 2 * NS

        def load_gates(e, batches):
            with nc.allow_non_contiguous_dma(reason="gates, one per partition"):
                for br in range(3):
                    for b in batches:
                        src = bass.AP(tensor=hT.tensor, offset=(C_G + br * N_HEADS) * T + SEQ + b * NS, ap=[[T, N_HEADS], [1, NS], [1, 1]])
                        e.dma_start(gate[:, br, b:b + 1], src).then_inc(m["loaded"], 16)

        @block.gpsimd
        def _(pool):
            for b in range(NB):
                if b == 1:
                    pool.wait_ge(m["tabled"], 4)
                if b >= 2:
                    pool.wait_ge(m["slc_out"], b - 1)
                pool.indirect_dma_start(out=kv[:, b % 2, :], out_offset=None, in_=rows_in_cache,
                                        in_offset=bass.IndirectOffsetOnAxis(ap=keep.chunk_row[:, b:b + 1], axis=0)).then_inc(kv_in[b % 2], 16)

        @block.sync
        def _(sp):
            ld = m["loaded"]
            for a in range(2):
                for ab in range(2):
                    src = io["phi_w1"][a, 16 * ab:16 * (ab + 1)].rearrange("(m j) e f -> m (j e) f", j=2).rearrange("m p f -> p m f")
                    sp.dma_start(w1[:, a, :, ab * HD:(ab + 1) * HD], src).then_inc(m["w1_in"], 16)
            sp.dma_start(w2[:, :, :], io["phi_w2"].rearrange("a f e -> f a e")).then_inc(ld, 16)
            sp.dma_start(q[:, :, :], hT[C_Q:C_Q + N_HEADS * HD, SEQ:T].rearrange("(h e) t -> e h t", e=HD)).then_inc(ld, 16)
            for a, s in enumerate((2, 4)):
                sp.dma_start(k_new[:, a, :], hT[C_KV + s * P:C_KV + (s + 1) * P, SEQ:T]).then_inc(ld, 16)
            load_gates(sp, range(0, NB // 2))
            sample_table(sp, nat_w, vec, KIND_WIN, 0, N_HEADS, PAST - C_WIN, LW, ld)
            for b in range(NB):
                if b >= 2:
                    sp.wait_ge(m["win_out"], b - 1)
                sp.dma_start(v_new[:, 0, b % 2, :], new_kv[b, :, 3 * P:4 * P]).then_inc(win_in[b % 2], 16)
                sp.dma_start(v_new[:, 1, b % 2, :], new_win[b, :, P:2 * P]).then_inc(win_in[b % 2], 16)
                sp.dma_start(win[:, b % 2, :, :], state[b].rearrange("(c j) n -> c j n", j=4)).then_inc(win_in[b % 2], 16)

        @block.tensor
        def _(pe):
            def turned(group, sources, width, dtype_rows=P):
                n = turn_no[group]
                if n >= 2:
                    pe.wait_ge(tps_out[n % 2], out_count(n - 2))
                for i, (src, rows) in enumerate(sources):
                    last = pe.transpose(tps[n % 2][0:rows, i * width:(i + 1) * width], src, keep.ident[:, :])
                last.then_inc(tps_turned[n % 2], 1)

            def cmp_keys(b):
                pe.wait_ge(kv_in[b % 2], 16 * (b // 2 + 1))
                for i in range(8):
                    a, odd, f = i // 4, i // 2 % 2, i % 2
                    first = [(2 * (4 * f + u) + odd) * 512 + a * P for u in range(4)]
                    turned(("x", b, i), [(kv[:, b % 2, c:c + P], P) for c in first], P)

            def cmp_hidden(b):
                for i in (6, 7):
                    n = turn_no[("x", b, i)]
                    pe.wait_ge(tps_out[n % 2], out_count(n))
                if b:
                    pe.wait_ge(m["h_summed"], 2 * b)
                else:
                    pe.wait_ge(m["w1_in"], 64)
                if b >= 2:
                    pe.wait_ge(m["mixed"], 2 * (b - 1))
                for a in range(2):
                    for u in range(8):
                        last = pe.matmul(hps[:, a * 256:(a + 1) * 256].rearrange("p (g c) -> p g c", g=2), w1[:, a, u, :],
                                         xT[:, a, :, u, :], start=(u == 0), stop=(u == 7))
                    last.then_inc(m["h_done"], 1)

            def cmp_final(b):
                pe.wait_ge(m["activated"], 2 * b + 2)
                if b == 0:
                    pe.wait_ge(m["built"], 4)
                if b:
                    pe.wait_ge(m["imp_out"], b)
                for g in range(2):
                    pe.matmul(cps[g * HD:(g + 1) * HD, 0:NC], w2[:, 0, :], hid[:, 0, g, :], start=True, stop=True)
                for g in range(2):
                    last = pe.matmul(cps[0:NC, 128 + g * HD:128 + (g + 1) * HD], hid[:, 1, g, :], w2[:, 1, :], start=True, stop=True)
                last.then_inc(m["kc_done"], 1)
                pe.wait_ge(m["kc_out"], 2 * b + 2)
                pe.matmul(cps[:, 256:256 + NC], q_blk[:, b, :], kcT[:, :], start=True, stop=True).then_inc(m["cmp_scored"], 1)

            def cmp_choice(b):
                pe.wait_ge(m["cmp_normed"], b + 1)
                pe.matmul(cps[0:16, 384:384 + NC], keep.group_sum[:, :], pc[:, :], start=True, stop=True).then_inc(m["imp_done"], 1)
                turned(("pc", b, 0), [(pc[:, :], NC)], P)
                pe.wait_ge(m["pcT_ready"], b + 1)
                if b:
                    pe.wait_ge(m["o_ready"], b)
                pe.matmul(outp[:, 0:P], pcT[:, :], vc[:, :], start=True, stop=True).then_inc(m["cmp_out"], 1)

            def keys(b):
                for i in range(4):
                    turned(("k", b, i), [(kv[:, b % 2, (4 * i + u) * 512 + 256:(4 * i + u) * 512 + 384], P) for u in range(4)], P)
                pe.wait_ge(win_in[b % 2], 48 * (b // 2 + 1))
                turned(("kw", b, 0), [(win[:, b % 2, u, 0:P], P) for u in range(4)], P)

            def score_group(group, bank_cols, key_cols, pick):
                n = score_no[group]
                if n >= 3:
                    pe.wait_ge(shifted_out[n % 3], n // 3)
                mm = pe.matmul(logit[n % 3][:, 0:bank_cols], q_blk[:, group[1], :], key_cols, start=True, stop=pick is None)
                if pick is not None:
                    out = logit[n % 3][:, 0:bank_cols]
                    if bank_cols == 512:
                        out = out.rearrange("r (j k c) -> r j k c", j=4, c=4)
                    mm = pe.matmul(out, spread[:, :], pick, start=False, stop=True)
                mm.then_inc(scored[n % 3], 1)

            def scores(b):
                pe.wait_ge(m["chosen"], b + 1)
                for i in range(5):
                    if i == 4:
                        pe.wait_ge(m["kT_new"], b + 1)
                        pick = choice[:, b % 2, 32:33].to_broadcast([16, NS])
                        score_group(("s", b, 4), NS, kT[:, PAST:LS], pick)
                    else:
                        pe.wait_ge(m["kT_ready"], 4 * b + i + 1)
                        pick = choice[:, b % 2, None, 0:32, None].to_broadcast([16, 4, 32, 4])
                        score_group(("s", b, i), 512, kT[:, i * 512:(i + 1) * 512], pick)
                pe.wait_ge(m["kwT_ready"], b + 1)
                pe.wait_ge(m["kwT_new"], b + 1)
                score_group(("w", b, 0), 512, kwT[:, 0:512], None)
                score_group(("w", b, 1), NS, kwT[:, 512:LW], None)

            def turn_probs(b):
                pe.wait_ge(m["slc_exped"], b + 1)
                for i in range(4):
                    turned(("p", b, i), [(shifted[:, (4 * i + u) * P:(4 * i + u + 1) * P], P) for u in range(4)], P)
                turned(("p", b, 4), [(shifted[:, PAST:LS], NS)], P)
                pe.wait_ge(m["win_exped"], b + 1)
                turned(("pw", b, 0), [(shifted_w[:, u * P:(u + 1) * P], P) for u in range(4)], P)
                turned(("pw", b, 1), [(shifted_w[:, C_WIN:LW], NS)], P)

            def values(b):
                pe.wait_ge(m["pT_ready"], 5 * b + 5)
                if b:
                    pe.wait_ge(m["o_ready"], b)
                for j in range(STRIDE):
                    pe.matmul(outp[:, 128:256], pT[:, j, :], kv[:, b % 2, j * 512 + 384:(j + 1) * 512], start=(j == 0), stop=False)
                pe.matmul(outp[:, 128:256], pT[0:NS, STRIDE, :], v_new[:, 0, b % 2, :], start=False, stop=True).then_inc(m["slc_out"], 1)
                pe.wait_ge(m["pwT_ready"], 2 * b + 2)
                for j in range(4):
                    pe.matmul(outp[:, 256:384], pwT[:, j, :], win[:, b % 2, j, P:2 * P], start=(j == 0), stop=False)
                pe.matmul(outp[:, 256:384], pwT[0:NS, 4, :], v_new[:, 1, b % 2, :], start=False, stop=True).then_inc(m["win_out"], 1)

            def turn_out(b):
                pe.wait_ge(m["o_ready"], b + 1)
                pe.wait_ge(m["h_summed"], 2 * min(b + 2, NB))
                pe.transpose(hps[0:HD, 0:P], o[:, 2, :], keep.ident[:, :]).then_inc(m["o_turned"], 1)

            for b in range(-1, NB):
                if b >= 0:
                    keys(b)
                    scores(b)
                if b + 1 < NB:
                    cmp_keys(b + 1)
                    cmp_hidden(b + 1)
                if b >= 0:
                    turn_probs(b)
                if b + 1 < NB:
                    cmp_final(b + 1)
                if b >= 0:
                    values(b)
                if b + 1 < NB:
                    cmp_choice(b + 1)
                if b >= 0:
                    turn_out(b)

        def x_group(copy, b, i, g):
            a, odd, f = i // 4, i // 2 % 2, i % 2
            n = turn_no[("x", b, i)]
            copy(xT[odd * HD:(odd + 1) * HD, a, g, 4 * f:4 * f + 4, :],
                 tps[n % 2][g * HD:(g + 1) * HD, :].rearrange("p (m c) -> p m c", m=4)).then_inc(tps_out[n % 2], 1)

        @block.scalar
        def _(act):
            def turned(group, dst, src_of, done):
                n = turn_no[group]
                act.wait_ge(tps_turned[n % 2], n // 2 + 1)
                act.copy(dst, src_of(tps[n % 2])).then_inc(tps_out[n % 2], 1)
                act.wait_ge(tps_out[n % 2], out_count(n))
                act.sem_inc(done, 1)

            def exponentials(b):
                act.wait_ge(m["weighed"], 2 * b + 1)
                act.wait_ge(m["slc_max"], b + 1)
                act.activation(shifted[:, :], shifted[:, :], ACT.Exp, bias=nmax[:, 8:9], scale=-1.0, accum_out=total[:, 0:1]).then_inc(m["slc_exped"], 1)
                act.activation(shifted_w[:, :], shifted_w[:, :], ACT.Exp, bias=nmax[:, 9:10], scale=-1.0, accum_out=total[:, 1:2]).then_inc(m["win_exped"], 1)

            sample_table(act, nat, vec, KIND_FULL, 0, N_HEADS, 0, LS, m["loaded"])
            load_gates(act, range(NB // 2, NB))
            for b in range(-1, NB):
                if b >= 0:
                    if b:
                        act.wait_ge(m["slc_max"], b)
                    for i in range(4):
                        turned(("k", b, i), kT[:, i * 512:(i + 1) * 512], lambda t: t[:, :], m["kT_ready"])
                    act.copy(kT[:, PAST:LS], k_new[:, 0, b * NS:(b + 1) * NS]).then_inc(m["kT_new"], 1)
                    turned(("kw", b, 0), kwT[:, 0:C_WIN], lambda t: t[:, :], m["kwT_ready"])
                    act.copy(kwT[:, C_WIN:LW], k_new[:, 1, b * NS:(b + 1) * NS]).then_inc(m["kwT_new"], 1)
                if b + 1 < NB:
                    if b >= 0:
                        act.wait_ge(m["h_done"], 2 * (b + 1))
                    for i in range(8):
                        n = turn_no[("x", b + 1, i)]
                        act.wait_ge(tps_turned[n % 2], n // 2 + 1)
                        x_group(act.copy, b + 1, i, 0)
                        if b < 0 and i == 7:
                            act.wait_ge(m["loaded"], 16 * LOADS)
                            act.activation(gate[:, :, :], gate[:, :, :], ACT.Exp, scale=-1.0).then_inc(m["gated"], 1)
                        if i == 3 and b >= 0:
                            exponentials(b)
                    for a in range(2):
                        act.wait_ge(m["h_summed"], 2 * (b + 1) + a + 1)
                        act.activation(hid[:, a, :, :], h_sum[:, a, :, :], ACT.Gelu_apprx_tanh, bias=keep.cmp_const[:, a:a + 1]).then_inc(m["activated"], 1)
                    act.wait_ge(m["cmp_shifted"], b + 2)
                    act.activation(pc[:, :], sc_cmp[:, :], ACT.Exp, bias=nmax[:, 10:11], scale=-1.0, accum_out=total[:, 2:3]).then_inc(m["cmp_exped"], 1)
                else:
                    exponentials(b)

        @block.vector
        def _(dve):
            dve.memset(q_blk[:, :, :], 0.0).then_inc(m["zeroed"], 1)
            dve.memset(zeros[:, :], 0.0).then_inc(m["zeroed"], 1)
            dve.memset(imp[:, :], 0.0).then_inc(m["zeroed"], 1)
            dve.memset(blocks[:, :], 0.0).then_inc(m["zeroed"], 1)
            dve.wait_ge(m["zeroed"], 4)
            def prepare():
                dve.wait_ge(m["loaded"], 16 * LOADS)
                query_blocks(dve, q_blk, q, 2, N_HEADS // 2, m["built"])
                dve.tensor_copy(spread[:, :], keep.group_spread[:, :]).then_inc(m["built"], 1)
                dve.wait_ge(m["gated"], 1)
                dve.tensor_scalar(gate[:, :, :], gate[:, :, :], 1.0, None, ALU.add).then_inc(m["gated"], 1)
                dve.wait_ge(m["gated"], 2)
                dve.reciprocal(gate[:, :, :], gate[:, :, :]).then_inc(m["built"], 1)
                dve.tensor_copy(table[:, 0:PAST].rearrange("r (j c) -> r c j", j=STRIDE),
                                nat[:, 0:PAST].rearrange("r (c j) -> r c j", j=STRIDE)).then_inc(m["tabled"], 1)
                dve.tensor_copy(table[:, PAST:LS], nat[:, PAST:LS]).then_inc(m["tabled"], 1)
                dve.tensor_copy(table_w[:, 0:C_WIN].rearrange("r (j c) -> r c j", j=4),
                                nat_w[:, 0:C_WIN].rearrange("r (c j) -> r c j", j=4)).then_inc(m["tabled"], 1)
                dve.tensor_copy(table_w[:, C_WIN:LW], nat_w[:, C_WIN:LW]).then_inc(m["tabled"], 1)
                dve.wait_ge(m["tabled"], 4)
                dve.wait_ge(m["built"], 4)

            def shift(group, dst, bias, w, col):
                n = score_no[group]
                dve.wait_ge(scored[n % 3], n // 3 + 1)
                dve.tensor_tensor_reduce(out=dst, in0=logit[n % 3][:, 0:w], in1=bias, scale=-1.0, scalar=FLOOR,
                                         op0=ALU.add, op1=ALU.min, accum_out=nmax[:, col:col + 1]).then_inc(shifted_out[n % 3], 1)

            def hidden(b):
                for a in range(2):
                    ps = hps[:, a * 256:(a + 1) * 256].rearrange("p (g c) -> p g c", g=2)
                    dve.wait_ge(m["h_done"], 2 * b + 2)
                    if b:
                        dve.wait_ge(m["kc_done"], b)
                    dve.tensor_copy(h_next[:, a, :, :], ps[HD:P, :, 1:NCH]).then_inc(m["h_moved"], 1)
                    dve.wait_ge(m["h_moved"], 2 * b + a + 1)
                    dve.tensor_tensor(h_sum[:, a, :, :], ps[0:HD, :, 0:NC], h_next[:, a, :, :], ALU.add).then_inc(m["h_summed"], 1)

            def compressed(b):
                dve.wait_ge(m["kc_done"], b + 1)
                if b:
                    dve.wait_ge(m["cmp_out"], b)
                dve.tensor_copy(kcT[:, :], cps[:, 0:NC]).then_inc(m["kc_out"], 1)
                dve.tensor_copy(vc[:, :], cps[0:NC, 128:256]).then_inc(m["kc_out"], 1)
                dve.wait_ge(m["cmp_scored"], b + 1)
                dve.tensor_tensor_reduce(out=sc_cmp[:, :], in0=cps[:, 256:256 + NC], in1=zeros[:, 0:NC], scale=-1.0, scalar=FLOOR,
                                         op0=ALU.add, op1=ALU.min, accum_out=nmax[:, 10:11]).then_inc(m["cmp_shifted"], 1)

            def normalize(b):
                dve.wait_ge(m["cmp_exped"], b + 1)
                dve.reciprocal(wgt[:, 2:3], total[:, 2:3]).then_inc(m["cmp_total"], 1)
                dve.wait_ge(m["cmp_total"], b + 1)
                dve.tensor_scalar(pc[:, :], pc[:, :], wgt[:, 2:3], None, ALU.mult).then_inc(m["cmp_normed"], 1)

            def choose(b):
                dve.wait_ge(m["imp_done"], b + 1)
                dve.tensor_copy(imp[:, 1:NC + 1], cps[0:16, 384:384 + NC]).then_inc(m["imp_out"], 1)
                n = turn_no[("pc", b, 0)]
                dve.wait_ge(tps_turned[n % 2], n // 2 + 1)
                dve.tensor_copy(pcT[:, :], tps[n % 2][0:NC, 0:P]).then_inc(tps_out[n % 2], 1)
                dve.wait_ge(tps_out[n % 2], out_count(n))
                dve.sem_inc(m["pcT_ready"], 1)
                dve.wait_ge(m["imp_out"], b + 1)
                dve.tensor_tensor(pair[:, :], imp[:, 1:P + 1], imp[:, 0:P], ALU.add).then_inc(m["paired"], 1)
                dve.wait_ge(m["paired"], b + 1)
                dve.tensor_reduce(blocks[:, 0:32], pair[:, :].rearrange("r (k c) -> r k c", c=4), AX_X, ALU.add).then_inc(m["block_sums"], 1)
                dve.memset(blocks[:, 32:33], 0.0).then_inc(m["block_sums"], 1)
                dve.wait_ge(m["block_sums"], 2 * b + 2)
                dve.tensor_tensor(blocks[:, :], blocks[:, :], keep.sel_bonus[:, :], ALU.add).then_inc(m["bonus"], 1)
                for r in range(SEL_TOP // 8):
                    dve.wait_ge(m["bonus"], 3 * b + r + 1)
                    dve.max(best[:, r, :], blocks[:, :]).then_inc(m["picked"], 1)
                    dve.wait_ge(m["picked"], 2 * b + r + 1)
                    dve.match_replace(out=blocks[:, :], in_to_replace=best[:, r, :], in_values=blocks[:, :], imm_value=TAKEN).then_inc(m["bonus"], 1)
                dve.wait_ge(m["bonus"], 3 * b + 3)
                dve.tensor_scalar(choice[:, b % 2, :], blocks[:, :], TAKEN / 2, NEG, ALU.is_gt, ALU.mult).then_inc(m["chosen"], 1)

            def part(b, br, col, weight_col):
                for g in range(2):
                    r = slice(g * HD, (g + 1) * HD)
                    src = outp[r, col + g * HD:col + (g + 1) * HD]
                    if br == 0:
                        dve.tensor_scalar(o[r, 0, :], src, weight_col[r, :], None, ALU.mult).then_inc(m["o_part"], 1)
                    else:
                        dve.scalar_tensor_tensor(out=o[r, br, :], in0=src, scalar=weight_col[r, :], in1=o[r, br - 1, :],
                                                 op0=ALU.mult, op1=ALU.add).then_inc(m["o_part"], 1)

            for b in range(-1, NB):
                if b >= 0:
                    if b:
                        dve.wait_ge(m["slc_out"], b)
                    for i in range(4):
                        shift(("s", b, i), shifted[:, i * 512:(i + 1) * 512], table[:, i * 512:(i + 1) * 512], 512, i)
                    shift(("s", b, 4), shifted[:, PAST:LS], table[:, PAST:LS], NS, 4)
                    shift(("w", b, 0), shifted_w[:, 0:C_WIN], table_w[:, 0:C_WIN], 512, 5)
                    shift(("w", b, 1), shifted_w[:, C_WIN:LW], table_w[:, C_WIN:LW], NS, 6)
                    for i in range(3):
                        dve.wait_ge(shifted_out[i], len([g for g in scores_order[:7 * (b + 1)] if score_no[g] % 3 == i]))
                    dve.tensor_reduce(nmax[:, 8:9], nmax[:, 0:5], AX_X, ALU.min).then_inc(m["weighed"], 1)
                    dve.tensor_reduce(nmax[:, 9:10], nmax[:, 5:7], AX_X, ALU.min).then_inc(m["slc_max"], 1)
                if b + 1 < NB:
                    for i in range(8):
                        n = turn_no[("x", b + 1, i)]
                        dve.wait_ge(tps_turned[n % 2], n // 2 + 1)
                        if b >= 0 and i == 0:
                            dve.wait_ge(m["h_done"], 2 * (b + 1))
                        x_group(dve.tensor_copy, b + 1, i, 1)
                    if b < 0:
                        prepare()
                    hidden(b + 1)
                if b >= 0:
                    for i in range(5):
                        rows, cnt = (P, 4) if i < 4 else (NS, 1)
                        n = turn_no[("p", b, i)]
                        dve.wait_ge(tps_turned[n % 2], n // 2 + 1)
                        dve.tensor_copy(pT[0:rows, 4 * i:4 * i + cnt, :], tps[n % 2][0:rows, 0:cnt * P].rearrange("p (j r) -> p j r", j=cnt)).then_inc(tps_out[n % 2], 1)
                        dve.wait_ge(tps_out[n % 2], out_count(n))
                        dve.sem_inc(m["pT_ready"], 1)
                    for i in range(2):
                        rows, cnt = (P, 4) if i < 1 else (NS, 1)
                        n = turn_no[("pw", b, i)]
                        dve.wait_ge(tps_turned[n % 2], n // 2 + 1)
                        dve.tensor_copy(pwT[0:rows, 4 * i:4 * i + cnt, :], tps[n % 2][0:rows, 0:cnt * P].rearrange("p (j r) -> p j r", j=cnt)).then_inc(tps_out[n % 2], 1)
                        dve.wait_ge(tps_out[n % 2], out_count(n))
                        dve.sem_inc(m["pwT_ready"], 1)
                if b + 1 < NB:
                    compressed(b + 1)
                if b >= 0:
                    dve.wait_ge(m["win_exped"], b + 1)
                    dve.reciprocal(wgt[:, 0:2], total[:, 0:2]).then_inc(m["inverted"], 1)
                    dve.wait_ge(m["inverted"], b + 1)
                    dve.tensor_tensor(wgt[:, 0:2], gate[:, 1:3, b], wgt[:, 0:2], ALU.mult).then_inc(m["weighed"], 1)
                if b + 1 < NB:
                    normalize(b + 1)
                if b >= 0:
                    dve.wait_ge(m["weighed"], 2 * b + 2)
                    dve.wait_ge(m["win_out"], b + 1)
                    part(b, 0, 0, gate[:, 0, b:b + 1])
                    dve.wait_ge(m["o_part"], 6 * b + 2)
                    part(b, 1, 128, wgt[:, 0:1])
                    dve.wait_ge(m["o_part"], 6 * b + 4)
                    part(b, 2, 256, wgt[:, 1:2])
                    dve.wait_ge(m["o_part"], 6 * b + 6)
                    dve.sem_inc(m["o_ready"], 1)
                if b + 1 < NB:
                    choose(b + 1)
                if b >= 0:
                    dve.wait_ge(m["o_turned"], b + 1)
                    src = hps[0:HD, 0:P].rearrange("e (h two q) -> e h two q", two=2, q=NS)
                    for odd in range(2):
                        dve.tensor_copy(keep.mixT[odd * HD:(odd + 1) * HD, :, SEQ + b * NS:SEQ + (b + 1) * NS], src[:, :, odd, :]).then_inc(m["mixed"], 1)


class Keep:
    pass


@contextmanager
def x_parts(nc, keep, name):
    with nc.sbuf_tensor(name + "_h", [P, KC, T], F32R) as keep.xh, nc.sbuf_tensor(name + "_l", [P, KC, T], F32R) as keep.xl:
        yield


def build(nc, io):
    keep, dram = Keep(), Keep()
    dram.vec_up = nc.dram_tensor("vec_up", [3, N_HEADS, LU], F32, kind="Internal").ap()
    dram.pscore = nc.dram_tensor("pscore", [P, NQ - 1, SEQ], F32, kind="Internal").ap()
    dram.hT_ab = nc.dram_tensor("hT_ab", [AB_COLS, T], F32, kind="Internal").ap()
    dram.hT_c = nc.dram_tensor("hT_c", [C_COLS, T], F32, kind="Internal").ap()
    dram.vec = nc.dram_tensor("vec", [3, N_HEADS, LV], F32, kind="Internal").ap()
    with ExitStack() as ctx:
        def sb(name, shape, dt=F32):
            return ctx.enter_context(nc.sbuf_tensor(name, shape, dt))

        keep.xtok = sb("xtok", [P, NT, D])
        keep.mixT = sb("mixT", [P, KC, T])
        keep.ident = sb("ident", [P, P])
        keep.ident_bf = sb("ident_bf", [P, P], BF16)
        keep.causal = sb("causal", [P, P])
        keep.chunk_row = sb("chunk_row", [P, NB], I32)
        keep.eps = sb("eps", [P, 1])
        copied = ctx.enter_context(nc.semaphore("state_copied"))
        const_in = ctx.enter_context(nc.semaphore("const_in"))
        keep.kidx_in = [ctx.enter_context(nc.semaphore(f"kidx_in{b}")) for b in range(NB)]
        keep.a_kv_in = [ctx.enter_context(nc.semaphore(f"a_kv_in{i}")) for i in range(3)]
        keep.c_kv_in = [ctx.enter_context(nc.semaphore(f"c_kv_in{i}")) for i in range(2)]
        consts = [("same_token", [P, 16]), ("pick_row", [TS, NB, TS]), ("new_causal", [TS, NS]), ("group_sum", [P, 16]),
                  ("group_spread", [16, P]), ("sel_bonus", [16, N_SEL])]
        held = {name: sb(name, shape) for name, shape in consts}
        keep.same_token, keep.pick_row, keep.new_causal = held["same_token"], held["pick_row"], held["new_causal"]
        keep.group_sum, keep.group_spread, keep.sel_bonus = held["group_sum"], held["group_spread"], held["sel_bonus"]
        keep.pending = ctx.enter_context(nc.semaphore("pending"))
        keep.pending_count = 0
        keep.gate_tok = sb("gate_tok", [P, NQ, 48])
        keep.cmp_const = sb("cmp_const", [HD, 2])

        for name, shape in consts:
            whole = tuple(slice(0, n) for n in shape)
            nc.sync.dma_start(held[name][whole], io["c_" + name]).then_inc(const_in, 16)
        nc.vector.memset(keep.eps[:, :], LN_EPS)
        nc.sync.wait_ge(const_in, 16 * len(consts))

        with x_parts(nc, keep, "x0"), nc.sbuf_tensor("zero", [P, D], F32) as keep.zero:
            setup_phase(nc, io, keep, dram)
            empty = keep.zero[:, None, :].to_broadcast([P, 12, D])
            project_phase(nc, "proj_ab", io["w_in_ab"], AB_COLS, dram.hT_ab, keep,
                          late_stores=[(io["o_p_b_kv"][0:3 * SEQ, :].rearrange("(p n) c -> p n c", p=P), empty)])
        with ExitStack() as ab:
            score = ab.enter_context(nc.sbuf_tensor("sample_score", [TS, LS], F32))
            with nc.sbuf_tensor("tok_ab", [P, NT, TAB], F32) as tok:
                token_major_phase(nc, "tok_ab", dram.hT_ab, [(A_K, 256, TA_K), (A_KI, 72, TA_KI), (B_K, 1024, TB_K)], tok, [
                    (io["o_p_a_kv"].rearrange("(i p) c -> p i c", p=P), tok[:, 0:NQ, 0:256]),
                    (io["o_p_a_kidx"].rearrange("(i p) c -> p i c", p=P), tok[:, 0:NQ, TA_KI:TA_W]),
                    (io["o_p_b_kv"][3 * SEQ:, :].rearrange("(i p) c -> p i c", p=P), tok[:, 0:NQ, TB_K:TAB]),
                    (io["o_s_a_kv"].rearrange("b q c -> (b q) c"), tok[0:TS, NQ, 0:256]),
                    (io["o_s_a_kidx"].rearrange("b q c -> (b q) c"), tok[0:TS, NQ, TA_KI:TA_W]),
                ] + [(io["o_s_b_kv"][b, PAST - NS:PAST, :], tok[b * NS:(b + 1) * NS, NQ, TB_K:TAB]) for b in range(NB)], keep)
                sample_indexer_phase(nc, dram.hT_ab, io["cache_a_kidx"], io, score, keep)
                prompt_indexer_phase(nc, dram.hT_ab, tok, dram.pscore, keep)
            sample_b_phase(nc, dram.hT_ab, dram.vec, io["state_b_kv"], io["o_s_b_kv"][:, PAST - NS:PAST, :], io, score, keep)
            with ExitStack() as pr:
                sel_bias = pr.enter_context(nc.sbuf_tensor("sel_bias", [P, NQ - 1, SEQ], BF16))
                sample_a_phase(nc, dram.hT_ab, dram.vec, io["cache_a_kv"], io["o_s_a_kv"], io, score, dram.pscore, sel_bias, keep)
                v_tok = pr.enter_context(nc.sbuf_tensor("v_tok", [P, NQ, P + 512], F32))
                prompt_attention_phase(nc, "pab", [
                    dict(heads=H_B, k=B_K, kv=H_B, v=P, kind=KIND_DIL, h0=8, sel=False, gate=None),
                    dict(heads=H_A, k=A_K, kv=2, v=0, kind=KIND_FULL, h0=0, sel=True, gate=None),
                ], [(B_Q + h * HD, H_A + h, [(0, h)]) for h in range(H_B)] + [(A_Q + h * HD, h, [(1, h)]) for h in range(H_A)],
                    dram.hT_ab, dram.vec_up, v_tok, keep, tok_loads=[
                    (v_tok[:, :, 0:P], io["o_p_a_kv"].rearrange("(i p) c -> p i c", p=P)[:, :, P:2 * P]),
                    (v_tok[:, :, P:], io["o_p_b_kv"][3 * SEQ:, :].rearrange("(i p) c -> p i c", p=P)[:, :, 512:D]),
                ], sel_bias=sel_bias)
        with x_parts(nc, keep, "x1"):
            output_phase(nc, "out_ab", io["w_out_ab"], io["ln1_g"][0], io["ln1_b"][0], keep)
            ffn_phase(nc, "ffn0", io["ffn_up"][0], io["ffn_conv_w"][0], io["ffn_conv_b"][0], io["ffn_down"][0], io["state_ffn"][0],
                      io["ln2_g"][0], io["ln2_b"][0], io["o_p_ffn"][0], io["o_s_ffn"][0], None, StateCopy(io, 0, copied), keep)

            project_phase(nc, "proj_c", io["w_in_c"], C_COLS, dram.hT_c, keep)

        with ExitStack() as c:
            tok = c.enter_context(nc.sbuf_tensor("tok_c", [P, NT, TC], F32))
            token_major_phase(nc, "tok_c", dram.hT_c, [(C_KV, 768, 0), (C_G, 48, TC_G)], tok, [
                (io["o_p_c_kv"].rearrange("(i p) c -> p i c", p=P), tok[:, 0:NQ, 0:512]),
                (io["o_p_c_win"].rearrange("(i p) c -> p i c", p=P), tok[:, 0:NQ, 512:768]),
                (io["o_s_c_kv"].rearrange("b q c -> (b q) c"), tok[0:TS, NQ, 0:512]),
            ] + [(io["o_s_c_win"][b, C_WIN - NS:C_WIN, :], tok[b * NS:(b + 1) * NS, NQ, 512:768]) for b in range(NB)], keep)
            with nc.sbuf_tensor("mix_c", [P, NQ, D], F32) as mix:
                prompt_compressed_phase(nc, dram.hT_c, tok, mix, io, keep)
                turn_mix_phase(nc, "mix_c_turn", mix, keep)
            prompt_attention_phase(nc, "pc", [
                dict(heads=N_HEADS, k=C_KV + 2 * P, kv=2, v=3 * P, kind=KIND_FULL, h0=0, sel=False, gate=N_HEADS),
                dict(heads=N_HEADS, k=C_KV + 4 * P, kv=2, v=5 * P, kind=KIND_WIN, h0=0, sel=False, gate=2 * N_HEADS),
            ], [(C_Q + h * HD, h, [(0, h), (1, h)]) for h in range(N_HEADS)], dram.hT_c, dram.vec_up, tok, keep)
        sample_c_phase(nc, dram.hT_c, dram.vec, io["cache_c_kv"], io["state_c_kv"], io["o_s_c_kv"],
                       io["o_s_c_win"][:, C_WIN - NS:C_WIN, :], io, keep)
        with x_parts(nc, keep, "x2"):
            output_phase(nc, "out_c", io["w_out_c"], io["ln1_g"][1], io["ln1_b"][1], keep)
            ffn_phase(nc, "ffn1", io["ffn_up"][1], io["ffn_conv_w"][1], io["ffn_conv_b"][1], io["ffn_down"][1], io["state_ffn"][1],
                      io["ln2_g"][1], io["ln2_b"][1], io["o_p_ffn"][1], io["o_s_ffn"][1], (io["o_y_prompt"], io["o_y_sample"]),
                      StateCopy(io, 1, copied), keep)


def t5_buckets(dist):
    n = np.maximum(dist, 0)
    nf = np.maximum(n, 1).astype(np.float32)
    far = 16 + (np.log(nf / np.float32(16)) / np.float32(np.log(8.0)) * np.float32(16)).astype(np.int32)
    return np.where(n < 16, n, np.minimum(far, 31))


def distance_rows(dist):
    rows = np.zeros((33, 3, len(dist)), np.float32)
    rows[t5_buckets(dist), :, np.arange(len(dist))] = 1.0
    held = sum(((dist >= 0) & (dist <= w) & (dist % d == 0)).astype(np.float64) for w, d in B_WINDOWS)
    rows[32, KIND_FULL] = np.where(dist >= 0, 0.0, NEG)
    rows[32, KIND_WIN] = np.where((dist >= 0) & (dist < C_WIN), 0.0, NEG)
    rows[32, KIND_DIL] = np.where(held > 0, np.log(np.maximum(held, 1.0)), NEG)
    return rows


def shape_constants():
    onehot, onehot_up = distance_rows(FAR - np.arange(LV)), distance_rows(np.arange(LU) + 1 - P)
    i = np.arange(P)
    j2hq = np.arange(P)
    bq = np.arange(TS)
    pick = np.zeros((TS, NB, TS), np.float32)
    for b in range(NB):
        pick[:, b, :] = (bq[:, None] // NS == b) & (bq[:, None] % NS == np.arange(TS)[None, :] % NS)
    group = (j2hq[:, None] // 64 == np.arange(16)[None, :] // NS) & (j2hq[:, None] % NS == np.arange(16)[None, :] % NS)
    cmp_mask = np.full((P, NQ, 32), NEG, np.float32)
    for t in range(NQ):
        pos = t * P + i[:, None]
        cmp_mask[:, t, 0:31] = np.where(np.arange(31)[None, :] * STRIDE + 2 * STRIDE - 1 <= pos, 0.0, NEG)
    blk = np.arange(N_SEL)
    cur = PAST // 64
    return {
        "c_ident": np.eye(P, dtype=np.float32),
        "c_causal": np.where(i[None, :] <= i[:, None], 0.0, NEG).astype(np.float32),
        "c_onehot": onehot,
        "c_onehot_up": onehot_up,
        "c_same_token": group.astype(np.float32),
        "c_group_sum": group.astype(np.float32),
        "c_group_spread": np.ascontiguousarray(group.T).astype(np.float32),
        "c_pick_row": pick,
        "c_new_causal": np.where(np.arange(NS)[None, :] <= bq[:, None] % NS, 0.0, NEG).astype(np.float32),
        "c_cmp_mask": cmp_mask,
        "c_sel_bonus": np.tile(np.where((blk == 0) | (blk == cur) | (blk == cur - 1), SEL_BONUS, 0.0), (16, 1)).astype(np.float32),
    }


VIEWS = {
    "x_prompt": (1, SEQ, D), "x_sample": (NB, NS, D), "cache_a_kv": (160, PAGE, 2, 2, HD), "cache_a_kidx": (160, PAGE, HD),
    "cache_c_kv": (160, PAGE, 4, 2, HD), "state_b_kv": (NB, PAST, D), "state_c_kv": (NB, C_WIN, 256),
    "state_ffn": (2, NB, 2, 2 * D_FF), "page_table": (NB, 16), "rel_bias": (32, 16), "w_in_ab": (D, AB_COLS), "w_out_ab": (D, D),
    "w_in_c": (D, C_COLS), "w_out_c": (D, D), "phi_pe": (2, 32, HD), "phi_w1": (2, 32, HD, HD), "phi_b1": (2, HD),
    "phi_w2": (2, HD, HD), "ln1_g": (2, D), "ln1_b": (2, D), "ln2_g": (2, D), "ln2_b": (2, D), "ffn_up": (2, D, 2 * D_FF),
    "ffn_conv_w": (2, CONV_W, 2 * D_FF), "ffn_conv_b": (2, 2 * D_FF), "ffn_down": (2, D_FF, D),
}
OUTS = [
    ("y_prompt", (1, SEQ, D), (1, SEQ, D)), ("y_sample", (NB, NS, D), (NB, NS, D)),
    ("p_a_kv", (SEQ, 256), (1, 1, SEQ, 2, 2, HD)), ("p_a_kidx", (SEQ, HD), (1, 1, SEQ, HD)),
    ("p_b_kv", (PAST, D), (1, 1, PAST, 2, 8, HD)), ("p_c_kv", (SEQ, 512), (1, 1, SEQ, 4, 2, HD)),
    ("p_c_win", (SEQ, 256), (1, 1, C_WIN, 2, 2, HD)), ("p_ffn", (2, 2, 2 * D_FF), (2, 1, 2, 2 * D_FF)),
    ("s_a_kv", (NB, NS, 256), (1, NB, NS, 2, 2, HD)), ("s_a_kidx", (NB, NS, HD), (1, NB, NS, HD)),
    ("s_b_kv", (NB, PAST, D), (1, NB, PAST, 2, 8, HD)), ("s_c_kv", (NB, NS, 512), (1, NB, NS, 4, 2, HD)),
    ("s_c_win", (NB, C_WIN, 256), (1, NB, C_WIN, 2, 2, HD)), ("s_ffn", (2, 2 * NB, 2 * D_FF), (2, NB, 2, 2 * D_FF)),
]


def kernel(**inputs):
    import concourse.bacc as bacc
    from concourse.bass_utils import run_bass_kernel_spmd

    nc = bacc.Bacc("TRN2", target_bir_lowering=False, num_devices=1)
    arrays, io = {}, {}
    for name, shape in VIEWS.items():
        arrays[name] = np.ascontiguousarray(inputs[name]).reshape(shape)
    arrays.update(shape_constants())
    for name, a in arrays.items():
        io[name] = nc.dram_tensor(name, list(a.shape), mybir.dt.from_np(a.dtype), kind="ExternalInput").ap()
    for name, view, _ in OUTS:
        io["o_" + name] = nc.dram_tensor("out_" + name, list(view), F32, kind="ExternalOutput").ap()
    build(nc, io)
    r = run_bass_kernel_spmd(nc, [arrays], core_ids=[0]).results[0]
    return tuple(r["out_" + name].reshape(shape) for name, _, shape in OUTS)
```
